# Optimizing a Trainium2 kernel written in Bass

```python
import math
import jax, jax.numpy as jnp
from jax import lax
import numpy as np

D_MODEL = 1024
BATCH = 1
SEQ = 256
DEPTH = 1

CHUNK = 64
D_MIX = D_MODEL
D_SSM = D_MIX // 2
D_ATT = D_MIX - D_SSM
SSM_GROUP = 16
N_SSM_GROUPS = D_SSM // SSM_GROUP
SSM_STATE = 64
HEAD_DIM = 64
N_HEADS = D_ATT // HEAD_DIM
LEFT_CHUNKS = 8
BAND = (LEFT_CHUNKS + 1) * CHUNK
MAX_REL = 128
D_FF = -(-8 * D_MODEL // (3 * 256)) * 256
D_IN = D_SSM + 3 * D_ATT
EPS = 1e-6
DT_MIN = 1e-3
DT_MAX = 1e-1


def rmsnorm(x, g):
    xf = x.astype(jnp.float32)
    y = xf * lax.rsqrt(jnp.mean(xf * xf, axis=-1, keepdims=True) + EPS)
    return (y * g.astype(jnp.float32)).astype(x.dtype)

def s5_mixer(u, lam_re, lam_im, log_dt, b_re, b_im, c_re, c_im, d_skip, w_glu, b_glu):
    bsz, seq, _ = u.shape
    f32 = jnp.float32
    uf = u.astype(f32).reshape(bsz, seq, N_SSM_GROUPS, SSM_GROUP)
    lam = lax.complex(lam_re.astype(f32), lam_im.astype(f32))
    dt = jnp.exp(log_dt.astype(f32))[:, None]
    lam_bar = jnp.exp(lam * dt)
    b_mat = lax.complex(b_re.astype(f32), b_im.astype(f32))
    b_bar = ((lam_bar - 1.0) / lam)[..., None] * b_mat
    bu = jnp.einsum('bsgh,gph->bsgp', uf.astype(jnp.complex64), b_bar)
    a = jnp.broadcast_to(lam_bar, bu.shape)

    def combine(left, right):
        a_l, b_l = left
        a_r, b_r = right
        return a_r * a_l, a_r * b_l + b_r

    _, states = lax.associative_scan(combine, (a, bu), axis=1)
    c_mat = lax.complex(c_re.astype(f32), c_im.astype(f32))
    y = jnp.einsum('bsgp,ghp->bsgh', states, c_mat).real + d_skip.astype(f32) * uf
    y = jax.nn.gelu(y.reshape(bsz, seq, D_SSM))
    y = y * jax.nn.sigmoid(y @ w_glu.astype(f32) + b_glu.astype(f32))
    return y.astype(u.dtype)

def chunked_attention(q, k, v, rel_bias):
    bsz, seq, _ = q.shape
    n_chunks = seq // CHUNK
    shp = (bsz, n_chunks, CHUNK, N_HEADS, HEAD_DIM)
    qc, kc, vc = q.reshape(shp), k.reshape(shp), v.reshape(shp)
    pad = ((0, 0), (LEFT_CHUNKS, 0), (0, 0), (0, 0), (0, 0))
    kp, vp = jnp.pad(kc, pad), jnp.pad(vc, pad)
    kb = jnp.concatenate([kp[:, j:j + n_chunks] for j in range(LEFT_CHUNKS + 1)], axis=2)
    vb = jnp.concatenate([vp[:, j:j + n_chunks] for j in range(LEFT_CHUNKS + 1)], axis=2)
    key_chunk = jnp.arange(n_chunks)[:, None] - LEFT_CHUNKS + (jnp.arange(BAND) // CHUNK)[None, :]
    valid = key_chunk >= 0
    rel = jnp.arange(BAND)[None, :] - LEFT_CHUNKS * CHUNK - jnp.arange(CHUNK)[:, None]
    idx = jnp.clip(rel, -MAX_REL, MAX_REL) + MAX_REL
    bias = rel_bias.astype(jnp.float32)[:, idx]
    scores = jnp.einsum('bnqhd,bnkhd->bhnqk', qc, kb).astype(jnp.float32) / math.sqrt(HEAD_DIM)
    scores = scores + bias[None, :, None, :, :]
    scores = jnp.where(valid[None, None, :, None, :], scores, -1e30)
    probs = jax.nn.softmax(scores, axis=-1)
    out = jnp.einsum('bhnqk,bnkhd->bnqhd', probs.astype(v.dtype), vb)
    return out.reshape(bsz, seq, D_ATT)

def first_inputs(seed: int = 0) -> dict:
    key = jax.random.key(seed)
    ks = jax.random.split(key, 24)
    f32 = jnp.float32
    L, G, P, H = DEPTH, N_SSM_GROUPS, SSM_STATE, SSM_GROUP

    def nrm(k, shape, scale):
        return jax.random.normal(k, shape, f32) * scale

    def gain(k, n):
        return 1.0 + 0.05 * jax.random.normal(k, (L, n), f32)

    lam_re = -0.5 + 0.01 * jax.random.normal(ks[3], (L, G, P), f32)
    lam_im = math.pi * jnp.arange(P, dtype=f32)[None, None, :] + 0.01 * jax.random.normal(ks[4], (L, G, P), f32)
    log_dt = jax.random.uniform(ks[5], (L, G), f32, math.log(DT_MIN), math.log(DT_MAX))
    return {
        "x": jax.random.normal(ks[0], (BATCH, SEQ, D_MODEL), f32),
        "norm_mix_g": gain(ks[1], D_MODEL),
        "w_in": nrm(ks[2], (L, D_MODEL, D_IN), D_MODEL ** -0.5),
        "ssm_lam_re": lam_re,
        "ssm_lam_im": lam_im,
        "ssm_log_dt": log_dt,
        "ssm_b_re": nrm(ks[6], (L, G, P, H), (2.0 * H) ** -0.5),
        "ssm_b_im": nrm(ks[7], (L, G, P, H), (2.0 * H) ** -0.5),
        "ssm_c_re": nrm(ks[8], (L, G, H, P), (2.0 * P) ** -0.5),
        "ssm_c_im": nrm(ks[9], (L, G, H, P), (2.0 * P) ** -0.5),
        "ssm_d": nrm(ks[10], (L, G, H), 1.0),
        "ssm_w_glu": nrm(ks[11], (L, D_SSM, D_SSM), D_SSM ** -0.5),
        "ssm_b_glu": nrm(ks[12], (L, D_SSM), 0.02),
        "attn_rel_bias": nrm(ks[13], (L, N_HEADS, 2 * MAX_REL + 1), 0.5),
        "norm_ssm_out_g": gain(ks[14], D_SSM),
        "norm_att_out_g": gain(ks[15], D_ATT),
        "w_out": nrm(ks[16], (L, D_MIX, D_MODEL), D_MIX ** -0.5),
        "norm_ffn_g": gain(ks[17], D_MODEL),
        "w_gate": nrm(ks[18], (L, D_MODEL, D_FF), D_MODEL ** -0.5),
        "w_up": nrm(ks[19], (L, D_MODEL, D_FF), D_MODEL ** -0.5),
        "w_down": nrm(ks[20], (L, D_FF, D_MODEL), D_FF ** -0.5),
        "norm_final_g": 1.0 + 0.05 * jax.random.normal(ks[21], (D_MODEL,), f32),
    }

def first_block(x, norm_mix_g, w_in, ssm_lam_re, ssm_lam_im, ssm_log_dt, ssm_b_re, ssm_b_im,
              ssm_c_re, ssm_c_im, ssm_d, ssm_w_glu, ssm_b_glu, attn_rel_bias,
              norm_ssm_out_g, norm_att_out_g, w_out, norm_ffn_g, w_gate, w_up, w_down,
              norm_final_g):
    for l in range(DEPTH):
        h = rmsnorm(x, norm_mix_g[l])
        proj = h @ w_in[l]
        u_ssm = proj[..., :D_SSM]
        q = proj[..., D_SSM:D_SSM + D_ATT]
        k = proj[..., D_SSM + D_ATT:D_SSM + 2 * D_ATT]
        v = proj[..., D_SSM + 2 * D_ATT:]
        y_ssm = s5_mixer(u_ssm, ssm_lam_re[l], ssm_lam_im[l], ssm_log_dt[l], ssm_b_re[l], ssm_b_im[l],
                         ssm_c_re[l], ssm_c_im[l], ssm_d[l], ssm_w_glu[l], ssm_b_glu[l])
        y_att = chunked_attention(q, k, v, attn_rel_bias[l])
        mixed = jnp.concatenate([rmsnorm(y_ssm, norm_ssm_out_g[l]),
                                 rmsnorm(y_att, norm_att_out_g[l])], axis=-1)
        x = x + mixed @ w_out[l]
        h2 = rmsnorm(x, norm_ffn_g[l])
        x = x + (jax.nn.silu(h2 @ w_gate[l]) * (h2 @ w_up[l])) @ w_down[l]
    return rmsnorm(x, norm_final_g)


SB_HEADS = 8
DIL_GROUPS = ((128, 1), (512, 4), (2048, 16))
DIL_HEADS_PER_GROUP = 4
N_DIL_GROUPS = len(DIL_GROUPS)
DIL_HEADS = DIL_HEADS_PER_GROUP * N_DIL_GROUPS
SB_WIDTH = SB_HEADS * HEAD_DIM
DIL_WIDTH = DIL_HEADS * HEAD_DIM
DIL_OUT_WIDTH = DIL_HEADS_PER_GROUP * HEAD_DIM
IN_COLS = 3 * SB_WIDTH + 3 * DIL_WIDTH + 2 * D_MODEL
Q_BLOCK = 128
ROPE_THETA = 10000.0
PEER_HEADS = 8
PEER_NKEYS = 128
PEER_EXPERTS = PEER_NKEYS * PEER_NKEYS
PEER_QDIM = 256
PEER_HALF = PEER_QDIM // 2
PEER_TOPK = 16
PEER_TOKEN_CHUNK = 128
N_MOD = 6


def rms_norm(x, g):
    xf = x.astype(jnp.float32)
    y = xf * lax.rsqrt(jnp.mean(xf * xf, axis=-1, keepdims=True) + EPS)
    return (y * g.astype(jnp.float32)).astype(x.dtype)

def modulate(h, shift, scale):
    return h * (1.0 + scale[:, None, :]) + shift[:, None, :]

def rope(x, pos):
    half = HEAD_DIM // 2
    inv = ROPE_THETA ** (-jnp.arange(half, dtype=jnp.float32) / half)
    ang = pos.astype(jnp.float32)[:, None] * inv[None, :]
    cos = jnp.cos(ang)[None, :, None, :]
    sin = jnp.sin(ang)[None, :, None, :]
    xf = x.astype(jnp.float32)
    x1, x2 = xf[..., :half], xf[..., half:]
    return jnp.concatenate([x1 * cos - x2 * sin, x1 * sin + x2 * cos], axis=-1).astype(x.dtype)

def stick_breaking_attention(q, k, v):
    S = q.shape[1]
    scale = HEAD_DIM ** -0.5
    outs = []
    for blk in range(S // Q_BLOCK):
        t0 = blk * Q_BLOCK
        kl = t0 + Q_BLOCK
        qb, kb, vb = q[:, t0:kl], k[:, :kl], v[:, :kl]
        z = jnp.einsum('bqhd,bkhd->bhqk', qb, kb).astype(jnp.float32) * scale
        t_idx = t0 + jnp.arange(Q_BLOCK)
        s_idx = jnp.arange(kl)
        mask = s_idx[None, :] < t_idx[:, None]
        log_1m_beta = jnp.where(mask, jax.nn.log_sigmoid(-z), 0.0)
        after = lax.cumsum(log_1m_beta, axis=3, reverse=True) - log_1m_beta
        a = jnp.where(mask, jnp.exp(jax.nn.log_sigmoid(z) + after), 0.0)
        outs.append(jnp.einsum('bhqk,bkhd->bqhd', a.astype(v.dtype), vb))
    return jnp.concatenate(outs, axis=1)

def dilated_attention(q, k, v):
    B, S = q.shape[:2]
    scale = HEAD_DIM ** -0.5
    n_blocks = S // Q_BLOCK

    def block(blk):
        t = blk * Q_BLOCK + jnp.arange(Q_BLOCK)
        qb = lax.dynamic_slice_in_dim(q, blk * Q_BLOCK, Q_BLOCK, axis=1)
        outs, lses = [], []
        for g, (w, r) in enumerate(DIL_GROUPS):
            n = w // r + 1
            idx = t[:, None] - r * jnp.arange(n)[None, :]
            valid = idx >= 0
            idx_c = jnp.maximum(idx, 0)
            kg = jnp.take(k[:, :, g], idx_c, axis=1)
            vg = jnp.take(v[:, :, g], idx_c, axis=1)
            z = jnp.einsum('bqhd,bqnhd->bhqn', qb[:, :, g], kg).astype(jnp.float32) * scale
            z = jnp.where(valid[None, None], z, -jnp.inf)
            lse = jax.nn.logsumexp(z, axis=-1)
            p = jnp.exp(z - lse[..., None])
            outs.append(jnp.einsum('bhqn,bqnhd->bqhd', p.astype(vg.dtype), vg).astype(jnp.float32))
            lses.append(lse)
        wts = jax.nn.softmax(jnp.stack(lses, axis=0), axis=0)
        wts = jnp.transpose(wts, (0, 1, 3, 2))[..., None]
        return jnp.sum(wts * jnp.stack(outs, axis=0), axis=0).astype(q.dtype)

    out = lax.map(block, jnp.arange(n_blocks))
    return jnp.transpose(out, (1, 0, 2, 3, 4)).reshape(B, S, DIL_HEADS_PER_GROUP, HEAD_DIM)

def peer_ffn(h, w_pq, peer_keys, peer_u, peer_v):
    B, S, D = h.shape
    T = B * S
    ht = h.reshape(T, D)
    q = (ht @ w_pq).reshape(T, PEER_HEADS, 2, PEER_HALF)
    sub = jnp.einsum('thpc,hpnc->thpn', q, peer_keys).astype(jnp.float32)
    s_top, i_top = lax.top_k(sub, PEER_TOPK)
    cand_s = (s_top[:, :, 0, :, None] + s_top[:, :, 1, None, :]).reshape(T, PEER_HEADS, PEER_TOPK * PEER_TOPK)
    cand_i = (i_top[:, :, 0, :, None] * PEER_NKEYS + i_top[:, :, 1, None, :]).reshape(T, PEER_HEADS, PEER_TOPK * PEER_TOPK)
    best_s, pos = lax.top_k(cand_s, PEER_TOPK)
    expert = jnp.take_along_axis(cand_i, pos, axis=-1)
    gate = jax.nn.softmax(best_s, axis=-1)
    hk = PEER_HEADS * PEER_TOPK
    n_chunks = T // PEER_TOKEN_CHUNK

    def chunk(args):
        xc, ec, gc = args
        u = jnp.take(peer_u, ec, axis=0)
        act = jax.nn.gelu(jnp.einsum('cd,ckd->ck', xc, u))
        vv = jnp.take(peer_v, ec, axis=0)
        return jnp.einsum('ck,ckd->cd', gc.astype(xc.dtype) * act, vv)

    out = lax.map(chunk, (ht.reshape(n_chunks, PEER_TOKEN_CHUNK, D),
                          expert.reshape(n_chunks, PEER_TOKEN_CHUNK, hk),
                          gate.reshape(n_chunks, PEER_TOKEN_CHUNK, hk)))
    return out.reshape(B, S, D)

def second_inputs(seed: int = 0) -> dict:
    key = jax.random.key(seed)
    ks = jax.random.split(key, 16)
    D = D_MODEL
    f = jnp.float32
    nrm = lambda k, shape, s: jax.random.normal(k, shape, f) * s
    return {
        "x": nrm(ks[0], (BATCH, SEQ, D), 1.0),
        "c": nrm(ks[1], (BATCH, D), 1.0),
        "w_ada": nrm(ks[2], (DEPTH, D, N_MOD * D), 0.5 * D ** -0.5),
        "b_ada": nrm(ks[3], (DEPTH, N_MOD * D), 0.01),
        "g_mix": 1.0 + nrm(ks[4], (DEPTH, D), 0.02),
        "w_in": nrm(ks[5], (DEPTH, D, IN_COLS), D ** -0.5),
        "w_sb_o": nrm(ks[6], (DEPTH, SB_WIDTH, D), SB_WIDTH ** -0.5),
        "w_dil_o": nrm(ks[7], (DEPTH, DIL_OUT_WIDTH, D), DIL_OUT_WIDTH ** -0.5),
        "w_out": nrm(ks[8], (DEPTH, D, D), D ** -0.5),
        "g_ffn": 1.0 + nrm(ks[9], (DEPTH, D), 0.02),
        "w_pq": nrm(ks[10], (DEPTH, D, PEER_HEADS * PEER_QDIM), D ** -0.5),
        "peer_keys": nrm(ks[11], (DEPTH, PEER_HEADS, 2, PEER_NKEYS, PEER_HALF), PEER_HALF ** -0.5),
        "peer_u": nrm(ks[12], (DEPTH, PEER_EXPERTS, D), D ** -0.5),
        "peer_v": nrm(ks[13], (DEPTH, PEER_EXPERTS, D), PEER_HEADS ** -0.5),
        "g_final": 1.0 + nrm(ks[14], (D,), 0.02),
    }

def second_block(x, c, w_ada, b_ada, g_mix, w_in, w_sb_o, w_dil_o, w_out, g_ffn, w_pq,
              peer_keys, peer_u, peer_v, g_final):
    B, S, D = x.shape
    pos = jnp.arange(S)
    splits = np.cumsum([SB_WIDTH] * 3 + [DIL_WIDTH] * 3 + [D_MODEL]).tolist()
    for layer in range(DEPTH):
        mod = jax.nn.silu(c) @ w_ada[layer] + b_ada[layer]
        sh1, sc1, gt1, sh2, sc2, gt2 = jnp.split(mod, N_MOD, axis=-1)

        h = modulate(rms_norm(x, g_mix[layer]), sh1, sc1)
        proj = h @ w_in[layer]
        q_sb, k_sb, v_sb, q_d, k_d, v_d, gate_sb, gate_d = jnp.split(proj, splits, axis=-1)

        hs = (B, S, SB_HEADS, HEAD_DIM)
        o_sb = stick_breaking_attention(q_sb.reshape(hs), k_sb.reshape(hs), v_sb.reshape(hs))

        hd = (B, S, DIL_HEADS, HEAD_DIM)
        gd = (B, S, N_DIL_GROUPS, DIL_HEADS_PER_GROUP, HEAD_DIM)
        q_dr = rope(q_d.reshape(hd), pos).reshape(gd)
        k_dr = rope(k_d.reshape(hd), pos).reshape(gd)
        o_d = dilated_attention(q_dr, k_dr, v_d.reshape(gd))

        br_sb = o_sb.reshape(B, S, SB_WIDTH) @ w_sb_o[layer]
        br_d = o_d.reshape(B, S, DIL_OUT_WIDTH) @ w_dil_o[layer]
        merged = jax.nn.sigmoid(gate_sb) * br_sb + jax.nn.sigmoid(gate_d) * br_d
        x = x + gt1[:, None, :] * (merged @ w_out[layer])

        h2 = modulate(rms_norm(x, g_ffn[layer]), sh2, sc2)
        x = x + gt2[:, None, :] * peer_ffn(h2, w_pq[layer], peer_keys[layer], peer_u[layer], peer_v[layer])
    return rms_norm(x, g_final)


def setup_inputs(seed=0):
    out = dict(first_inputs(seed))
    for name, value in second_inputs(seed + 1).items():
        if name != "x":
            out[name + "_2"] = value
    return out


def reference(
    x, norm_mix_g, w_in, ssm_lam_re, ssm_lam_im, ssm_log_dt, ssm_b_re, ssm_b_im, ssm_c_re,
    ssm_c_im, ssm_d, ssm_w_glu, ssm_b_glu, attn_rel_bias, norm_ssm_out_g, norm_att_out_g, w_out,
    norm_ffn_g, w_gate, w_up, w_down, norm_final_g, c_2, w_ada_2, b_ada_2, g_mix_2, w_in_2,
    w_sb_o_2, w_dil_o_2, w_out_2, g_ffn_2, w_pq_2, peer_keys_2, peer_u_2, peer_v_2, g_final_2,
):
    x = first_block(
        x, norm_mix_g, w_in, ssm_lam_re, ssm_lam_im, ssm_log_dt, ssm_b_re, ssm_b_im, ssm_c_re,
        ssm_c_im, ssm_d, ssm_w_glu, ssm_b_glu, attn_rel_bias, norm_ssm_out_g, norm_att_out_g,
        w_out, norm_ffn_g, w_gate, w_up, w_down, norm_final_g,
    )
    return second_block(
        x, c_2, w_ada_2, b_ada_2, g_mix_2, w_in_2, w_sb_o_2, w_dil_o_2, w_out_2, g_ffn_2,
        w_pq_2, peer_keys_2, peer_u_2, peer_v_2, g_final_2,
    )


_drawn_inputs = setup_inputs


def setup_inputs(seed=0):
    import zlib

    import numpy as np

    out = dict(_drawn_inputs(seed))
    spreads = {}
    factors = {'ssm_lam_re': 8.0,
     'ssm_b_glu': 8.0,
     'b_ada_2': 5.93,
     'g_mix_2': 8.0,
     'g_ffn_2': 6.362,
     'g_final_2': 2.849}
    for name, (base, spread) in spreads.items():
        noise = np.random.default_rng([zlib.crc32(name.encode()), seed]).standard_normal(out[name].shape)
        drawn = base * np.exp(spread * noise) if base else spread * noise
        out[name] = __import__('jax').numpy.asarray(drawn.astype(out[name].dtype))
    for name, factor in factors.items():
        out[name] = (out[name] * factor).astype(out[name].dtype)
    return out
```

```python
from contextlib import ExitStack

import concourse.bass as bass
from concourse import mybir

F32 = mybir.dt.float32
U32 = mybir.dt.uint32
I32 = mybir.dt.int32
ALU = mybir.AluOpType
ACT = mybir.ActivationFunctionType
AX = mybir.AxisListType.X

P = 128
D = 1024
SEQ = 256
NT = SEQ // P
KD = D // P
DFF = 2816
NFF = DFF // 256
GROUPS, STATE, GCH = 32, 64, 16
NST = GROUPS * STATE // P
HD = 64
HEADS = 8
DIL = 3
DIL_HEADS = 4
PEER_HEADS = 8
TOPK = 16
EPS = 1e-6
NEG = -1e30
SCALE = HD ** -0.5
RING = 6
UNIT = 2048
NU, NV = 8, 8
LAG = 8
ND = 16

U_IN, U_GLU, U_OUT, U_FF = 0, 8, 9, 13
U_IN2 = U_FF + 3 * NFF
U_SBO, U_DILO, U_OUT2, U_PQ, U_KEYS = U_IN2 + 23, U_IN2 + 25, U_IN2 + 26, U_IN2 + 30, U_IN2 + 38
UNITS = U_KEYS + 1

V_GMIX, V_GFFN, V_GSSM, V_GATT, V_D, V_BGLU, V_GMIX2, V_C, V_LRE, V_LIM, V_LDT = 0, 8, 16, 20, 24, 28, 32, 40, 48, 64, 80
NVEC = 96

C_ID, C_REV, C_TRI, C_ONE, C_MASK1, C_NEGM, C_BIAS, C_DM0, C_DM1, C_COS, C_SIN, C_IOTA = (
    0, 128, 256, 384, 512, 1024, 1408, 1792, 2176, 2944, 3072, 3200)
NCONST = 3216


def build(nc, x, consts, vecs, weights, ssm_b, ssm_c, rel_ext, g_final1, w_ada, b_ada, g_ffn2, g_final2,
          peer_u, peer_v, out, dbg=None):
    with ExitStack() as ctx:
        def sem(name):
            return ctx.enter_context(nc.semaphore(name))

        arena = ctx.enter_context(nc.sbuf_tensor("arena", [P, 53100], F32))
        psum = ctx.enter_context(nc.psum_tensor("psum", [P, 8, 512], F32))

        top = [0]

        def take(words, at=None):
            a = top[0] if at is None else at
            if at is None:
                top[0] += words
            assert a + words <= 53100, (a, words)
            return arena[:, a:a + words]

        cst = take(NCONST)
        vec = take(NVEC)
        xres = take(NT * D).rearrange("p (t d) -> p t d", t=NT)
        hT = take(KD * SEQ).rearrange("p (k s) -> p k s", k=KD)
        ring = take(RING * UNIT).rearrange("p (r w) -> p r w", r=RING)
        stat = take(256)
        ada_at = top[0]
        ada_slot = take(4096).rearrange("p (k n) -> p k n", k=KD)
        ada_acc = take(6144)
        ph = top[0]

        ident = cst[:, C_ID:C_ID + P]
        rev = cst[:, C_REV:C_REV + P]
        tri = cst[:, C_TRI:C_TRI + P]
        ones = cst[:, C_ONE:C_ONE + P]
        mask1 = cst[:, C_MASK1:C_MASK1 + 512].rearrange("p (t k) -> p t k", t=2)
        negm = cst[:, C_NEGM:C_NEGM + 384]
        sbias = cst[:, C_BIAS:C_BIAS + 384]
        dmask = [cst[:, C_DM0:C_DM0 + 384].rearrange("p (g k) -> p g k", g=DIL),
                 cst[:, C_DM1:C_DM1 + 768].rearrange("p (g k) -> p g k", g=DIL)]
        cos = cst[:, C_COS:C_COS + 128].rearrange("p (t d) -> p t d", t=NT)
        sin = cst[:, C_SIN:C_SIN + 128].rearrange("p (t d) -> p t d", t=NT)
        iota = cst[:, C_IOTA:C_IOTA + TOPK]

        o = ph
        Z = take(8192, o).rearrange("p (j r t) -> p j r t", j=NST, r=2); zo = o; o += 8192
        T1 = take(1024, o).rearrange("p (j r t) -> p j r t", j=2, r=2); o += 1024
        T2 = take(1024, o).rearrange("p (j r t) -> p j r t", j=2, r=2); o += 1024
        T1v = lambda c: arena[:, zo + 8192 + 256 * c:zo + 8192 + 256 * (c + 1)]
        BZ = take(1024, o).rearrange("p (c r m) -> p c r m", c=4, r=2); o += 1024
        CT = take(1024, o).rearrange("p (j r m) -> p j r m", j=NST, r=2); o += 1024
        CP = take(1024, o).rearrange("p (j r m) -> p j r m", j=NST, r=2); o += 1024
        uT = take(1024, o).rearrange("p (c s) -> p c s", c=4); o += 1024
        qT = take(1024, o).rearrange("p (c s) -> p c s", c=4); o += 1024
        kT = take(1024, o).rearrange("p (c s) -> p c s", c=4); o += 1024
        vN = take(1024, o).rearrange("p (t c) -> p t c", t=NT); o += 1024
        HB = take(2048, o).rearrange("p (h m) -> p h m", h=HEADS); o += 2048
        S1 = take(1024, o).rearrange("p (b t k) -> p b t k", b=2, t=2); o += 1024
        PT1 = take(768, o).rearrange("p (b k) -> p b k", b=2); o += 768
        sm1 = take(256, o); o += 256
        E = take(8192, ada_at).rearrange("p (j r t) -> p j r t", j=NST, r=2)
        mixT = take(2048, ada_at + 8192).rearrange("p (k s) -> p k s", k=KD)
        xn1 = take(2048, zo).rearrange("p (t d) -> p t d", t=NT)
        etmp = take(4096, zo + 2048)
        gy = take(1024, zo).rearrange("p (c s) -> p c s", c=4)
        sg = take(1024, zo + 1024).rearrange("p (c s) -> p c s", c=4)
        sqr = take(2048, zo + 2048).rearrange("p (c s) -> p c s", c=KD)
        cv = take(512, zo + 4096)
        cq = take(512, zo + 4608)
        cy = take(512, zo + 5120)
        ct = take(512, zo + 5632)
        fo = zo + 8192
        silu = take(1024, fo).rearrange("p (b n) -> p b n", b=2)
        actT = take(1024, fo + 1024).rearrange("p (b f s) -> p b f s", b=2, f=2)
        gfin1 = take(1024, fo + 2048)
        xn2 = take(2048, zo + 6144).rearrange("p (t d) -> p t d", t=NT)
        coef = [sm1[:, 16 * i:16 * i + 16] for i in range(16)]
        ssq, var, sq, rstd, nt1 = (stat[:, 2 * i:2 * i + 2] for i in range(5))
        siluc = stat[:, 16:24]
        modc = stat[:, 32:48]
        gm2 = stat[:, 48:56]
        mx1, nmx1 = stat[:, 64:68], stat[:, 68:72]
        sum1, rs1 = stat[:, 72:76], stat[:, 76:80]
        junk = stat[:, 80:81]

        o = ph
        qkd = take(3072, o).rearrange("p (t n) -> p t n", t=NT); o += 3072
        vd = take(1536, o).rearrange("p (t n) -> p t n", t=NT); o += 1536
        vsb = take(1024, o).rearrange("p (t n) -> p t n", t=NT); o += 1024
        qTs = take(1024, o).rearrange("p (c s) -> p c s", c=4); o += 1024
        kTs = take(1024, o).rearrange("p (c s) -> p c s", c=4); o += 1024
        gT = take(4096, o).rearrange("p (c s) -> p c s", c=16); o += 4096
        ropeA = take(1536, o); o += 1536
        ropeB = take(1536, o); o += 1536
        qkdT = take(3072, o).rearrange("p (c s) -> p c s", c=12); o += 3072
        xn3 = take(2048, o - 3072).rearrange("p (t d) -> p t d", t=NT)
        sba = take(768, o).rearrange("p (b n) -> p b n", b=2); o += 768
        sbl = take(768, o).rearrange("p (b n) -> p b n", b=2); o += 768
        S2 = take(1536, o).rearrange("p (b n) -> p b n", b=2); o += 1536
        PT2 = take(1536, o).rearrange("p (b n) -> p b n", b=2); o += 1536
        tmp2 = S2[:, 0, 0:512]
        rows = take(4096, ada_at).rearrange("p (v d) -> p v d", v=4)
        aa = ada_at + 4096
        osbT = take(1024, aa).rearrange("p (c s) -> p c s", c=4)
        odT = take(512, aa + 1024).rearrange("p (c s) -> p c s", c=2)
        merT = take(2048, aa + 1536).rearrange("p (c s) -> p c s", c=KD)
        gffn2r = take(1024, aa + 3584)
        gfin2r = take(1024, aa + 4608)

        o = ph
        h2 = take(2048, o).rearrange("p (t d) -> p t d", t=NT); o += 2048
        sub = take(16 * 256, o); o += 16 * 256
        U = ring[:, 0:4, :].rearrange("p r w -> p (r w)").rearrange("p (b d) -> p b d", b=NU)
        qpT = take(4096, o).rearrange("p (c s) -> p c s", c=16)
        V = take(NV * 1024, o).rearrange("p (b d) -> p b d", b=NV); o += NV * 1024
        stg = take(512, o).rearrange("p (b n) -> p b n", b=2); o += 512
        stop = take(64, o).rearrange("p (b q k) -> p b q k", b=2, q=2); o += 64
        itop = take(64, o).bitcast(U32).rearrange("p (b q k) -> p b q k", b=2, q=2); o += 64
        itopf = take(32, o).rearrange("p (q k) -> p q k", q=2); o += 32
        cand = take(256, o); o += 256
        best = take(16, o); o += 16
        pos = take(16, o).bitcast(U32); o += 16
        ij = take(32, o).bitcast(U32).rearrange("p (q k) -> p q k", q=2); o += 32
        ijf = take(32, o).rearrange("p (q k) -> p q k", q=2); o += 32
        oh = take(512, o).rearrange("p (q k i) -> p q k i", q=2, k=TOPK); o += 512
        e12 = take(32, o).rearrange("p (q k) -> p q k", q=2); o += 32
        expert = take(32, o).bitcast(U32).rearrange("p (b k) -> p b k", b=2); o += 32
        gate = take(32, o).rearrange("p (b k) -> p b k", b=2); o += 32
        gexp = take(16, o); o += 16
        gnb, gsum, grs = take(1, o), take(1, o + 1), take(1, o + 2); o += 4
        dots = take(32, o).rearrange("p (b k) -> p b k", b=2); o += 32
        gel = take(32, o).rearrange("p (b k) -> p b k", b=2); o += 32
        diag = hT.rearrange("p k s -> p (k s)").rearrange("p (b m) -> p b m", b=ND)
        fin = take(1024, aa + 1536)

        x_in, c_in, vec_in, b_in, cc_in, h_in = (sem(n) for n in ("x_in", "c_in", "vec_in", "b_in", "cc_in", "h_in"))
        gf_in, bada_in, ada_in, rows_in, out_done = (sem(n) for n in ("gf_in", "bada_in", "ada_in", "rows_in", "out_done"))
        unit_in = [sem(f"unit_in{s}") for s in range(RING)]
        units_used = sem("units_used")
        dve_step = sem("dve_step")
        act_step = sem("act_step")
        var_ready, sqrt_ready = sem("var_ready"), sem("sqrt_ready")
        xn_ready = sem("xn_ready")
        turned = sem("turned")
        hT_act, hT_dve = sem("hT_act"), sem("hT_dve")
        proj_out = sem("proj_out")
        trig_in, trig_out = sem("trig_in"), sem("trig_out")
        bu_ready, bu_used = sem("bu_ready"), sem("bu_used")
        cp_ready = sem("cp_ready")
        states_ready, y_ready = sem("states_ready"), sem("y_ready")
        sc_ready, masked, probs, probs_n, pT_ready, pT_out, o_ready, o_out = (
            sem(n) for n in ("sc_ready", "masked", "probs", "probs_n", "pT_ready", "pT_out", "o_ready", "o_out"))
        yd_ready, gy_ready, sig_ready, glu_ready, sqr_ready, csum_ready, mix_ready = (
            sem(n) for n in ("yd_ready", "gy_ready", "sig_ready", "glu_ready", "sqr_ready", "csum_ready", "mix_ready"))
        xadd = sem("xadd")
        silu_ready, act_ready = sem("silu_ready"), sem("act_ready")
        ada_used, ada_ready, siluc_ready, acc_zero = (sem(n) for n in ("ada_used", "ada_ready", "siluc_ready", "acc_zero"))
        mod_ready, modc_out, rows_out = sem("mod_ready"), sem("modc_out"), sem("rows_out")
        x_final1 = sem("x_final1")
        z_ready, e_ready, l_ready, ex_ready, cum_ready, at_ready = (
            sem(n) for n in ("z_ready", "e_ready", "l_ready", "ex_ready", "cum_ready", "at_ready"))
        sbo_ready, sbo_out = sem("sbo_ready"), sem("sbo_out")
        roped, qkT_ready, qkT_out = sem("roped"), sem("qkT_ready"), sem("qkT_out")
        dsc_ready, dmasked, dprobs, dprobs_n, dpT_ready, dpT_out, do_ready, do_out = (
            sem(n) for n in ("dsc_ready", "dmasked", "dprobs", "dprobs_n", "dpT_ready", "dpT_out", "do_ready", "do_out"))
        br_ready, mer_ready = sem("br_ready"), sem("mer_ready")
        grow_ready, h2_ready = sem("grow_ready"), sem("h2_ready")
        sub_ready, sub_out = sem("sub_ready"), sem("sub_out")
        staged, routing, best_ready, gexp_ready, routed = (
            sem(n) for n in ("staged", "routing", "best_ready", "gexp_ready", "routed"))
        u_in = [sem(f"u_in{b}") for b in range(NU)]
        v_in = [sem(f"v_in{b}") for b in range(NV)]
        u_used = sem("u_used")
        v_used = sem("v_used")
        gelued, diag_ready, tile_done, acc_out = (
            sem(n) for n in ("gelued", "diag_ready", "tile_done", "acc_out"))
        zeros_ready = sem("zeros_ready")
        idx_read = sem("idx_read")
        peer_go = sem("peer_go")

        zeros = ring[:, 5, 0:512]

        block = ctx.enter_context(nc.Block())

        def stepper(eng, own):
            counts = {}

            def mark(ins, s=own, loop=None):
                ins.then_inc(s, 1)
                counts[s.name] = counts.get(s.name, 0) + 1
                return counts[s.name]

            def step(ins, s=own):
                eng.wait_ge(s, mark(ins, s))

            return mark, step

        @block.sync
        def _(sp):
            for s in range(RING):
                sp.dma_start(ring[:, s, :], weights[s]).then_inc(unit_in[s], 16)
            rounds = (UNITS - RING) // RING
            with sp.Fori(0, rounds) as i:
                for s in range(RING):
                    sp.wait_ge(units_used, i * RING + s + 1)
                    sp.dma_start(ring[:, s, :], weights[bass.ds((i + 1) * RING + s, 1)].rearrange("a p w -> (a p) w")
                                 ).then_inc(unit_in[s], 16)
            for n in range(RING * (rounds + 1), UNITS):
                sp.wait_ge(units_used, n - RING + 1)
                sp.dma_start(ring[:, n % RING, :], weights[n]).then_inc(unit_in[n % RING], 16)
            for t in range(NT):
                sp.wait_ge(acc_out, t + 1)
                sp.dma_start(out[t * P:(t + 1) * P, :], xres[:, t, :]).then_inc(out_done, 16)
            sp.wait_ge(out_done, 16 * NT)
            if dbg is not None:
                sp.dma_start(dbg, arena[:, :]).then_inc(out_done, 16)
                sp.wait_ge(out_done, 16 * (NT + 1))

        @block.gpsimd
        def _(pool):
            pool.dma_start(BZ, ssm_b).then_inc(b_in, 16)
            pool.dma_start(CT, ssm_c).then_inc(cc_in, 16)
            for h in range(HEADS):
                src = bass.AP(rel_ext.tensor, h * 384, [[1, P], [1, 256]])
                pool.dma_start(HB[:, h, :], src).then_inc(h_in, 16)
            pool.wait_ge(acc_zero, 1)
            pool.dma_start(ada_acc[0:1, :], b_ada).then_inc(bada_in, 16)
            pool.wait_ge(xadd, 4)
            pool.dma_start(gfin1, g_final1.partition_broadcast(P)).then_inc(gf_in, 16)
            pool.dma_start(ada_slot, w_ada[0].rearrange("p (k n) -> p k n", k=KD)).then_inc(ada_in, 16)
            with pool.Fori(0, 11) as i:
                pool.wait_ge(ada_used, i + 1)
                pool.nop()
                pool.dma_start(ada_slot, w_ada[bass.ds(i + 1, 1)].rearrange("a p (k n) -> (a p) k n", k=KD)
                               ).then_inc(ada_in, 16)
            pool.wait_ge(mod_ready, 9)
            pool.wait_ge(rows_out, 8)
            pool.dma_start(gffn2r, g_ffn2.partition_broadcast(P)).then_inc(rows_in, 16)
            pool.dma_start(gfin2r, g_final2.partition_broadcast(P)).then_inc(rows_in, 16)
            pool.wait_ge(sub_out, 8)
            pool.wait_ge(peer_go, 1)

            def gather(table, buf, used, ahead, arrived, b, k, n, read=None):
                turn = pool.to_reg(n + ahead)
                pool.wait_ge(peer_go, 1)
                pool.wait_ge(used, turn)
                pool.indirect_dma_start(buf, None, table, bass.IndirectOffsetOnAxis(ap=expert[:, b, k:k + 1], axis=0),
                                        engine_sem=read).then_inc(arrived, 16)

            def row_u(b, k, n):
                gather(peer_u, U[:, k % NU, :], u_used, 1, u_in[k % NU], b, k, n)

            def row_v(b, k, n):
                gather(peer_v, V[:, k % NV, :], v_used, ND - NV + 1, v_in[k % NV], b, k, n, idx_read if k == TOPK - 1 else None)

            def head(b, m, last=False):
                for k in range(TOPK):
                    row_v(b, k, m * TOPK + k)
                    if k < TOPK - LAG:
                        row_u(b, k + LAG, m * TOPK + (k + LAG))
                    elif not last:
                        if k == TOPK - LAG:
                            following = pool.to_reg(m + 2)
                            pool.wait_ge(peer_go, 1)
                            pool.wait_ge(routed, following)
                        row_u(1 - b, k + LAG - TOPK, m * TOPK + (k + LAG))

            pool.wait_ge(routed, 1)
            for k in range(LAG):
                row_u(0, k, k)
            with pool.Fori(0, NT * PEER_HEADS // 2 - 1) as i:
                head(0, i * 2)
                head(1, i * 2 + 1)
            head(0, 14)
            head(1, 15, last=True)

        @block.tensor
        def _(pe):
            mm = nc.tensor.matmul

            def unit(n, i=None, per=1):
                value = 16 * (n // RING + 1)
                pe.wait_ge(unit_in[n % RING], value if i is None else i * (16 * per) + value)
                return ring[:, n % RING, :]

            def turn(src, want):
                for k in range(KD):
                    for t in range(NT):
                        if k == 0:
                            pe.wait_ge(xn_ready, want + t + 1)
                        ins = nc.tensor.transpose(
                            psum[:, 4 + k // 2, (k % 2) * 256 + t * P:(k % 2) * 256 + (t + 1) * P],
                            src[:, t, k * P:(k + 1) * P], ident)
                    if k % 2 == 1:
                        ins.then_inc(turned, 1)

            def have_hT(n):
                pe.wait_ge(hT_act, 4 * n)
                pe.wait_ge(hT_dve, 4 * n)

            def block_T(banks, lo, hi, src, chunks=4):
                for c in range(chunks):
                    for k in range(KD):
                        w = (lo if k < 4 else hi).rearrange("p (k n) -> p k n", k=4)
                        ins = mm(psum[:, banks + c // 2, (c % 2) * 256:(c % 2) * 256 + 256],
                                 w[:, k % 4, c * P:(c + 1) * P], src[:, k, :], start=k == 0, stop=k == KD - 1)
                return ins

            def block_N(banks, lo, hi, src):
                for t in range(NT):
                    for k in range(KD):
                        w = (lo if k < 4 else hi).rearrange("p (k n) -> p k n", k=4)
                        ins = mm(psum[:, banks + t, :], src[:, k, t * P:(t + 1) * P], w[:, k % 4, :],
                                 start=k == 0, stop=k == KD - 1)
                return ins

            pe.wait_ge(c_in, 16)
            turn(xn1, 0)
            have_hT(1)
            pe.wait_ge(b_in, 16)

            def bu(q):
                if q < 2:
                    pe.wait_ge(hT_act, 4); pe.wait_ge(hT_dve, 4)
                else:
                    pe.wait_ge(bu_used, q - 1)
                for j in (2 * q, 2 * q + 1):
                    r = 32 * (j % 4)
                    for ri in range(2):
                        ins = mm(psum[:, 4 + j % 4, ri * 256:ri * 256 + 256], BZ[r:r + 32, j // 4, ri, :],
                                 uT[r:r + 32, j // 4, :], start=True, stop=True)
                ins.then_inc(bu_ready, 1)

            for b in range(4):
                lo, hi = unit(U_IN + 2 * b), unit(U_IN + 2 * b + 1)
                if b >= 2:
                    pe.wait_ge(proj_out, 2 * (b - 1))
                (block_T if b < 3 else block_N)(2 * (b % 2), lo, hi, hT).then_inc(units_used, 2)
                if b == 0:
                    pe.wait_ge(proj_out, 2)
                bu(2 * b)
                bu(2 * b + 1)

            pe.wait_ge(proj_out, 8)
            pe.wait_ge(h_in, 16 * HEADS)

            def scores(h):
                r, c = 64 * (h % 2), h // 2
                if h >= 2:
                    pe.wait_ge(masked, h - 1)
                bank = psum[:, h % 2, :].rearrange("p (t k) -> p t k", t=2)
                for t in range(NT):
                    mm(bank[:, t, :], qT[r:r + 64, c, t * P:(t + 1) * P], kT[r:r + 64, c, :], start=True, stop=False)
                    if t == 0:
                        mm(bank[:, 0, 0:P], rev, HB[:, h, P:2 * P], start=False, stop=True)
                    else:
                        ins = mm(bank[:, 1, :], rev, HB[:, h, :], start=False, stop=True)
                ins.then_inc(sc_ready, 1)

            def turn_probs(h):
                pe.wait_ge(probs_n, h + 1)
                if h >= 2:
                    pe.wait_ge(pT_out, h - 1)
                for n, (t, k) in enumerate(((0, 0), (1, 0), (1, 1))):
                    ins = nc.tensor.transpose(psum[:, 2 + h % 2, n * P:(n + 1) * P], S1[:, h % 2, t, k * P:(k + 1) * P], ident)
                ins.then_inc(pT_ready, 1)

            def values(h):
                pe.wait_ge(pT_out, h + 1)
                if h % 2 == 0 and h >= 4:
                    pe.wait_ge(o_out, h // 2 - 1)
                if h < 4:
                    pe.wait_ge(bu_used, 8)
                dst = psum[64 * (h % 2):64 * (h % 2) + 64, 4 + (h // 2) % 2, :]
                mm(dst[:, 0:256], vN[:, 0, h * HD:(h + 1) * HD], PT1[:, h % 2, 0:256], start=True, stop=False)
                mm(dst[:, P:256], vN[:, 1, h * HD:(h + 1) * HD], PT1[:, h % 2, 256:384],
                   start=False, stop=True).then_inc(o_ready, 1)

            for h in range(HEADS + 2):
                if h < HEADS:
                    scores(h)
                if 1 <= h <= HEADS:
                    turn_probs(h - 1)
                if h >= 2:
                    values(h - 2)

            pe.wait_ge(cp_ready, 1)
            for q in range(NST // 2):
                pe.wait_ge(states_ready, q + 1)
                for j in (2 * q, 2 * q + 1):
                    c, r = j // 4, 32 * (j % 4)
                    dst = psum[r:r + 32, 6 + c // 2, (c % 2) * 256:(c % 2) * 256 + 256]
                    for ri in range(2):
                        ins = mm(dst, CP[:, j, ri, :], Z[:, j, ri, :], start=ri == 0, stop=ri == 1)
            ins.then_inc(y_ready, 1)

            glu = unit(U_GLU).rearrange("p (k n) -> p k n", k=4)
            pe.wait_ge(gy_ready, 4)
            for c in range(4):
                for k in range(4):
                    ins = mm(psum[:, c // 2, (c % 2) * 256:(c % 2) * 256 + 256], glu[:, k, c * P:(c + 1) * P],
                             gy[:, k, :], start=k == 0, stop=k == 3)
            ins.then_inc(units_used, 1)

            pe.wait_ge(sqr_ready, 2)
            for br in range(2):
                for k in range(4):
                    ins = mm(psum[:, 2, br * 256:br * 256 + 256], ones, sqr[:, 4 * br + k, :], start=k == 0, stop=k == 3)
            ins.then_inc(csum_ready, 1)

            pe.wait_ge(mix_ready, 8)
            for b in range(2):
                lo, hi = unit(U_OUT + 2 * b), unit(U_OUT + 2 * b + 1)
                block_N(2 * b, lo, hi, mixT).then_inc(units_used, 2)

            pe.wait_ge(xadd, 4)
            turn(xn2, 2)
            have_hT(2)

            def gate_up(par, n, f, i=None):
                g, u = unit(n, i), unit(n + 1, i)
                if f >= 2:
                    pe.wait_ge(act_ready, f - 1 if i is None else i * 2 + (f - 1))
                for which, w in enumerate((g, u)):
                    w = w.rearrange("p (k n) -> p k n", k=KD)
                    for s in range(2):
                        for k in range(KD):
                            ins = mm(psum[:, 4 + 2 * par + which, s * 256:s * 256 + 256], w[:, k, s * P:(s + 1) * P],
                                     hT[:, k, :], start=k == 0, stop=k == KD - 1)
                ins.then_inc(units_used, 2)

            def down(par, n, f, i=None):
                w = unit(n, i).rearrange("p (s n) -> p s n", s=2)
                pe.wait_ge(act_ready, f + 1 if i is None else i * 2 + (f + 1))
                first, last = (f == 0), (i is None and f == NFF - 1)
                for s in range(2):
                    for t in range(NT):
                        for b in range(2):
                            ins = mm(psum[:, 2 * t + b, :], actT[:, par, s, t * P:(t + 1) * P], w[:, s, b * 512:(b + 1) * 512],
                                     start=first and s == 0, stop=last and s == 1, skip_group_check=True)
                ins.then_inc(units_used, 1)

            gate_up(0, U_FF, 0)
            gate_up(1, U_FF + 2, 1)
            down(0, U_FF + 4, 0)
            gate_up(0, U_FF + 5, 2)
            down(1, U_FF + 7, 1)
            with pe.Fori(0, 4) as i:
                gate_up(1, U_FF + 8, 3, i)
                down(0, U_FF + 10, 2, i)
                gate_up(0, U_FF + 11, 4, i)
                down(1, U_FF + 13, 3, i)
            down(0, U_FF + 32, 10)

            pe.wait_ge(ada_ready, 1)
            for n in range(16):
                ins = mm(psum[:, 4, n:n + 1], ada_acc[:, n * P:(n + 1) * P], ones[:, 0:1], start=True, stop=True)
            ins.then_inc(mod_ready, 1)
            for n in range(8):
                bank = 5 + n % 2
                if n >= 2:
                    pe.wait_ge(rows_out, n - 1)
                mm(psum[:, bank, :], ones, ada_acc[:, 2048 + n * 512:2048 + (n + 1) * 512],
                   start=True, stop=True).then_inc(mod_ready, 1)

            pe.wait_ge(modc_out, 1)
            pe.wait_ge(rows_out, 8)
            turn(xn3, 4)
            have_hT(3)
            n = U_IN2
            for b in range(12):
                if b >= 2:
                    pe.wait_ge(proj_out, 8 + 2 * (b - 1))
                if b == 7:
                    w = unit(n).rearrange("p (k n) -> p k n", k=KD)
                    for t in range(NT):
                        for k in range(KD):
                            ins = mm(psum[:, 2 * (b % 2) + t, 0:256], hT[:, k, t * P:(t + 1) * P], w[:, k, :],
                                     start=k == 0, stop=k == KD - 1)
                    ins.then_inc(units_used, 1)
                    n += 1
                    continue
                lo, hi = unit(n), unit(n + 1)
                (block_T if b < 2 or b > 7 else block_N)(2 * (b % 2), lo, hi, hT).then_inc(units_used, 2)
                n += 2

            for c in range(12):
                if c == 0:
                    pe.wait_ge(roped, 2)
                if c >= 8 and c % 2 == 0:
                    pe.wait_ge(qkT_out, c // 2 - 3)
                for t in range(NT):
                    ins = nc.tensor.transpose(
                        psum[:, 4 + (c // 2) % 4, (c % 2) * 256 + t * P:(c % 2) * 256 + (t + 1) * P],
                        qkd[:, t, c * P:(c + 1) * P], ident)
                if c % 2 == 1:
                    ins.then_inc(qkT_ready, 1)

            pe.wait_ge(proj_out, 8 + 24)

            def logits(h, bank, stop):
                r, c = 64 * (h % 2), h // 2
                mm(psum[:, bank, 0:256], kTs[r:r + 64, c, 0:P], qTs[r:r + 64, c, :], start=True, stop=stop)
                if not stop:
                    mm(psum[:, bank, 0:256], tri, sbl[:, h % 2, 0:256], start=False, stop=False)
                    mm(psum[:, bank, P:256], ones, sbl[:, h % 2, 256:384], start=False, stop=True)
                ins = mm(psum[:, bank, 256:384], kTs[r:r + 64, c, P:256], qTs[r:r + 64, c, P:256], start=True, stop=stop)
                if not stop:
                    ins = mm(psum[:, bank, 256:384], tri, sbl[:, h % 2, 256:384], start=False, stop=True)
                return ins

            for h in range(HEADS + 2):
                if h < HEADS:
                    if h >= 2:
                        pe.wait_ge(l_ready, h - 1)
                    logits(h, h % 2, True).then_inc(z_ready, 1)
                if 1 <= h <= HEADS:
                    g = h - 1
                    pe.wait_ge(l_ready, g + 1)
                    if g >= 2:
                        pe.wait_ge(ex_ready, g - 1)
                    logits(g, 2 + g % 2, False).then_inc(cum_ready, 1)
                if h >= 2:
                    g = h - 2
                    pe.wait_ge(at_ready, g + 1)
                    if g == 0:
                        pe.wait_ge(qkT_out, 6)
                    if g % 2 == 0 and g >= 4:
                        pe.wait_ge(sbo_out, g // 2 - 1)
                    dst = psum[64 * (g % 2):64 * (g % 2) + 64, 4 + (g // 2) % 2, :]
                    mm(dst[:, 0:256], vsb[:, 0, g * HD:(g + 1) * HD], sba[:, g % 2, 0:256], start=True, stop=False)
                    mm(dst[:, P:256], vsb[:, 1, g * HD:(g + 1) * HD], sba[:, g % 2, 256:384],
                       start=False, stop=True).then_inc(sbo_ready, 1)

            def dunit(n):
                return n % NT, n // NT

            def dscores(n):
                t, i = dunit(n)
                if n < 2:
                    pe.wait_ge(ex_ready, HEADS)
                if n >= 2:
                    pe.wait_ge(dmasked, n - 1)
                keys = P * (t + 1)
                for g in range(DIL):
                    hd = g * DIL_HEADS + i
                    r, c = 64 * (hd % 2), hd // 2
                    bank, off = 2 * (n % 2) + (g * keys) // 512, (g * keys) % 512
                    ins = mm(psum[:, bank, off:off + keys], qkdT[r:r + 64, c, t * P:(t + 1) * P],
                             qkdT[r:r + 64, 6 + c, 0:keys], start=True, stop=True)
                ins.then_inc(dsc_ready, 1)

            def dturn(n):
                t, i = dunit(n)
                pe.wait_ge(dprobs_n, n + 1)
                if n == 0:
                    pe.wait_ge(sbo_out, 4)
                if n >= 1:
                    pe.wait_ge(dpT_out, n)
                for m in range(DIL * (t + 1)):
                    ins = nc.tensor.transpose(psum[:, 4 + m // 4, (m % 4) * P:(m % 4 + 1) * P],
                                              S2[:, n % 2, m * P:(m + 1) * P], ident)
                ins.then_inc(dpT_ready, 1)

            def dvalues(n):
                t, i = dunit(n)
                pe.wait_ge(dpT_out, n + 1)
                dst = psum[64 * (i % 2):64 * (i % 2) + 64, 6 + (i // 2) % 2, t * P:(t + 1) * P]
                for m in range(DIL * (t + 1)):
                    g, st = m // (t + 1), m % (t + 1)
                    hd = g * DIL_HEADS + i
                    ins = mm(dst, vd[:, st, hd * HD:(hd + 1) * HD], PT2[:, n % 2, m * P:(m + 1) * P],
                             start=m == 0, stop=m == DIL * (t + 1) - 1)
                ins.then_inc(do_ready, 1)

            for n in range(8 + 2):
                if n < 8:
                    dscores(n)
                if 1 <= n <= 8:
                    dturn(n - 1)
                if n >= 2:
                    dvalues(n - 2)

            pe.wait_ge(do_out, 2)
            wsb = [unit(U_SBO), unit(U_SBO + 1)]
            wdl = unit(U_DILO).rearrange("p (k n) -> p k n", k=2)
            for c in range(KD):
                if c >= 4:
                    pe.wait_ge(mer_ready, c - 3)
                ws = wsb[c // 4].rearrange("p (k n) -> p k n", k=4)
                for k in range(4):
                    mm(psum[:, c % 4, 0:256], ws[:, k, (c % 4) * P:(c % 4 + 1) * P], osbT[:, k, :], start=k == 0, stop=k == 3)
                for k in range(2):
                    ins = mm(psum[:, c % 4, 256:512], wdl[:, k, c * P:(c + 1) * P], odT[:, k, :], start=k == 0, stop=k == 1)
                ins.then_inc(br_ready, 1)

            pe.wait_ge(mer_ready, KD)
            for b in range(2):
                lo, hi = unit(U_OUT2 + 2 * b), unit(U_OUT2 + 2 * b + 1)
                block_N(2 * b, lo, hi, merT).then_inc(units_used, 5 if b == 0 else 2)

            turn(h2, 6)
            have_hT(4)
            for b in range(4):
                if b == 0:
                    pe.wait_ge(xadd, 12)
                if b >= 2:
                    pe.wait_ge(proj_out, 32 + 2 * (b - 1))
                lo, hi = unit(U_PQ + 2 * b), unit(U_PQ + 2 * b + 1)
                block_T(2 * (b % 2), lo, hi, hT).then_inc(units_used, 2)
            keys = unit(U_KEYS).rearrange("p (c n) -> p c n", c=16)
            pe.wait_ge(proj_out, 40)
            for t in range(NT):
                for g in range(4):
                    if t * 4 + g >= 4:
                        pe.wait_ge(sub_out, t * 4 + g - 3)
                    for c in range(4):
                        ins = mm(psum[:, 4 + g, c * P:(c + 1) * P], qpT[:, 4 * g + c, t * P:(t + 1) * P],
                                 keys[:, 4 * g + c, :], start=True, stop=True)
                    ins.then_inc(sub_ready, 1)

            for t in range(NT):
                acc = 2 * t
                pe.wait_ge(zeros_ready, 1)
                for b in range(2):
                    mm(psum[:, acc + b, :], ident, zeros, start=True, stop=False, skip_group_check=True)
                with pe.Fori(0, PEER_HEADS // 2) as i:
                    for b in range(2):
                        for k in range(TOPK):
                            v = k % NV
                            uses = (t * PEER_HEADS + b) * (TOPK // NV) + k // NV + 1
                            pe.wait_ge(v_in[v], i * (2 * TOPK // NV * 16) + 16 * uses)
                            if k % 4 == 0:
                                pe.wait_ge(diag_ready, i * 8 + (t * PEER_HEADS + b) * 4 + k // 4 + 1)
                            for c in range(2):
                                ins = mm(psum[:, acc + c, :], diag[:, k % ND, :], V[:, v, c * 512:(c + 1) * 512],
                                         start=False, stop=False, skip_group_check=True)
                            ins.then_inc(v_used, 1)
                for c in range(2):
                    ins = mm(psum[:, acc + c, :], ident, zeros, start=False, stop=True, skip_group_check=True)
                ins.then_inc(tile_done, 1)

        @block.scalar
        def _(act):
            mark, step = stepper(act, act_step)
            A = nc.scalar.activation
            act.dma_start(xres, x.rearrange("(t p) d -> p t d", p=P)).then_inc(x_in, 16)
            act.dma_start(vec, vecs).then_inc(vec_in, 16)
            act.dma_start(cst, consts).then_inc(c_in, 16)

            def root(n, src, dst):
                act.wait_ge(var_ready, n)
                mark(A(dst, src, ACT.Sqrt), sqrt_ready)

            def out_of_turn(n, scale, bias):
                for k in (0, 1, 4, 5):
                    act.wait_ge(turned, 4 * n + k // 2 + 1)
                    mark(A(hT[:, k, :], psum[:, 4 + k // 2, (k % 2) * 256:(k % 2) * 256 + 256], ACT.Identity, scale=scale(k), bias=bias(k)), hT_act)

            root(1, var, sq)
            act.wait_ge(vec_in, 16)
            out_of_turn(0, lambda k: vec[:, V_GMIX + k:V_GMIX + k + 1], lambda k: 0.0)
            act.wait_ge(trig_in, 1)
            mark(A(coef[3], coef[1], ACT.Sin), trig_out)
            mark(A(coef[2], coef[4], ACT.Sin), trig_out)

            def pair_out(done, banks, dst, scale=1.0, func=ACT.Copy, width=512):
                act.wait_ge(units_used, done)
                for t in range(2):
                    mark(A(dst(t), psum[:, banks + t, 0:width], func, scale=scale), proj_out)

            def cols(dst, at=0):
                return lambda t: dst[:, at + 2 * t:at + 2 * t + 2, :].rearrange("p c s -> p (c s)")

            pair_out(U_IN + 2, 0, cols(uT))
            pair_out(U_IN + 4, 2, cols(qT), SCALE)
            pair_out(U_IN + 6, 0, cols(kT))
            pair_out(U_IN + 8, 2, lambda t: vN[:, t, :])
            for h in range(HEADS + 1):
                if h < HEADS:
                    act.wait_ge(masked, h + 1)
                    for t in range(NT):
                        mark(A(S1[:, h % 2, t, :], S1[:, h % 2, t, :], ACT.Exp, bias=nmx1[:, 2 * (h % 2) + t:2 * (h % 2) + t + 1],
                               accum_out=sum1[:, 2 * (h % 2) + t:2 * (h % 2) + t + 1]), probs)
                if h >= 1:
                    g = h - 1
                    act.wait_ge(pT_ready, g + 1)
                    if g >= 2:
                        act.wait_ge(o_ready, g - 1)
                    mark(A(PT1[:, g % 2, :], psum[:, 2 + g % 2, 0:384], ACT.Copy), pT_out)
                if h >= 3 and h % 2 == 1:
                    c = (h - 3) // 2
                    act.wait_ge(o_ready, 2 * c + 2)
                    mark(A(mixT[:, 4 + c, :], psum[:, 4 + c % 2, 0:256], ACT.Copy), o_out)
            act.wait_ge(o_ready, HEADS)
            mark(A(mixT[:, 7, :], psum[:, 5, 0:256], ACT.Copy), o_out)
            for c in range(4):
                act.wait_ge(yd_ready, c + 1)
                mark(A(gy[:, c, :], T1v(c), ACT.Gelu_apprx_tanh), gy_ready)
            act.wait_ge(units_used, U_GLU + 1)
            for c in range(4):
                mark(A(sg[:, c, :], psum[:, c // 2, (c % 2) * 256:(c % 2) * 256 + 256], ACT.Sigmoid,
                       bias=vec[:, V_BGLU + c:V_BGLU + c + 1]), sig_ready)
            act.wait_ge(o_out, 4)
            mark(A(sqr[:, 4:8, :], mixT[:, 4:8, :], ACT.Square), sqr_ready)
            act.wait_ge(glu_ready, 4)
            mark(A(sqr[:, 0:4, :], mixT[:, 0:4, :], ACT.Square), sqr_ready)
            root(2, cv, cq)
            root(3, var, sq)
            out_of_turn(1, lambda k: vec[:, V_GFFN + k:V_GFFN + k + 1], lambda k: 0.0)
            mark(A(siluc, vec[:, V_C:V_C + 8], ACT.Silu), siluc_ready)

            def gate_out(par, done, f, i=None):
                act.wait_ge(units_used, done if i is None else i * 6 + done)
                if f >= 2:
                    act.wait_ge(act_ready, f - 1 if i is None else i * 2 + (f - 1))
                A(silu[:, par, :], psum[:, 4 + 2 * par, :], ACT.Silu).then_inc(silu_ready, 1)

            gate_out(0, U_FF + 2, 0)
            gate_out(1, U_FF + 4, 1)
            gate_out(0, U_FF + 7, 2)
            with act.Fori(0, 4) as i:
                gate_out(1, U_FF + 10, 3, i)
                gate_out(0, U_FF + 13, 4, i)
            root(4, var, sq)
            root(5, var, sq)
            for n in range(8):
                act.wait_ge(mod_ready, n + 2)
                if n == 0:
                    act.wait_ge(ada_ready, 1)
                mark(A(rows[:, n // 2, (n % 2) * 512:(n % 2 + 1) * 512], psum[:, 5 + n % 2, :], ACT.Copy), rows_out)
            act.wait_ge(modc_out, 2)
            out_of_turn(2, lambda k: gm2[:, k:k + 1], lambda k: modc[:, k:k + 1])
            d = U_IN2
            pair_out(d + 2, 0, cols(qTs), SCALE)
            pair_out(d + 4, 2, cols(kTs))
            pair_out(d + 6, 0, lambda t: vsb[:, t, :])
            for b in range(3):
                act.wait_ge(units_used, d + 8 + 2 * b)
                for t in range(NT):
                    src, dst = psum[:, 2 * ((3 + b) % 2) + t, :], qkd[:, t, b * 512:(b + 1) * 512]
                    if b == 1:
                        step(A(dst[:, 0:256], src[:, 0:256], ACT.Copy, scale=SCALE))
                        mark(A(dst[:, 256:512], src[:, 256:512], ACT.Copy), proj_out)
                    else:
                        mark(A(dst, src, ACT.Copy, scale=SCALE if b == 0 else 1.0), proj_out)
            pair_out(d + 14, 0, lambda t: vd[:, t, 0:512])
            pair_out(d + 15, 2, lambda t: vd[:, t, 512:768], width=256)
            for b in range(4):
                pair_out(d + 17 + 2 * b, 2 * (b % 2), cols(gT, 4 * b), func=ACT.Sigmoid)
            for c in range(6):
                act.wait_ge(qkT_ready, c + 1)
                mark(A(qkdT[:, 2 * c:2 * c + 2, :].rearrange("p c s -> p (c s)"), psum[:, 4 + c % 4, :], ACT.Copy), qkT_out)
            for h in range(HEADS + 2):
                if h < HEADS:
                    act.wait_ge(z_ready, h + 1)
                    b = h % 2
                    if h >= 2:
                        act.wait_ge(sbo_ready, h - 1)
                    step(A(sba[:, b, :], psum[:, b, 0:384], ACT.Abs))
                    step(A(sba[:, b, :], sba[:, b, :], ACT.Exp, scale=-1.0))
                    mark(A(sba[:, b, :], sba[:, b, :], ACT.Ln, bias=ones[:, 0:1]), e_ready)
                if h >= 1 and h <= HEADS:
                    g = h - 1
                    act.wait_ge(ex_ready, g + 1)
                    mark(A(sba[:, g % 2, :], sba[:, g % 2, :], ACT.Exp), at_ready)
                if h in (4, 6, 8):
                    c = h // 2 - 2
                    act.wait_ge(sbo_ready, 2 * c + 2)
                    mark(A(osbT[:, c, :], psum[:, 4 + c % 2, 0:256], ACT.Copy), sbo_out)
            act.wait_ge(sbo_ready, HEADS)
            mark(A(osbT[:, 3, :], psum[:, 5, 0:256], ACT.Copy), sbo_out)
            for n in range(8 + 2):
                if n < 8:
                    act.wait_ge(dmasked, n + 1)
                    w = DIL * P * (n % 2 + 1)
                    mark(A(S2[:, n % 2, 0:w], S2[:, n % 2, 0:w], ACT.Exp, bias=nmx1[:, n % 2:n % 2 + 1],
                           accum_out=sum1[:, n % 2:n % 2 + 1]), dprobs)
                if 1 <= n <= 8:
                    g = n - 1
                    act.wait_ge(dpT_ready, g + 1)
                    if g >= 2:
                        act.wait_ge(do_ready, g - 1)
                    w = DIL * P * (g % 2 + 1)
                    src = psum[:, 4:6, :].rearrange("p b n -> p (b n)")[:, 0:w]
                    mark(A(PT2[:, g % 2, 0:w], src, ACT.Copy), dpT_out)
                if n >= 5 and n % 4 == 1:
                    c = (n - 5) // 4
                    act.wait_ge(do_ready, 4 * c + 4)
                    mark(A(odT[:, c, :], psum[:, 6 + c, 0:256], ACT.Copy), do_out)
            root(6, var, sq)
            for b in (0, 2):
                act.wait_ge(turned, 12 + b + 1)
                step(A(hT[:, 2 * b, :], psum[:, 4 + b, 0:256], ACT.Copy), hT_act)
                step(A(hT[:, 2 * b + 1, :], psum[:, 4 + b, 256:512], ACT.Copy), hT_act)
            for b in range(4):
                pair_out(U_PQ + 2 * b + 2, 2 * (b % 2), cols(qpT, 4 * b))
            for n in range(8):
                act.wait_ge(sub_ready, n + 1)
                mark(A(sub[:, n * 512:(n + 1) * 512], psum[:, 4 + n % 4, :], ACT.Copy), sub_out)
            act.wait_ge(sub_out, 8)

            def stage(b, m):
                A(stg[:, b, :], sub[:, bass.ds(m * 256, 256)], ACT.Copy).then_inc(staged, 1)

            def gates(m):
                act.wait_ge(best_ready, m + 1)
                A(gexp[:, :], best[:, :], ACT.Exp, bias=gnb[:, :], accum_out=gsum[:, :]).then_inc(gexp_ready, 1)

            def gelus(b, m, quarters):
                for q in quarters:
                    act.wait_ge(u_used, m * TOPK + (4 * q + 4 + NU))
                    A(gel[:, b, 4 * q:4 * q + 4], dots[:, b, 4 * q:4 * q + 4], ACT.Gelu_apprx_tanh).then_inc(gelued, 1)

            def head(b, m, gate=True, more=True):
                gelus(b, m, (0, 1))
                if gate:
                    gates(m + 1)
                if more:
                    stage(1 - b, m + 3)
                gelus(b, m, (2, 3))

            stage(0, 0)
            stage(1, 1)
            gates(0)
            stage(0, 2)
            with act.Fori(0, 6) as i:
                head(0, i * 2)
                head(1, i * 2 + 1)
            head(0, 12)
            head(1, 13, more=False)
            head(0, 14, more=False)
            root(7, var, sq)
            head(1, 15, gate=False, more=False)
            root(8, var, sq)

        @block.vector
        def _(dve):
            mark, step = stepper(dve, dve_step)
            TT, TS = nc.vector.tensor_tensor, nc.vector.tensor_scalar
            STT = nc.vector.scalar_tensor_tensor
            roots = [0]

            def root(v, s, y, t):
                roots[0] += 1
                dve.wait_ge(sqrt_ready, roots[0])
                step(nc.vector.reciprocal(y, s))
                step(TT(t, y, y, ALU.mult))
                step(TT(t, t, v, ALU.mult))
                step(TS(t, t, -0.5, 1.5, ALU.mult, ALU.add))
                step(TT(y, y, t, ALU.mult))

            def norm(tiles=(0, 1), junk_at=None):
                lo, hi = tiles[0], tiles[-1] + 1
                for t in tiles:
                    step(nc.vector.tensor_tensor_reduce(out=junk_at, in0=xres[:, t, :], in1=xres[:, t, :], scale=1.0,
                                                        scalar=0.0, op0=ALU.mult, op1=ALU.add, accum_out=ssq[:, t:t + 1]))
                if len(tiles) == 1:
                    pass
                step(TS(var, ssq, 1.0 / D, EPS, ALU.mult, ALU.add), var_ready)
                root(var, sq, rstd, nt1)

            def hT_out(n, scale, bias=None):
                for k in (2, 3, 6, 7):
                    dve.wait_ge(turned, 4 * n + k // 2 + 1)
                    src = psum[:, 4 + k // 2, (k % 2) * 256:(k % 2) * 256 + 256]
                    if bias is None:
                        ins = TS(hT[:, k, :], src, scale(k), None, ALU.mult)
                    else:
                        ins = TS(hT[:, k, :], src, scale(k), bias(k), ALU.mult, ALU.add)
                    mark(ins, hT_dve)

            dve.wait_ge(x_in, 16)
            norm(junk_at=take(1024, zo + 2048))
            for t in range(NT):
                mark(TS(xn1[:, t, :], xres[:, t, :], rstd[:, t:t + 1], None, ALU.mult), xn_ready)

            dve.wait_ge(vec_in, 16)
            lre, lim, ldt = (vec[:, v:v + 16] for v in (V_LRE, V_LIM, V_LDT))
            r_, th, cs, sn, cth, dt, t_, n_, p_, den, kr, ki, lbr, lbi = coef[0:14]
            hT_out(0, lambda k: vec[:, V_GMIX + k:V_GMIX + k + 1])
            MAGIC = 1.5 * 2.0 ** 23

            def exp_exact(dst, src):
                step(TS(n_, src, 1.4426950408889634, MAGIC, ALU.mult, ALU.add))
                step(TS(n_, n_, MAGIC, None, ALU.subtract))
                step(TS(n_, n_, -126.0, 127.0, ALU.max, ALU.min))
                step(STT(out=t_, in0=n_, scalar=-0.693359375, in1=src, op0=ALU.mult, op1=ALU.add))
                step(STT(out=t_, in0=n_, scalar=2.12194440e-4, in1=t_, op0=ALU.mult, op1=ALU.add))
                step(TS(p_, t_, 1.0 / 5040, None, ALU.mult))
                for c in (720.0, 120.0, 24.0, 6.0, 2.0, 1.0):
                    step(STT(out=p_, in0=p_, scalar=1.0 / c, in1=t_, op0=ALU.add, op1=ALU.mult))
                step(TS(t_.bitcast(I32), n_, 127.0, 2.0 ** 23, ALU.add, ALU.mult))
                step(STT(out=dst, in0=p_, scalar=1.0, in1=t_, op0=ALU.add, op1=ALU.mult))

            exp_exact(dt, ldt)
            step(TT(th, lim, dt, ALU.mult))
            step(TT(den, lre, dt, ALU.mult))
            exp_exact(r_, den)
            step(TS(n_, th, 0.15915494309189535, MAGIC, ALU.mult, ALU.add))
            step(TS(n_, n_, MAGIC, None, ALU.subtract))
            for c in (6.28125, 1.9350051879882812e-3, 3.0199159819567e-7):
                step(STT(out=th, in0=n_, scalar=-c, in1=th, op0=ALU.mult, op1=ALU.add))
            step(TS(th, th, 3.1415925, -3.1415925, ALU.min, ALU.max))
            step(STT(out=cth, in0=th, scalar=-1.0, in1=th, op0=ALU.mult, op1=ALU.max))
            step(TS(cth, cth, -1.0, 1.5707963267948966, ALU.mult, ALU.add), trig_in)
            dve.wait_ge(trig_out, 2)
            step(TT(lbr, r_, cs, ALU.mult))
            step(TS(lbr, lbr, -1.0, None, ALU.add))
            step(TT(lbi, r_, sn, ALU.mult))
            step(TT(den, lre, lre, ALU.mult))
            step(TT(t_, lim, lim, ALU.mult))
            step(TT(den, den, t_, ALU.add))
            step(nc.vector.reciprocal(den, den))
            step(TT(kr, lbr, lre, ALU.mult))
            step(TT(t_, lbi, lim, ALU.mult))
            step(TT(kr, kr, t_, ALU.add))
            step(TT(kr, kr, den, ALU.mult))
            step(TT(ki, lbi, lre, ALU.mult))
            step(TT(t_, lbr, lim, ALU.mult))
            step(TT(ki, ki, t_, ALU.subtract))
            step(TT(ki, ki, den, ALU.mult))
            dve.wait_ge(cc_in, 16)
            wide = [P, NST, 32]
            tc1 = T1.rearrange("p j r t -> p (j r t)")[:, 0:512].rearrange("p (j m) -> p j m", j=NST)
            krb, kib = kr.unsqueeze(2).to_broadcast(wide), ki.unsqueeze(2).to_broadcast(wide)
            step(TT(CP[:, :, 0, :], CT[:, :, 0, :], krb, ALU.mult))
            step(TT(tc1, CT[:, :, 1, :], kib, ALU.mult))
            step(TT(CP[:, :, 0, :], CP[:, :, 0, :], tc1, ALU.subtract))
            step(TT(CP[:, :, 1, :], CT[:, :, 0, :], kib, ALU.mult))
            step(TT(tc1, CT[:, :, 1, :], krb, ALU.mult))
            step(STT(out=CP[:, :, 1, :], in0=CP[:, :, 1, :], scalar=-1.0, in1=tc1, op0=ALU.mult, op1=ALU.subtract), cp_ready)
            pr, pi = coef[14], coef[15]
            step(nc.vector.memset(E[:, :, 0, 0:1], 1.0))
            step(nc.vector.memset(E[:, :, 1, 0:1], 0.0))
            step(nc.vector.tensor_copy(pr, cs))
            step(nc.vector.tensor_copy(pi, sn))
            n = 1
            while n < SEQ:
                new, old = E[:, :, :, n:2 * n], E[:, :, :, 0:n]
                shape = [P, NST, 2, n]
                tmp = etmp[:, 0:NST * 2 * n].rearrange("p (j r t) -> p j r t", j=NST, r=2)
                mark(TT(new, old, pr.unsqueeze(2).unsqueeze(3).to_broadcast(shape), ALU.mult))
                step(TT(tmp, old, pi.unsqueeze(2).unsqueeze(3).to_broadcast(shape), ALU.mult))
                mark(TT(new[:, :, 0, :], new[:, :, 0, :], tmp[:, :, 1, :], ALU.subtract))
                step(TT(new[:, :, 1, :], new[:, :, 1, :], tmp[:, :, 0, :], ALU.add))
                if 2 * n < SEQ:
                    step(TT(t_, pr, pr, ALU.mult))
                    step(TT(p_, pi, pi, ALU.mult))
                    step(STT(out=pi, in0=pi, scalar=2.0, in1=pr, op0=ALU.mult, op1=ALU.mult))
                    step(TT(pr, t_, p_, ALU.subtract))
                n *= 2

            def e_pair(q, ri):
                return E[:, 2 * q:2 * q + 2, ri, :].unsqueeze(2).to_broadcast([P, 2, 2, SEQ])

            for q in range(NST // 2):
                dve.wait_ge(bu_ready, q + 1)
                b = 4 + 2 * (q % 2)
                src = psum[:, b:b + 2, :].rearrange("p j (r t) -> p j r t", r=2)
                z = Z[:, 2 * q:2 * q + 2, :, :]
                mark(TT(T1, src, e_pair(q, 0), ALU.mult))
                step(TT(T2, src, e_pair(q, 1), ALU.mult), bu_used)
                mark(TT(z[:, :, 0, :], T1[:, :, 0, :], T2[:, :, 1, :], ALU.add))
                step(TT(z[:, :, 1, :], T1[:, :, 1, :], T2[:, :, 0, :], ALU.subtract))

            for h in range(HEADS + 1):
                if h < HEADS:
                    b = h % 2
                    dve.wait_ge(sc_ready, h + 1)
                    if h >= 2:
                        dve.wait_ge(pT_ready, h - 1)
                    step(TT(S1[:, b, :, :], psum[:, b, :].rearrange("p (t k) -> p t k", t=2), mask1, ALU.add))
                    step(nc.vector.reduce_max(mx1[:, 2 * b:2 * b + 2], S1[:, b, :, :], AX))
                    step(TS(nmx1[:, 2 * b:2 * b + 2], mx1[:, 2 * b:2 * b + 2], -1.0, None, ALU.mult), masked)
                if h >= 1:
                    b = (h - 1) % 2
                    dve.wait_ge(probs, 2 * h)
                    step(nc.vector.reciprocal(rs1[:, 2 * b:2 * b + 2], sum1[:, 2 * b:2 * b + 2]))
                    step(TS(S1[:, b, 0, :], S1[:, b, 0, :], rs1[:, 2 * b:2 * b + 1], None, ALU.mult))
                    step(TS(S1[:, b, 1, :], S1[:, b, 1, :], rs1[:, 2 * b + 1:2 * b + 2], None, ALU.mult), probs_n)

            for q in range(NST // 2):
                for j in (2 * q, 2 * q + 1):
                    for ri in range(2):
                        ins = nc.vector.tensor_tensor_scan(Z[:, j, ri, :], r_[:, j:j + 1].to_broadcast([P, SEQ]), Z[:, j, ri, :],
                                                           0.0, ALU.mult, ALU.add)
                        (step if j % 2 and ri else mark)(ins)
                z = Z[:, 2 * q:2 * q + 2, :, :]
                mark(TT(T1, z, e_pair(q, 0), ALU.mult))
                step(TT(T2, z, e_pair(q, 1), ALU.mult))
                mark(TT(z[:, :, 0, :], T1[:, :, 0, :], T2[:, :, 1, :], ALU.subtract))
                step(TT(z[:, :, 1, :], T1[:, :, 1, :], T2[:, :, 0, :], ALU.add), states_ready)
            dve.wait_ge(y_ready, 1)
            for c in range(4):
                mark(STT(out=T1v(c), in0=uT[:, c, :], scalar=vec[:, V_D + c:V_D + c + 1],
                         in1=psum[:, 6 + c // 2, (c % 2) * 256:(c % 2) * 256 + 256], op0=ALU.mult, op1=ALU.add), yd_ready)
            for c in range(4):
                dve.wait_ge(sig_ready, c + 1)
                mark(TT(mixT[:, c, :], gy[:, c, :], sg[:, c, :], ALU.mult), glu_ready)
            dve.wait_ge(csum_ready, 1)
            step(TS(cv, psum[:, 2, :], 1.0 / 512, EPS, ALU.mult, ALU.add), var_ready)
            root(cv, cq, cy, ct)
            for c in range(KD):
                g = vec[:, V_GSSM + c:V_GSSM + c + 1]
                mark(STT(out=mixT[:, c, :], in0=mixT[:, c, :], scalar=g, in1=cy[:, (c // 4) * 256:(c // 4) * 256 + 256],
                         op0=ALU.mult, op1=ALU.mult), mix_ready)
            for b in range(2):
                dve.wait_ge(units_used, U_OUT + 2 * b + 2)
                for t in range(NT):
                    step(TT(xres[:, t, b * 512:(b + 1) * 512], xres[:, t, b * 512:(b + 1) * 512], psum[:, 2 * b + t, :], ALU.add), xadd)

            step(nc.vector.memset(ada_acc, 0.0), acc_zero)
            norm(junk_at=take(1024, zo + 5120))
            for t in range(NT):
                mark(TS(xn2[:, t, :], xres[:, t, :], rstd[:, t:t + 1], None, ALU.mult), xn_ready)
            hT_out(1, lambda k: vec[:, V_GFFN + k:V_GFFN + k + 1])
            dve.wait_ge(siluc_ready, 1)
            dve.wait_ge(bada_in, 16)
            ada_order = sem("ada_order")

            def window(w, i=None, last=False):
                at = w if i is None else i * 2 + w
                dve.wait_ge(ada_in, 16 * (w + 1) if i is None else i * 32 + 16 * (w + 1))
                dst = ada_acc[:, bass.ds(at * 512, 512)] if i is not None else ada_acc[:, w * 512:(w + 1) * 512]
                for k in range(KD):
                    ins = STT(out=dst, in0=ada_slot[:, k, :], scalar=siluc[:, k:k + 1], in1=dst, op0=ALU.mult, op1=ALU.add)
                    if k < KD - 1:
                        ins.then_inc(ada_order, 1)
                        n = w * (KD - 1) + k + 1
                        dve.wait_ge(ada_order, n if i is None else i * (2 * (KD - 1)) + n)
                    else:
                        ins.then_inc(ada_ready if last else ada_used, 1)

            def act_out(par, f, i=None):
                dve.wait_ge(silu_ready, f + 1 if i is None else i * 2 + f + 1)
                if f >= 2:
                    done = U_FF + 5 + 3 * (f - 2)
                    dve.wait_ge(units_used, done if i is None else i * 6 + done)
                TT(actT[:, par, :, :].rearrange("p f s -> p (f s)"), silu[:, par, :], psum[:, 5 + 2 * par, :],
                   ALU.mult).then_inc(act_ready, 1)

            for f in range(3):
                act_out(f % 2, f)
                window(f)
            with dve.Fori(0, 4) as i:
                act_out(1, 3, i)
                window(3, i)
                act_out(0, 4, i)
                window(4, i)
            window(11, last=True)
            dve.wait_ge(units_used, U_FF + 3 * NFF)
            for t in range(NT):
                for b in range(2):
                    step(TT(xres[:, t, b * 512:(b + 1) * 512], xres[:, t, b * 512:(b + 1) * 512], psum[:, 2 * t + b, :], ALU.add), xadd)
            norm(junk_at=take(1024, zo + 5120))
            dve.wait_ge(gf_in, 16)
            for t in range(NT):
                step(STT(out=xres[:, t, :], in0=xres[:, t, :], scalar=rstd[:, t:t + 1], in1=gfin1, op0=ALU.mult, op1=ALU.mult))
            norm(junk_at=take(1024, zo + 5120))
            for t in range(NT):
                mark(TS(xn3[:, t, :], xres[:, t, :], rstd[:, t:t + 1], None, ALU.mult), xn_ready)
            dve.wait_ge(mod_ready, 1)
            step(nc.vector.tensor_copy(modc, psum[:, 4, 0:16]), modc_out)
            step(STT(out=gm2, in0=modc[:, 8:16], scalar=1.0, in1=vec[:, V_GMIX2:V_GMIX2 + 8], op0=ALU.add, op1=ALU.mult), modc_out)
            hT_out(2, lambda k: gm2[:, k:k + 1], lambda k: modc[:, k:k + 1])

            dve.wait_ge(proj_out, 8 + 12)
            for t in range(NT):
                qk = qkd[:, t, :].rearrange("p (h r d) -> p h r d", h=24, r=2)
                A3 = ropeA.rearrange("p (h r d) -> p h r d", h=24, r=2)
                B3 = ropeB.rearrange("p (h r d) -> p h r d", h=24, r=2)
                cb = cos[:, t, :].unsqueeze(1).to_broadcast([P, 24, 64])
                mark(TT(ropeA.rearrange("p (h d) -> p h d", h=24), qkd[:, t, :].rearrange("p (h d) -> p h d", h=24), cb, ALU.mult))
                for r in range(2):
                    sb_ = sin[:, t, 32 * r:32 * r + 32].unsqueeze(1).to_broadcast([P, 24, 32])
                    (mark if r == 0 else step)(TT(B3[:, :, r, :], qk[:, :, 1 - r, :], sb_, ALU.mult))
                step(TT(qkd[:, t, :], ropeA, ropeB, ALU.add), roped)

            for h in range(HEADS + 1):
                if h < HEADS:
                    b = h % 2
                    dve.wait_ge(e_ready, h + 1)
                    if h >= 2:
                        dve.wait_ge(cum_ready, h - 1)
                    step(STT(out=sbl[:, b, :], in0=psum[:, b, 0:384], scalar=0.0, in1=sba[:, b, :], op0=ALU.max, op1=ALU.add))
                    step(TT(sbl[:, b, :], sbl[:, b, :], negm, ALU.mult), l_ready)
                    dve.wait_ge(cum_ready, h + 1)
                    step(STT(out=sba[:, b, :], in0=psum[:, 2 + b, 0:384], scalar=0.0, in1=sbias, op0=ALU.min, op1=ALU.add), ex_ready)

            for n in range(8 + 1):
                if n < 8:
                    t, b = n % 2, n % 2
                    w = P * (t + 1)
                    dve.wait_ge(dsc_ready, n + 1)
                    if n >= 2:
                        dve.wait_ge(dpT_ready, n - 1)
                    src = psum[:, 2 * b:2 * b + 2, :].rearrange("p b n -> p (b n)")[:, 0:DIL * w]
                    step(TT(S2[:, b, 0:DIL * w], src, dmask[t].rearrange("p g k -> p (g k)"), ALU.add))
                    step(nc.vector.reduce_max(mx1[:, b:b + 1], S2[:, b, 0:DIL * w], AX))
                    step(TS(nmx1[:, b:b + 1], mx1[:, b:b + 1], -1.0, None, ALU.mult), dmasked)
                if n >= 1:
                    b = (n - 1) % 2
                    w = DIL * P * (b + 1)
                    dve.wait_ge(dprobs, n)
                    step(nc.vector.reciprocal(rs1[:, b:b + 1], sum1[:, b:b + 1]))
                    step(TS(S2[:, b, 0:w], S2[:, b, 0:w], rs1[:, b:b + 1], None, ALU.mult), dprobs_n)

            dve.wait_ge(proj_out, 8 + 24)
            for c in range(KD):
                dve.wait_ge(br_ready, c + 1)
                both = tmp2.rearrange("p (r s) -> p r s", r=2)
                gates = gT.rearrange("p (r c) s -> p r c s", r=2)[:, :, c, :]
                step(TT(both, psum[:, c % 4, :].rearrange("p (r s) -> p r s", r=2), gates, ALU.mult))
                step(TT(merT[:, c, :], both[:, 0, :], both[:, 1, :], ALU.add), mer_ready)
            dve.wait_ge(rows_out, 8)
            for b in range(2):
                dve.wait_ge(units_used, U_OUT2 + 2 * b + 2)
                for t in range(NT):
                    cs_ = slice(b * 512, (b + 1) * 512)
                    step(TT(tmp2, psum[:, 2 * b + t, :], rows[:, 0, cs_], ALU.mult))
                    step(TT(xres[:, t, cs_], xres[:, t, cs_], tmp2, ALU.add), xadd)
            dve.wait_ge(rows_in, 32)
            step(STT(out=rows[:, 2, :], in0=rows[:, 2, :], scalar=1.0, in1=gffn2r, op0=ALU.add, op1=ALU.mult))
            norm(junk_at=h2[:, 0, :])
            for t in range(NT):
                step(STT(out=h2[:, t, :], in0=xres[:, t, :], scalar=rstd[:, t:t + 1], in1=rows[:, 2, :], op0=ALU.mult, op1=ALU.mult))
                step(TT(h2[:, t, :], h2[:, t, :], rows[:, 1, :], ALU.add), xn_ready)
            for k in (2, 3, 6, 7):
                dve.wait_ge(turned, 12 + k // 2 + 1)
                mark(nc.vector.tensor_copy(hT[:, k, :], psum[:, 4 + k // 2, (k % 2) * 256:(k % 2) * 256 + 256]), hT_dve)

            dve.wait_ge(sub_out, 8)
            step(nc.vector.memset(zeros, 0.0), zeros_ready)
            LOW = -3.4e38

            def route(b, m):
                def s(ins):
                    dve.drain()

                dve.wait_ge(staged, m + 1)
                nc.vector.memset(stat[:, 81:82], 0.0)
                dve.drain()
                for q in range(2):
                    row = stg[:, b, q * P:(q + 1) * P]
                    lo, hi = stop[:, b, q, 0:8], stop[:, b, q, 8:16]
                    s(nc.vector.max(lo, row))
                    s(nc.vector.max_index(itop[:, b, q, 0:8], lo, row))
                    s(nc.vector.match_replace(row, lo, row, LOW))
                    s(nc.vector.max(hi, row))
                    s(nc.vector.max_index(itop[:, b, q, 8:16], hi, row))
                c3 = cand.rearrange("p (i j) -> p i j", i=TOPK)
                sh = [P, TOPK, TOPK]
                s(TT(c3, stop[:, b, 0, :].unsqueeze(2).to_broadcast(sh), stop[:, b, 1, :].unsqueeze(1).to_broadcast(sh), ALU.add))
                s(nc.vector.max(best[:, 0:8], cand))
                s(nc.vector.max_index(pos[:, 0:8], best[:, 0:8], cand))
                s(nc.vector.match_replace(cand, best[:, 0:8], cand, LOW))
                s(nc.vector.max(best[:, 8:16], cand))
                s(TS(gnb, best[:, 0:1], -1.0, None, ALU.mult))
                nc.vector.max_index(pos[:, 8:16], best[:, 8:16], cand).then_inc(best_ready, 1)
                dve.wait_ge(best_ready, m + 1)
                s(nc.vector.tensor_copy(itopf, itop[:, b, :, :]))
                s(TS(ij[:, 0, :], pos, 4, None, ALU.logical_shift_right))
                s(TS(ij[:, 1, :], pos, 15, None, ALU.bitwise_and))
                s(nc.vector.tensor_copy(ijf, ij))
                sh4 = [P, 2, TOPK, TOPK]
                s(TT(oh, ijf.unsqueeze(3).to_broadcast(sh4), iota.unsqueeze(1).unsqueeze(1).to_broadcast(sh4), ALU.is_equal))
                s(TT(oh, oh, itopf.unsqueeze(2).to_broadcast(sh4), ALU.mult))
                s(nc.vector.tensor_reduce(e12, oh, AX, ALU.add))
                dve.wait_ge(gexp_ready, m + 1)
                s(nc.vector.reciprocal(grs, gsum))
                s(TS(gate[:, b, :], gexp, grs, None, ALU.mult))
                STT(out=expert[:, b, :], in0=e12[:, 0, :], scalar=128.0, in1=e12[:, 1, :], op0=ALU.mult,
                    op1=ALU.add).then_inc(routed, 1)
                dve.wait_ge(routed, m + 1)

            def dots_of(b, m, t, q):
                for k in range(4 * q, 4 * q + 4):
                    u = k % NU
                    dve.wait_ge(u_in[u], m * (TOPK // NU * 16) + 16 * (k // NU + 1))
                    nc.vector.tensor_tensor_reduce(out=U[:, u, :], in0=U[:, u, :], in1=h2[:, t, :], scale=1.0, scalar=0.0,
                                                   op0=ALU.mult, op1=ALU.add, accum_out=dots[:, b, k:k + 1]).then_inc(u_used, 1)

            def weigh(b, m, q):
                dve.wait_ge(gelued, m * 4 + q + 1)
                for k in range(4 * q, 4 * q + 4):
                    dve.wait_ge(v_used, m * TOPK + k + 1)
                    ins = TS(diag[:, k % ND, :], ident, gel[:, b, k:k + 1], gate[:, b, k:k + 1], ALU.mult, ALU.mult)
                ins.then_inc(diag_ready, 1)

            def head(b, m, t, more=True):
                dots_of(b, m, t, 0)
                dots_of(b, m, t, 1)
                weigh(b, m, 0)
                if more:
                    dve.wait_ge(idx_read, m + 1)
                    route(1 - b, m + 1)
                dots_of(b, m, t, 2)
                weigh(b, m, 1)
                dots_of(b, m, t, 3)
                weigh(b, m, 2)
                weigh(b, m, 3)

            for _ in range(NU):
                step(nc.vector.memset(junk, 0.0), u_used)
            for _ in range(ND):
                step(nc.vector.memset(junk, 0.0), v_used)
            step(nc.vector.memset(junk, 0.0), idx_read)
            step(nc.vector.memset(junk, 0.0), peer_go)

            def finish(t):
                dve.wait_ge(tile_done, t + 1)
                for c in range(2):
                    cs_ = slice(c * 512, (c + 1) * 512)
                    step(TT(fin[:, cs_], psum[:, 2 * t + c, :], rows[:, 3, cs_], ALU.mult))
                step(TT(xres[:, t, :], xres[:, t, :], fin, ALU.add))
                norm((t,), junk_at=fin)
                step(STT(out=xres[:, t, :], in0=xres[:, t, :], scalar=rstd[:, t:t + 1], in1=gfin2r, op0=ALU.mult, op1=ALU.mult), acc_out)

            route(0, 0)
            with dve.Fori(0, PEER_HEADS // 2) as i:
                head(0, i * 2, 0)
                head(1, i * 2 + 1, 0)
            with dve.Fori(0, PEER_HEADS // 2 - 1) as i:
                head(0, i * 2 + 8, 1)
                head(1, i * 2 + 9, 1)
            head(0, 14, 1)
            finish(0)
            head(1, 15, 1, more=False)
            finish(1)


def shape_constants(np):
    f = np.float32
    c = np.zeros((P, NCONST), f)
    i = np.arange(P)
    c[:, C_ID:C_ID + P] = np.eye(P)
    c[:, C_REV:C_REV + P] = np.eye(P)[::-1]
    c[:, C_TRI:C_TRI + P] = i[:, None] >= i[None, :]
    c[:, C_ONE:C_ONE + P] = 1.0
    q = np.arange(SEQ)
    seen = (q[None, :] // 64) <= (q[:, None] // 64)
    c[:, C_MASK1:C_MASK1 + 512] = np.where(seen, 0.0, NEG).reshape(NT, P, SEQ).transpose(1, 0, 2).reshape(P, 512)
    before = (i[:, None] < i[None, :])
    open_ = np.concatenate([before, np.ones((P, P), bool), before], axis=1)
    c[:, C_NEGM:C_NEGM + 384] = -open_.astype(f)
    c[:, C_BIAS:C_BIAS + 384] = np.where(open_, 0.0, NEG)
    back = q[:, None] - q[None, :]
    for t, at in ((0, C_DM0), (1, C_DM1)):
        w = P * (t + 1)
        for g, (win, r) in enumerate(((128, 1), (512, 4), (2048, 16))):
            ok = (back >= 0) & (back <= win) & (back % r == 0)
            c[:, at + g * w:at + (g + 1) * w] = np.where(ok, 0.0, NEG)[t * P:(t + 1) * P, :w]
    half = HD // 2
    inv = (f(10000.0) ** (-np.arange(half, dtype=f) / f(half))).astype(f)
    ang = q.astype(f)[:, None] * inv[None, :]
    cs, sn = np.cos(ang).astype(f), np.sin(ang).astype(f)
    c[:, C_COS:C_COS + 128] = np.concatenate([cs, cs], 1).reshape(NT, P, 64).transpose(1, 0, 2).reshape(P, 128)
    c[:, C_SIN:C_SIN + 128] = np.concatenate([-sn, sn], 1).reshape(NT, P, 64).transpose(1, 0, 2).reshape(P, 128)
    c[:, C_IOTA:C_IOTA + TOPK] = np.arange(TOPK)
    return c


def weight_stream(np, a):
    units = []

    def add(w):
        assert w.shape[0] == P and w[0].size == UNIT, w.shape
        units.append(w.reshape(P, UNIT))

    def chunked(w):
        return w.reshape(w.shape[0] // P, P, w.shape[1]).transpose(1, 0, 2)

    def columns(w, lo):
        w = chunked(w)
        for k in range(0, w.shape[1], 4):
            add(w[:, k:k + 4, lo:lo + 512])

    w_in = a["w_in"][0]
    for b in range(4):
        columns(w_in, b * 512)
    columns(a["ssm_w_glu"][0], 0)
    for b in range(2):
        columns(a["w_out"][0], b * 512)
    gate, up, down = (chunked(a[n][0]) for n in ("w_gate", "w_up", "w_down"))
    for f in range(NFF + 1):
        if f < NFF:
            add(gate[:, :, f * 256:(f + 1) * 256])
            add(up[:, :, f * 256:(f + 1) * 256])
        if f >= 1:
            add(down[:, 2 * (f - 1):2 * f, :])
    w_in2 = a["w_in_2"][0]
    for b in range(7):
        columns(w_in2, b * 512)
    add(chunked(w_in2)[:, :, 3584:3840])
    for b in range(4):
        columns(w_in2, 3840 + b * 512)
    for b in range(2):
        columns(a["w_sb_o_2"][0], b * 512)
    add(chunked(a["w_dil_o_2"][0]))
    for b in range(2):
        columns(a["w_out_2"][0], b * 512)
    for b in range(4):
        columns(a["w_pq_2"][0], b * 512)
    add(a["peer_keys_2"][0].reshape(16, P, P).transpose(2, 0, 1))
    assert len(units) == UNITS
    return np.stack(units)


def kernel(**inputs):
    import numpy as np
    import concourse.bacc as bacc
    from concourse.bass_utils import run_bass_kernel_spmd

    a = {k: np.asarray(v) for k, v in inputs.items()}

    def cols(v):
        return v.reshape(-1, P).T

    def states(v):
        return v.reshape(NST, P).T

    vecs = np.concatenate([
        cols(a["norm_mix_g"]), cols(a["norm_ffn_g"]), cols(a["norm_ssm_out_g"]), cols(a["norm_att_out_g"]),
        cols(a["ssm_d"]), cols(a["ssm_b_glu"]), cols(a["g_mix_2"]), cols(a["c_2"]),
        states(a["ssm_lam_re"]), states(a["ssm_lam_im"]), states(np.repeat(a["ssm_log_dt"][0], STATE))], axis=1)
    ssm_b = np.zeros((P, 4, 2, P), np.float32)
    ssm_c = np.zeros((P, NST, 2, 32), np.float32)
    for g in range(GROUPS):
        j, half = g // 2, g % 2
        r = 32 * (j % 4) + GCH * half
        for ri, (b, c) in enumerate((("ssm_b_re", "ssm_c_re"), ("ssm_b_im", "ssm_c_im"))):
            ssm_b[r:r + GCH, j // 4, ri, STATE * half:STATE * (half + 1)] = a[b][0, g].T
            ssm_c[STATE * half:STATE * (half + 1), j, ri, GCH * half:GCH * (half + 1)] = a[c][0, g].T
    rel = a["attn_rel_bias"][0]
    rel_ext = np.concatenate([np.repeat(rel[:, :1], 127, axis=1), rel], axis=1)
    w_ada = a["w_ada_2"][0].reshape(KD, P, 12, 512).transpose(2, 1, 0, 3).reshape(12, P, KD * 512)
    arrays = {
        "x": a["x"][0], "consts": shape_constants(np), "vecs": vecs, "weights": weight_stream(np, a),
        "ssm_b": ssm_b, "ssm_c": ssm_c, "rel_ext": rel_ext, "g_final1": a["norm_final_g"][None], "w_ada": w_ada,
        "b_ada": a["b_ada_2"], "g_ffn2": a["g_ffn_2"], "g_final2": a["g_final_2"][None],
        "peer_u": a["peer_u_2"][0], "peer_v": a["peer_v_2"][0],
    }
    arrays = {k: np.ascontiguousarray(v) for k, v in arrays.items()}
    nc = bacc.Bacc("TRN2", target_bir_lowering=False, num_devices=1)
    args = {k: nc.dram_tensor(f"in_{k}", v.shape, mybir.dt.from_np(v.dtype), kind="ExternalInput").ap()
            for k, v in arrays.items()}
    out = nc.dram_tensor("out_x", (SEQ, D), F32, kind="ExternalOutput").ap()
    build(nc, out=out, **args)
    r = run_bass_kernel_spmd(nc, [{f"in_{k}": v for k, v in arrays.items()}], core_ids=[0])
    return r.results[0]["out_x"].reshape(1, SEQ, D)
```

```python
from contextlib import ExitStack

import concourse.bass as bass
from concourse import mybir

F32 = mybir.dt.float32
U32 = mybir.dt.uint32
I32 = mybir.dt.int32
ALU = mybir.AluOpType
ACT = mybir.ActivationFunctionType
AX = mybir.AxisListType.X

P = 128
D = 1024
SEQ = 256
NT = SEQ // P
KD = D // P
DFF = 2816
NFF = DFF // 256
GROUPS, STATE, GCH = 32, 64, 16
NST = GROUPS * STATE // P
HD = 64
HEADS = 8
DIL = 3
DIL_HEADS = 4
PEER_HEADS = 8
TOPK = 16
EPS = 1e-6
NEG = -1e30
SCALE = HD ** -0.5
RING = 6
UNIT = 2048
NU, NV = 8, 8
LAG = 8
ND = 16

U_IN, U_GLU, U_OUT, U_FF = 0, 8, 9, 13
U_IN2 = U_FF + 3 * NFF
U_GATES, U_SBO, U_DILO, U_OUT2, U_PQ = U_IN2 + 15, U_IN2 + 23, U_IN2 + 25, U_IN2 + 26, U_IN2 + 30
UNITS = U_PQ + 8

V_GMIX, V_GFFN, V_GSSM, V_GATT, V_D, V_BGLU, V_GMIX2, V_C, V_LRE, V_LIM, V_LDT = 0, 8, 16, 20, 24, 28, 32, 40, 48, 64, 80
NVEC = 96

C_ID, C_REV, C_TRI, C_ONE, C_MASK1, C_NEGM, C_BIAS, C_DM0, C_DM1, C_COS, C_SIN, C_IOTA = (
    0, 128, 256, 384, 512, 1024, 1408, 1792, 2176, 2944, 3072, 3200)
NCONST = 3216


def build(nc, x, consts, vecs, weights, sub_keys, ssm_b, ssm_c, rel_ext, g_final1, w_ada, b_ada, g_ffn2, g_final2,
          peer_u, peer_v, out, dbg=None):
    with ExitStack() as ctx:
        def sem(name):
            return ctx.enter_context(nc.semaphore(name))

        arena = ctx.enter_context(nc.sbuf_tensor("arena", [P, 53100], F32))
        psum = ctx.enter_context(nc.psum_tensor("psum", [P, 8, 512], F32))

        top = [0]

        def take(words, at=None):
            a = top[0] if at is None else at
            if at is None:
                top[0] += words
            assert a + words <= 53100, (a, words)
            return arena[:, a:a + words]

        cst = take(NCONST)
        vec = take(NVEC)
        xres = take(NT * D).rearrange("p (t d) -> p t d", t=NT)
        hT = take(KD * SEQ).rearrange("p (k s) -> p k s", k=KD)
        ring = take(RING * UNIT).rearrange("p (r w) -> p r w", r=RING)
        stat = take(256)
        ada_at = top[0]
        ada_slot = take(4096).rearrange("p (k n) -> p k n", k=KD)
        ada_acc = take(6144)
        ph = top[0]

        ident = cst[:, C_ID:C_ID + P]
        rev = cst[:, C_REV:C_REV + P]
        tri = cst[:, C_TRI:C_TRI + P]
        ones = cst[:, C_ONE:C_ONE + P]
        mask1 = cst[:, C_MASK1:C_MASK1 + 512].rearrange("p (t k) -> p t k", t=2)
        negm = cst[:, C_NEGM:C_NEGM + 384]
        sbias = cst[:, C_BIAS:C_BIAS + 384]
        dmask = [cst[:, C_DM0:C_DM0 + 384].rearrange("p (g k) -> p g k", g=DIL),
                 cst[:, C_DM1:C_DM1 + 768].rearrange("p (g k) -> p g k", g=DIL)]
        cos = cst[:, C_COS:C_COS + 128].rearrange("p (t d) -> p t d", t=NT)
        sin = cst[:, C_SIN:C_SIN + 128].rearrange("p (t d) -> p t d", t=NT)
        iota = cst[:, C_IOTA:C_IOTA + TOPK]

        o = ph
        Z = take(8192, o).rearrange("p (j r t) -> p j r t", j=NST, r=2); zo = o; o += 8192
        pair_shape = lambda place: place.rearrange("p (j r t) -> p j r t", j=2, r=2)
        T1 = pair_shape(take(1024, o)); o += 1024
        T2 = pair_shape(take(1024, o)); o += 1024
        TB = hT.rearrange("p k s -> p (k s)")
        T1v = lambda c: arena[:, zo + 8192 + 256 * c:zo + 8192 + 256 * (c + 1)]
        BZ = take(1024, o).rearrange("p (c r m) -> p c r m", c=4, r=2); o += 1024
        CT = take(1024, o).rearrange("p (j r m) -> p j r m", j=NST, r=2); o += 1024
        CP = take(1024, o).rearrange("p (j r m) -> p j r m", j=NST, r=2); o += 1024
        uT = take(1024, o).rearrange("p (c s) -> p c s", c=4); o += 1024
        qT = take(1024, o).rearrange("p (c s) -> p c s", c=4); o += 1024
        kT = take(1024, o).rearrange("p (c s) -> p c s", c=4); o += 1024
        vN = take(1024, o).rearrange("p (t c) -> p t c", t=NT); o += 1024
        HB = take(2048, o).rearrange("p (h m) -> p h m", h=HEADS); o += 2048
        S1 = take(1024, o).rearrange("p (b t k) -> p b t k", b=2, t=2); o += 1024
        S1s = [S1[:, 0, :, :], S1[:, 1, :, :], BZ.rearrange("p c r m -> p (c r m)")[:, 0:512].rearrange("p (t k) -> p t k", t=2)]
        PT1 = take(768, o).rearrange("p (b k) -> p b k", b=2); o += 768
        sm1 = take(256, o); o += 256
        T1s = [T1, pair_shape(take(1024, o))]; o += 1024
        T2s = [[T2, pair_shape(S1.rearrange("p b t k -> p (b t k)"))], [T2, pair_shape(TB[:, 0:1024])]]
        E = take(8192, ada_at).rearrange("p (j r t) -> p j r t", j=NST, r=2)
        mixT = take(2048, ada_at + 8192).rearrange("p (k s) -> p k s", k=KD)
        xn1 = take(2048, zo).rearrange("p (t d) -> p t d", t=NT)
        etmp = take(4096, zo + 2048)
        gy = take(1024, zo).rearrange("p (c s) -> p c s", c=4)
        sg = take(1024, zo + 1024).rearrange("p (c s) -> p c s", c=4)
        sqr = take(2048, zo + 2048).rearrange("p (c s) -> p c s", c=KD)
        cv = take(512, zo + 4096)
        cq = take(512, zo + 4608)
        cy = take(512, zo + 5120)
        ct = take(512, zo + 5632)
        fo = zo + 8192
        silu = take(1024, fo).rearrange("p (b n) -> p b n", b=2)
        actT = take(1024, fo + 1024).rearrange("p (b f s) -> p b f s", b=2, f=2)
        gfin1 = take(1024, fo + 2048)
        xn2 = take(2048, zo + 6144).rearrange("p (t d) -> p t d", t=NT)
        coef = [sm1[:, 16 * i:16 * i + 16] for i in range(16)]
        ssq, var, sq, rstd, nt1 = (stat[:, 2 * i:2 * i + 2] for i in range(5))
        siluc = stat[:, 16:24]
        modc = stat[:, 32:48]
        gm2 = stat[:, 48:56]
        mx3, nmx3, sum3, rs3 = (stat[:, 96 + 6 * i:102 + 6 * i] for i in range(4))
        mx1, nmx1 = stat[:, 64:68], stat[:, 68:72]
        sum1, rs1 = stat[:, 72:76], stat[:, 76:80]
        junk = stat[:, 80:81]

        o = ph
        qkd = take(3072, o).rearrange("p (t n) -> p t n", t=NT); o += 3072
        vd = take(1536, o).rearrange("p (t n) -> p t n", t=NT); o += 1536
        vsb = take(1024, o).rearrange("p (t n) -> p t n", t=NT); o += 1024
        qTs = take(1024, o).rearrange("p (c s) -> p c s", c=4); o += 1024
        kTs = take(1024, o).rearrange("p (c s) -> p c s", c=4); o += 1024
        gT = take(4096, o).rearrange("p (c s) -> p c s", c=16); o += 4096
        ropeA = take(1536, o); o += 1536
        ropeB = take(1536, o); o += 1536
        qkdT = take(3072, o).rearrange("p (c s) -> p c s", c=12); o += 3072
        xn3 = take(2048, o - 3072).rearrange("p (t d) -> p t d", t=NT)
        sba = take(768, o).rearrange("p (b n) -> p b n", b=2); o += 768
        sbl = take(768, o).rearrange("p (b n) -> p b n", b=2); o += 768
        S2 = take(1536, o).rearrange("p (b n) -> p b n", b=2); o += 1536
        PT2 = take(1536, o).rearrange("p (b n) -> p b n", b=2); o += 1536
        tmp2 = S2[:, 0, 0:512]
        rows = take(4096, ada_at).rearrange("p (v d) -> p v d", v=4)
        aa = ada_at + 4096
        osbT = take(1024, aa).rearrange("p (c s) -> p c s", c=4)
        odT = take(512, aa + 1024).rearrange("p (c s) -> p c s", c=2)
        merT = take(2048, aa + 1536).rearrange("p (c s) -> p c s", c=KD)
        gffn2r = take(1024, aa + 3584)
        gfin2r = take(1024, aa + 4608)

        o = ph
        h2 = take(2048, o).rearrange("p (t d) -> p t d", t=NT); o += 2048
        sub = take(16 * 256, o); o += 16 * 256
        qpT = take(4096, o).rearrange("p (c s) -> p c s", c=16); o += 4096
        U = [take(D, aa + D * b) for b in range(4)] + [take(D, o + D * b) for b in range(4)]; o += 4 * D
        V = [take(D, o + D * b) for b in range(6)] + [cst[:, C_MASK1 + D * b:C_MASK1 + D * (b + 1)] for b in range(2)]; o += 6 * D
        keys = cst[:, C_MASK1:C_MASK1 + UNIT].rearrange("p (c n) -> p c n", c=16)
        norm_junk = take(D, o - D)
        zeros = take(512, o); o += 512
        stg = take(512, o).rearrange("p (b n) -> p b n", b=2); o += 512
        stop = take(64, o).rearrange("p (b q k) -> p b q k", b=2, q=2); o += 64
        itop = take(64, o).bitcast(U32).rearrange("p (b q k) -> p b q k", b=2, q=2); o += 64
        itopf = take(32, o).rearrange("p (q k) -> p q k", q=2); o += 32
        cand = take(256, o); o += 256
        best = take(16, o); o += 16
        pos = take(16, o).bitcast(U32); o += 16
        ij = take(32, o).bitcast(U32).rearrange("p (q k) -> p q k", q=2); o += 32
        ijf = take(32, o).rearrange("p (q k) -> p q k", q=2); o += 32
        oh = take(512, o).rearrange("p (q k i) -> p q k i", q=2, k=TOPK); o += 512
        e12 = take(32, o).rearrange("p (q k) -> p q k", q=2); o += 32
        expert = take(32, o).bitcast(U32).rearrange("p (b k) -> p b k", b=2); o += 32
        gate = take(32, o).rearrange("p (b k) -> p b k", b=2); o += 32
        gexp = take(16, o); o += 16
        gnb, gsum, grs = take(1, o), take(1, o + 1), take(1, o + 2); o += 4
        dots = take(32, o).rearrange("p (b k) -> p b k", b=2); o += 32
        gel = take(32, o).rearrange("p (b k) -> p b k", b=2); o += 32
        diag = rows[:, 0:2, :].rearrange("p v d -> p (v d)").rearrange("p (b m) -> p b m", b=ND)
        fin = qpT[:, 0:4, :].rearrange("p c s -> p (c s)")

        x_in, c_in, vec_in, b_in, cc_in, h_in = (sem(n) for n in ("x_in", "c_in", "vec_in", "b_in", "cc_in", "h_in"))
        gf_in, bada_in, ada_in, rows_in, out_done = (sem(n) for n in ("gf_in", "bada_in", "ada_in", "rows_in", "out_done"))
        unit_in = [sem(f"unit_in{s}") for s in range(RING)]
        units_used = sem("units_used")
        dve_step = sem("dve_step")
        act_step = sem("act_step")
        var_ready, sqrt_ready = sem("var_ready"), sem("sqrt_ready")
        xn_ready = sem("xn_ready")
        turned = sem("turned")
        hT_act, hT_dve = sem("hT_act"), sem("hT_dve")
        proj_out = sem("proj_out")
        trig_in, trig_out = sem("trig_in"), sem("trig_out")
        bu_ready, bu_used = sem("bu_ready"), sem("bu_used")
        cp_ready = sem("cp_ready")
        states_ready, y_ready = sem("states_ready"), sem("y_ready")
        turned_back, forward = sem("turned_back"), sem("forward")
        sc_ready, masked, probs, probs_n, pT_ready, pT_out, o_ready, o_out = (
            sem(n) for n in ("sc_ready", "masked", "probs", "probs_n", "pT_ready", "pT_out", "o_ready", "o_out"))
        yd_ready, gy_ready, sig_ready, glu_ready, sqr_ready, csum_ready, mix_ready = (
            sem(n) for n in ("yd_ready", "gy_ready", "sig_ready", "glu_ready", "sqr_ready", "csum_ready", "mix_ready"))
        xadd = sem("xadd")
        silu_ready, act_ready = sem("silu_ready"), sem("act_ready")
        ada_used, ada_ready, siluc_ready, acc_zero = (sem(n) for n in ("ada_used", "ada_ready", "siluc_ready", "acc_zero"))
        mod_ready, modc_out, rows_out = sem("mod_ready"), sem("modc_out"), sem("rows_out")
        x_final1 = sem("x_final1")
        z_ready, e_ready, l_ready, ex_ready, cum_ready, at_ready = (
            sem(n) for n in ("z_ready", "e_ready", "l_ready", "ex_ready", "cum_ready", "at_ready"))
        sbo_ready, sbo_out = sem("sbo_ready"), sem("sbo_out")
        roped, qkT_ready, qkT_out = sem("roped"), sem("qkT_ready"), sem("qkT_out")
        dsc_ready, dmasked, dprobs, dprobs_n, dpT_ready, dpT_out, do_ready, do_out = (
            sem(n) for n in ("dsc_ready", "dmasked", "dprobs", "dprobs_n", "dpT_ready", "dpT_out", "do_ready", "do_out"))
        gate_ready, gates_left, gate_on = (sem(n) for n in ("gate_ready", "gates_left", "gate_on"))
        br_ready, mer_ready = sem("br_ready"), sem("mer_ready")
        grow_ready, h2_ready = sem("grow_ready"), sem("h2_ready")
        sub_ready, sub_out, keys_in = sem("sub_ready"), sem("sub_out"), sem("keys_in")
        out2_ready, first_ready = sem("out2_ready"), sem("first_ready")
        staged, routing, best_ready, gexp_ready, routed = (
            sem(n) for n in ("staged", "routing", "best_ready", "gexp_ready", "routed"))
        u_in = [sem(f"u_in{b}") for b in range(NU)]
        v_in = [sem(f"v_in{b}") for b in range(NV)]
        u_used = sem("u_used")
        v_used = sem("v_used")
        gelued, diag_ready, tile_done, acc_out = (
            sem(n) for n in ("gelued", "diag_ready", "tile_done", "acc_out"))
        zeros_ready = sem("zeros_ready")
        idx_read = sem("idx_read")
        peer_go = sem("peer_go")

        block = ctx.enter_context(nc.Block())

        def stepper(eng, own):
            counts = {}

            def mark(ins, s=own, loop=None):
                ins.then_inc(s, 1)
                counts[s.name] = counts.get(s.name, 0) + 1
                return counts[s.name]

            def step(ins, s=own):
                eng.wait_ge(s, mark(ins, s))

            return mark, step

        @block.sync
        def _(sp):
            sp.dma_start(xres, x.rearrange("(t p) d -> p t d", p=P)).then_inc(x_in, 16)
            sp.dma_start(vec, vecs).then_inc(vec_in, 16)
            sp.dma_start(cst, consts).then_inc(c_in, 16)
            for s in range(RING):
                sp.dma_start(ring[:, s, :], weights[s]).then_inc(unit_in[s], 16)
            rounds = (UNITS - RING) // RING
            with sp.Fori(0, rounds) as i:
                for s in range(RING):
                    sp.wait_ge(units_used, i * RING + s + 1)
                    sp.dma_start(ring[:, s, :], weights[bass.ds((i + 1) * RING + s, 1)].rearrange("a p w -> (a p) w")
                                 ).then_inc(unit_in[s], 16)
            for n in range(RING * (rounds + 1), UNITS):
                sp.wait_ge(units_used, n - RING + 1)
                sp.dma_start(ring[:, n % RING, :], weights[n]).then_inc(unit_in[n % RING], 16)
            for t in range(NT):
                sp.wait_ge(acc_out, t + 1)
                sp.dma_start(out[t * P:(t + 1) * P, :], xres[:, t, :]).then_inc(out_done, 16)
            sp.wait_ge(out_done, 16 * NT)
            if dbg is not None:
                sp.dma_start(dbg, arena[:, :]).then_inc(out_done, 16)
                sp.wait_ge(out_done, 16 * (NT + 1))

        @block.gpsimd
        def _(pool):
            pool.dma_start(BZ, ssm_b).then_inc(b_in, 16)
            pool.dma_start(CT, ssm_c).then_inc(cc_in, 16)
            for h in range(HEADS):
                src = bass.AP(rel_ext.tensor, h * 384, [[1, P], [1, 256]])
                pool.dma_start(HB[:, h, :], src).then_inc(h_in, 16)
            for q in range(NST // 2):
                pool.wait_ge(bu_used, q + 1)
                z, t1, t2 = Z[:, 2 * q:2 * q + 2, :, :], T1s[q % 2], T2s[0][q % 2]
                nc.gpsimd.tensor_tensor(z[:, :, 0, :], t1[:, :, 0, :], t2[:, :, 1, :], ALU.add)
                nc.gpsimd.tensor_tensor(z[:, :, 1, :], t1[:, :, 1, :], t2[:, :, 0, :], ALU.subtract).then_inc(turned_back, 1)
            for q in range(NST // 2):
                pool.wait_ge(forward, q + 1)
                z, t1, t2 = Z[:, 2 * q:2 * q + 2, :, :], T1s[q % 2], T2s[1][q % 2]
                nc.gpsimd.tensor_tensor(z[:, :, 0, :], t1[:, :, 0, :], t2[:, :, 1, :], ALU.subtract)
                nc.gpsimd.tensor_tensor(z[:, :, 1, :], t1[:, :, 1, :], t2[:, :, 0, :], ALU.add).then_inc(states_ready, 1)
            pool.wait_ge(xadd, 4)
            nc.gpsimd.memset(ada_acc, 0.0).then_inc(acc_zero, 1)
            pool.wait_ge(acc_zero, 1)
            pool.dma_start(ada_acc[0:1, :], b_ada).then_inc(bada_in, 16)
            pool.dma_start(gfin1, g_final1.partition_broadcast(P)).then_inc(gf_in, 16)
            pool.dma_start(ada_slot, w_ada[0].rearrange("p (k n) -> p k n", k=KD)).then_inc(ada_in, 16)
            with pool.Fori(0, 11) as i:
                pool.wait_ge(ada_used, i + 1)
                pool.nop()
                pool.dma_start(ada_slot, w_ada[bass.ds(i + 1, 1)].rearrange("a p (k n) -> (a p) k n", k=KD)
                               ).then_inc(ada_in, 16)
            pool.wait_ge(mod_ready, 9)
            pool.wait_ge(rows_out, 8)
            pool.dma_start(gffn2r, g_ffn2.partition_broadcast(P)).then_inc(rows_in, 16)
            pool.dma_start(gfin2r, g_final2.partition_broadcast(P)).then_inc(rows_in, 16)
            pool.wait_ge(dmasked, 8)
            pool.dma_start(cst[:, C_MASK1:C_MASK1 + UNIT], sub_keys).then_inc(keys_in, 16)
            pool.wait_ge(peer_go, 1)

            def gather(table, buf, used, ahead, arrived, b, k, n, read=None):
                turn = pool.to_reg(n + ahead)
                pool.wait_ge(peer_go, 1)
                pool.wait_ge(used, turn)
                pool.indirect_dma_start(buf, None, table, bass.IndirectOffsetOnAxis(ap=expert[:, b, k:k + 1], axis=0),
                                        engine_sem=read).then_inc(arrived, 16)

            def row_u(b, k, n):
                gather(peer_u, U[k % NU], u_used, 1, u_in[k % NU], b, k, n)

            def row_v(b, k, n):
                if k == 6:
                    pool.wait_ge(sub_out, 8)
                gather(peer_v, V[k % NV], v_used, ND - NV + 1, v_in[k % NV], b, k, n, idx_read if k == TOPK - 1 else None)

            def head(b, m, last=False):
                for k in range(TOPK):
                    row_v(b, k, m * TOPK + k)
                    if k < TOPK - LAG:
                        row_u(b, k + LAG, m * TOPK + (k + LAG))
                    elif not last:
                        if k == TOPK - LAG:
                            following = pool.to_reg(m + 2)
                            pool.wait_ge(peer_go, 1)
                            pool.wait_ge(routed, following)
                        row_u(1 - b, k + LAG - TOPK, m * TOPK + (k + LAG))

            pool.wait_ge(routed, 1)
            for k in range(LAG):
                row_u(0, k, k)
            with pool.Fori(0, NT * PEER_HEADS // 2 - 1) as i:
                head(0, i * 2)
                head(1, i * 2 + 1)
            head(0, 14)
            head(1, 15, last=True)

        @block.tensor
        def _(pe):
            mm = nc.tensor.matmul

            def unit(n, i=None, per=1):
                value = 16 * (n // RING + 1)
                pe.wait_ge(unit_in[n % RING], value if i is None else i * (16 * per) + value)
                return ring[:, n % RING, :]

            def turn(src, want, tiles=range(NT)):
                for k in range(KD):
                    for t in tiles:
                        if k == 0:
                            pe.wait_ge(xn_ready, want + t + 1)
                        ins = nc.tensor.transpose(
                            psum[:, 4 + k // 2, (k % 2) * 256 + t * P:(k % 2) * 256 + (t + 1) * P],
                            src[:, t, k * P:(k + 1) * P], ident)
                    if k % 2 == 1:
                        ins.then_inc(turned, 1)

            def have_hT(n):
                pe.wait_ge(hT_act, 4 * n)
                pe.wait_ge(hT_dve, 4 * n)

            def block_T(banks, lo, hi, src, lo_t=0, hi_t=SEQ):
                for c in range(4):
                    for k in range(KD):
                        w = (lo if k < 4 else hi).rearrange("p (k n) -> p k n", k=4)
                        ins = mm(psum[:, banks + c // 2, (c % 2) * 256 + lo_t:(c % 2) * 256 + hi_t],
                                 w[:, k % 4, c * P:(c + 1) * P], src[:, k, lo_t:hi_t], start=k == 0, stop=k == KD - 1)
                return ins

            def block_N(banks, lo, hi, src, tiles=range(NT)):
                for t in tiles:
                    for k in range(KD):
                        w = (lo if k < 4 else hi).rearrange("p (k n) -> p k n", k=4)
                        ins = mm(psum[:, banks + t, :], src[:, k, t * P:(t + 1) * P], w[:, k % 4, :],
                                 start=k == 0, stop=k == KD - 1)
                return ins

            pe.wait_ge(c_in, 16)
            turn(xn1, 0)
            have_hT(1)
            pe.wait_ge(b_in, 16)

            def bu(q):
                if q < 2:
                    pe.wait_ge(hT_act, 4); pe.wait_ge(hT_dve, 4)
                else:
                    pe.wait_ge(bu_used, q - 1)
                for j in (2 * q, 2 * q + 1):
                    r = 32 * (j % 4)
                    for ri in range(2):
                        ins = mm(psum[:, 4 + j % 4, ri * 256:ri * 256 + 256], BZ[r:r + 32, j // 4, ri, :],
                                 uT[r:r + 32, j // 4, :], start=True, stop=True)
                ins.then_inc(bu_ready, 1)

            for b in range(4):
                lo, hi = unit(U_IN + 2 * b), unit(U_IN + 2 * b + 1)
                if b >= 2:
                    pe.wait_ge(proj_out, 2 * (b - 1))
                (block_T if b < 3 else block_N)(2 * (b % 2), lo, hi, hT).then_inc(units_used, 2)
                if b == 0:
                    pe.wait_ge(proj_out, 2)
                    bu(0)
                    bu(1)
            for q in range(2, NST // 2):
                bu(q)

            pe.wait_ge(proj_out, 8)
            pe.wait_ge(h_in, 16 * HEADS)
            pe.wait_ge(cp_ready, 1)

            def scores(h):
                r, c = 64 * (h % 2), h // 2
                if h >= 2:
                    pe.wait_ge(masked, h - 1)
                bank = psum[:, h % 2, :].rearrange("p (t k) -> p t k", t=2)
                for t in range(NT):
                    mm(bank[:, t, :], qT[r:r + 64, c, t * P:(t + 1) * P], kT[r:r + 64, c, :], start=True, stop=False)
                    if t == 0:
                        mm(bank[:, 0, 0:P], rev, HB[:, h, P:2 * P], start=False, stop=True)
                    else:
                        ins = mm(bank[:, 1, :], rev, HB[:, h, :], start=False, stop=True)
                ins.then_inc(sc_ready, 1)

            def turn_probs(h):
                pe.wait_ge(probs_n, h + 1)
                if h >= 2:
                    pe.wait_ge(pT_out, h - 1)
                for n, (t, k) in enumerate(((0, 0), (1, 0), (1, 1))):
                    ins = nc.tensor.transpose(psum[:, 2 + h % 2, n * P:(n + 1) * P], S1s[h % 3][:, t, k * P:(k + 1) * P], ident)
                ins.then_inc(pT_ready, 1)

            def values(h):
                pe.wait_ge(pT_out, h + 1)
                if h % 2 == 0 and h >= 4:
                    pe.wait_ge(o_out, h // 2 - 1)
                if h == 0:
                    pe.wait_ge(bu_used, 8)
                dst = psum[64 * (h % 2):64 * (h % 2) + 64, 4 + (h // 2) % 2, :]
                mm(dst[:, 0:256], vN[:, 0, h * HD:(h + 1) * HD], PT1[:, h % 2, 0:256], start=True, stop=False)
                mm(dst[:, P:256], vN[:, 1, h * HD:(h + 1) * HD], PT1[:, h % 2, 256:384],
                   start=False, stop=True).then_inc(o_ready, 1)

            def read_states(q):
                pe.wait_ge(states_ready, q + 1)
                for j in (2 * q, 2 * q + 1):
                    c, r = j // 4, 32 * (j % 4)
                    dst = psum[r:r + 32, 6 + c // 2, (c % 2) * 256:(c % 2) * 256 + 256]
                    for ri in range(2):
                        ins = mm(dst, CP[:, j, ri, :], Z[:, j, ri, :], start=ri == 0, stop=ri == 1)
                return ins

            scores(0)
            scores(1)
            for h in range(HEADS + 1):
                if h + 2 < HEADS:
                    scores(h + 2)
                if h < HEADS:
                    turn_probs(h)
                if h >= 1:
                    values(h - 1)
                    ins = read_states(h - 1)
            ins.then_inc(y_ready, 1)

            glu = unit(U_GLU).rearrange("p (k n) -> p k n", k=4)
            pe.wait_ge(gy_ready, 4)
            for c in range(4):
                for k in range(4):
                    ins = mm(psum[:, c // 2, (c % 2) * 256:(c % 2) * 256 + 256], glu[:, k, c * P:(c + 1) * P],
                             gy[:, k, :], start=k == 0, stop=k == 3)
            ins.then_inc(units_used, 1)

            pe.wait_ge(sqr_ready, 2)
            for br in range(2):
                for k in range(4):
                    ins = mm(psum[:, 2, br * 256:br * 256 + 256], ones, sqr[:, 4 * br + k, :], start=k == 0, stop=k == 3)
            ins.then_inc(csum_ready, 1)

            pe.wait_ge(mix_ready, 8)
            for b in range(2):
                lo, hi = unit(U_OUT + 2 * b), unit(U_OUT + 2 * b + 1)
                block_N(2 * b, lo, hi, mixT).then_inc(units_used, 2)

            pe.wait_ge(xadd, 4)
            turn(xn2, 2)
            have_hT(2)

            def gate_up(par, n, f, i=None):
                g, u = unit(n, i), unit(n + 1, i)
                if f >= 2:
                    pe.wait_ge(act_ready, f - 1 if i is None else i * 2 + (f - 1))
                for which, w in enumerate((g, u)):
                    w = w.rearrange("p (k n) -> p k n", k=KD)
                    for s in range(2):
                        for k in range(KD):
                            ins = mm(psum[:, 4 + 2 * par + which, s * 256:s * 256 + 256], w[:, k, s * P:(s + 1) * P],
                                     hT[:, k, :], start=k == 0, stop=k == KD - 1)
                ins.then_inc(units_used, 2)

            def down(par, n, f, i=None):
                w = unit(n, i).rearrange("p (s n) -> p s n", s=2)
                pe.wait_ge(act_ready, f + 1 if i is None else i * 2 + (f + 1))
                first, last = (f == 0), (i is None and f == NFF - 1)
                for s in range(2):
                    for t in range(NT):
                        for b in range(2):
                            ins = mm(psum[:, 2 * t + b, :], actT[:, par, s, t * P:(t + 1) * P], w[:, s, b * 512:(b + 1) * 512],
                                     start=first and s == 0, stop=last and s == 1, skip_group_check=True)
                ins.then_inc(units_used, 1)

            gate_up(0, U_FF, 0)
            gate_up(1, U_FF + 2, 1)
            down(0, U_FF + 4, 0)
            gate_up(0, U_FF + 5, 2)
            down(1, U_FF + 7, 1)
            with pe.Fori(0, 4) as i:
                gate_up(1, U_FF + 8, 3, i)
                down(0, U_FF + 10, 2, i)
                gate_up(0, U_FF + 11, 4, i)
                down(1, U_FF + 13, 3, i)
            down(0, U_FF + 32, 10)

            pe.wait_ge(ada_ready, 1)
            for n in range(16):
                ins = mm(psum[:, 4, n:n + 1], ada_acc[:, n * P:(n + 1) * P], ones[:, 0:1], start=True, stop=True)
            ins.then_inc(mod_ready, 1)
            for n in range(8):
                bank = 5 + n % 2
                if n >= 2:
                    pe.wait_ge(rows_out, n - 1)
                mm(psum[:, bank, :], ones, ada_acc[:, 2048 + n * 512:2048 + (n + 1) * 512],
                   start=True, stop=True).then_inc(mod_ready, 1)

            pe.wait_ge(modc_out, 1)
            pe.wait_ge(rows_out, 8)
            turn(xn3, 4)
            have_hT(3)
            n = U_IN2
            for b in range(8):
                if b >= 2:
                    pe.wait_ge(proj_out, 8 + 2 * (b - 1))
                if b == 7:
                    w = unit(n).rearrange("p (k n) -> p k n", k=KD)
                    for t in range(NT):
                        for k in range(KD):
                            ins = mm(psum[:, 2 * (b % 2) + t, 0:256], hT[:, k, t * P:(t + 1) * P], w[:, k, :],
                                     start=k == 0, stop=k == KD - 1)
                    ins.then_inc(units_used, 1)
                    n += 1
                    continue
                lo, hi = unit(n), unit(n + 1)
                (block_T if b < 2 else block_N)(2 * (b % 2), lo, hi, hT).then_inc(units_used, 2)
                n += 2

            for c in range(12):
                if c == 0:
                    pe.wait_ge(roped, 2)
                if c >= 8 and c % 2 == 0:
                    pe.wait_ge(qkT_out, c // 2 - 3)
                for t in range(NT):
                    ins = nc.tensor.transpose(
                        psum[:, 4 + (c // 2) % 4, (c % 2) * 256 + t * P:(c % 2) * 256 + (t + 1) * P],
                        qkd[:, t, c * P:(c + 1) * P], ident)
                if c % 2 == 1:
                    ins.then_inc(qkT_ready, 1)

            def gate_chunk(m):
                b, c, bank = m // 4, m % 4, 6 + (m // 2) % 2 if m < 8 else 1
                lo, hi = unit(U_GATES + 2 * b), unit(U_GATES + 2 * b + 1)
                if m == 0:
                    pe.wait_ge(qkT_out, 6)
                elif m == 8:
                    pe.wait_ge(l_ready, HEADS)
                elif m >= 4 and m % 2 == 0:
                    pe.wait_ge(gates_left, m // 2 - (1 if m < 8 else 0))
                for k in range(KD):
                    w = (lo if k < 4 else hi).rearrange("p (k n) -> p k n", k=4)
                    ins = mm(psum[:, bank, (m % 2) * 256:(m % 2) * 256 + 256], w[:, k % 4, c * P:(c + 1) * P],
                             hT[:, k, :], start=k == 0, stop=k == KD - 1)
                if c == 1:
                    ins.then_inc(gate_ready, 1)
                if c == 3:
                    ins.then_inc(units_used, 2)

            pe.wait_ge(proj_out, 8 + 16)

            def logits(h, bank, stop):
                r, c = 64 * (h % 2), h // 2
                mm(psum[:, bank, 0:256], kTs[r:r + 64, c, 0:P], qTs[r:r + 64, c, :], start=True, stop=stop)
                if not stop:
                    mm(psum[:, bank, 0:256], tri, sbl[:, h % 2, 0:256], start=False, stop=False)
                    mm(psum[:, bank, P:256], ones, sbl[:, h % 2, 256:384], start=False, stop=True)
                ins = mm(psum[:, bank, 256:384], kTs[r:r + 64, c, P:256], qTs[r:r + 64, c, P:256], start=True, stop=stop)
                if not stop:
                    ins = mm(psum[:, bank, 256:384], tri, sbl[:, h % 2, 256:384], start=False, stop=True)
                return ins

            for h in range(HEADS + 2):
                if h < HEADS:
                    if h >= 2:
                        pe.wait_ge(l_ready, h - 1)
                    logits(h, h % 2, True).then_inc(z_ready, 1)
                    gate_chunk(h)
                if 1 <= h <= HEADS:
                    g = h - 1
                    pe.wait_ge(l_ready, g + 1)
                    if g >= 2:
                        pe.wait_ge(ex_ready, g - 1)
                    logits(g, 2 + g % 2, False).then_inc(cum_ready, 1)
                if h >= 2:
                    g = h - 2
                    pe.wait_ge(at_ready, g + 1)
                    if g == 0:
                        pe.wait_ge(qkT_out, 6)
                    if g % 2 == 0 and g >= 4:
                        pe.wait_ge(sbo_out, g // 2 - 1)
                    dst = psum[64 * (g % 2):64 * (g % 2) + 64, 4 + (g // 2) % 2, :]
                    mm(dst[:, 0:256], vsb[:, 0, g * HD:(g + 1) * HD], sba[:, g % 2, 0:256], start=True, stop=False)
                    mm(dst[:, P:256], vsb[:, 1, g * HD:(g + 1) * HD], sba[:, g % 2, 256:384],
                       start=False, stop=True).then_inc(sbo_ready, 1)

            def dunit(n):
                return n % NT, n // NT

            def dscores(n):
                t, i = dunit(n)
                if n < 2:
                    pe.wait_ge(ex_ready, HEADS)
                if n >= 2:
                    pe.wait_ge(dmasked, n - 1)
                keys = P * (t + 1)
                for g in range(DIL):
                    hd = g * DIL_HEADS + i
                    r, c = 64 * (hd % 2), hd // 2
                    bank, off = 2 * (n % 2) + (g * keys) // 512, (g * keys) % 512
                    ins = mm(psum[:, bank, off:off + keys], qkdT[r:r + 64, c, t * P:(t + 1) * P],
                             qkdT[r:r + 64, 6 + c, 0:keys], start=True, stop=True)
                ins.then_inc(dsc_ready, 1)

            def dturn(n):
                t, i = dunit(n)
                pe.wait_ge(dprobs_n, n + 1)
                if n == 0:
                    pe.wait_ge(sbo_out, 4)
                if n >= 1:
                    pe.wait_ge(dpT_out, n)
                for m in range(DIL * (t + 1)):
                    ins = nc.tensor.transpose(psum[:, 4 + m // 4, (m % 4) * P:(m % 4 + 1) * P],
                                              S2[:, n % 2, m * P:(m + 1) * P], ident)
                ins.then_inc(dpT_ready, 1)

            def dvalues(n):
                t, i = dunit(n)
                pe.wait_ge(dpT_out, n + 1)
                if n == 0:
                    pe.wait_ge(gates_left, 4)
                dst = psum[64 * (i % 2):64 * (i % 2) + 64, 6 + (i // 2) % 2, t * P:(t + 1) * P]
                for m in range(DIL * (t + 1)):
                    g, st = m // (t + 1), m % (t + 1)
                    hd = g * DIL_HEADS + i
                    ins = mm(dst, vd[:, st, hd * HD:(hd + 1) * HD], PT2[:, n % 2, m * P:(m + 1) * P],
                             start=m == 0, stop=m == DIL * (t + 1) - 1)
                ins.then_inc(do_ready, 1)

            for n in range(8 + 2):
                if n < 8:
                    dscores(n)
                    gate_chunk(8 + n)
                if 1 <= n <= 8:
                    dturn(n - 1)
                if n >= 2:
                    dvalues(n - 2)

            pe.wait_ge(do_out, 2)
            wsb = [unit(U_SBO), unit(U_SBO + 1)]
            wdl = unit(U_DILO).rearrange("p (k n) -> p k n", k=2)
            for c in range(KD):
                if c >= 4:
                    pe.wait_ge(mer_ready, c - 3)
                ws = wsb[c // 4].rearrange("p (k n) -> p k n", k=4)
                for k in range(4):
                    ins = mm(psum[:, c % 4, 0:256], ws[:, k, (c % 4) * P:(c % 4 + 1) * P], osbT[:, k, :], start=k == 0, stop=k == 3)
                if c == 4 or c == KD - 1:
                    ins.then_inc(units_used, 1)
                for k in range(2):
                    ins = mm(psum[:, c % 4, 256:512], wdl[:, k, c * P:(c + 1) * P], odT[:, k, :], start=k == 0, stop=k == 1)
                ins.then_inc(br_ready, 1)

            pe.wait_ge(mer_ready, KD)
            for t in range(NT):
                for b in range(2):
                    ins = block_N(2 * t + b - t, unit(U_OUT2 + 2 * b), unit(U_OUT2 + 2 * b + 1), merT, tiles=(t,))
                    if t == 0:
                        ins.then_inc(*((units_used, 1) if b == 0 else (out2_ready, 1)))
                    else:
                        ins.then_inc(units_used, 2)

            def sub_scores(n, bank):
                t, g = n // 4, n % 4
                for c in range(4):
                    ins = mm(psum[:, bank, c * P:(c + 1) * P], qpT[:, 4 * g + c, t * P:(t + 1) * P],
                             keys[:, 4 * g + c, :], start=True, stop=True)
                ins.then_inc(sub_ready, 1)

            lo, hi = unit(U_PQ), unit(U_PQ + 1)
            turn(h2, 6, tiles=(0,))
            pe.wait_ge(hT_act, 12 + 4)
            block_T(0, lo, hi, hT, 0, P).then_inc(first_ready, 1)
            turn(h2, 6, tiles=(1,))
            pe.wait_ge(keys_in, 16)
            pe.wait_ge(proj_out, 24 + 2)
            sub_scores(0, 3)
            pe.wait_ge(hT_act, 12 + 8)
            block_T(0, lo, hi, hT, P, SEQ).then_inc(units_used, 2)
            for b in range(1, 4):
                if b == 1:
                    pe.wait_ge(sub_out, 1)
                else:
                    pe.wait_ge(proj_out, 24 + 2 * b)
                lo, hi = unit(U_PQ + 2 * b), unit(U_PQ + 2 * b + 1)
                block_T(2 * (b % 2), lo, hi, hT).then_inc(units_used, 2)
            pe.wait_ge(proj_out, 24 + 10)
            for n in range(1, 8):
                if n >= 5:
                    pe.wait_ge(sub_out, n - 3)
                sub_scores(n, 4 + n % 4)

            for t in range(NT):
                acc = 2 * t
                pe.wait_ge(zeros_ready, 1)
                for b in range(2):
                    mm(psum[:, acc + b, :], ident, zeros, start=True, stop=False, skip_group_check=True)
                with pe.Fori(0, PEER_HEADS // 2) as i:
                    for b in range(2):
                        for k in range(TOPK):
                            v = k % NV
                            uses = (t * PEER_HEADS + b) * (TOPK // NV) + k // NV + 1
                            pe.wait_ge(v_in[v], i * (2 * TOPK // NV * 16) + 16 * uses)
                            if k % 4 == 0:
                                pe.wait_ge(diag_ready, i * 8 + (t * PEER_HEADS + b) * 4 + k // 4 + 1)
                            for c in range(2):
                                ins = mm(psum[:, acc + c, :], diag[:, k % ND, :], V[v][:, c * 512:(c + 1) * 512],
                                         start=False, stop=False, skip_group_check=True)
                            ins.then_inc(v_used, 1)
                for c in range(2):
                    ins = mm(psum[:, acc + c, :], ident, zeros, start=False, stop=True, skip_group_check=True)
                ins.then_inc(tile_done, 1)

        @block.scalar
        def _(act):
            mark, step = stepper(act, act_step)
            A = nc.scalar.activation

            def root(n, src, dst):
                act.wait_ge(var_ready, n)
                mark(A(dst, src, ACT.Sqrt), sqrt_ready)

            def out_of_turn(n, scale, bias):
                for k in (0, 1, 4, 5):
                    act.wait_ge(turned, 4 * n + k // 2 + 1)
                    mark(A(hT[:, k, :], psum[:, 4 + k // 2, (k % 2) * 256:(k % 2) * 256 + 256], ACT.Identity, scale=scale(k), bias=bias(k)), hT_act)

            root(1, var, sq)
            act.wait_ge(vec_in, 16)
            out_of_turn(0, lambda k: vec[:, V_GMIX + k:V_GMIX + k + 1], lambda k: 0.0)
            act.wait_ge(trig_in, 1)
            mark(A(coef[3], coef[1], ACT.Sin), trig_out)
            mark(A(coef[2], coef[4], ACT.Sin), trig_out)

            def pair_out(done, banks, dst, scale=1.0, func=ACT.Copy, width=512):
                act.wait_ge(units_used, done)
                for t in range(2):
                    mark(A(dst(t), psum[:, banks + t, 0:width], func, scale=scale), proj_out)

            def cols(dst, at=0):
                return lambda t: dst[:, at + 2 * t:at + 2 * t + 2, :].rearrange("p c s -> p (c s)")

            pair_out(U_IN + 2, 0, cols(uT))
            pair_out(U_IN + 4, 2, cols(qT), SCALE)
            pair_out(U_IN + 6, 0, cols(kT))
            pair_out(U_IN + 8, 2, lambda t: vN[:, t, :])
            def exponentials(h):
                act.wait_ge(masked, h + 1)
                for t in range(NT):
                    n = 2 * (h % 3) + t
                    mark(A(S1s[h % 3][:, t, :], S1s[h % 3][:, t, :], ACT.Exp, bias=nmx3[:, n:n + 1],
                           accum_out=sum3[:, n:n + 1]), probs)

            exponentials(0)
            exponentials(1)
            for h in range(HEADS):
                if h + 2 < HEADS:
                    exponentials(h + 2)
                act.wait_ge(pT_ready, h + 1)
                if h >= 2:
                    act.wait_ge(o_ready, h - 1)
                mark(A(PT1[:, h % 2, :], psum[:, 2 + h % 2, 0:384], ACT.Copy), pT_out)
                if h >= 3 and h % 2 == 1:
                    c = (h - 3) // 2
                    act.wait_ge(o_ready, 2 * c + 2)
                    mark(A(mixT[:, 4 + c, :], psum[:, 4 + c % 2, 0:256], ACT.Copy), o_out)
            act.wait_ge(o_ready, HEADS)
            mark(A(mixT[:, 7, :], psum[:, 5, 0:256], ACT.Copy), o_out)
            for c in range(4):
                act.wait_ge(yd_ready, c + 1)
                mark(A(gy[:, c, :], T1v(c), ACT.Gelu_apprx_tanh), gy_ready)
            act.wait_ge(units_used, U_GLU + 1)
            for c in range(4):
                mark(A(sg[:, c, :], psum[:, c // 2, (c % 2) * 256:(c % 2) * 256 + 256], ACT.Sigmoid,
                       bias=vec[:, V_BGLU + c:V_BGLU + c + 1]), sig_ready)
            act.wait_ge(o_out, 4)
            mark(A(sqr[:, 4:8, :], mixT[:, 4:8, :], ACT.Square), sqr_ready)
            act.wait_ge(glu_ready, 4)
            mark(A(sqr[:, 0:4, :], mixT[:, 0:4, :], ACT.Square), sqr_ready)
            root(2, cv, cq)
            root(3, var, sq)
            out_of_turn(1, lambda k: vec[:, V_GFFN + k:V_GFFN + k + 1], lambda k: 0.0)
            mark(A(siluc, vec[:, V_C:V_C + 8], ACT.Silu), siluc_ready)

            def gate_out(par, done, f, i=None):
                act.wait_ge(units_used, done if i is None else i * 6 + done)
                if f >= 2:
                    act.wait_ge(act_ready, f - 1 if i is None else i * 2 + (f - 1))
                A(silu[:, par, :], psum[:, 4 + 2 * par, :], ACT.Silu).then_inc(silu_ready, 1)

            gate_out(0, U_FF + 2, 0)
            gate_out(1, U_FF + 4, 1)
            gate_out(0, U_FF + 7, 2)
            with act.Fori(0, 4) as i:
                gate_out(1, U_FF + 10, 3, i)
                gate_out(0, U_FF + 13, 4, i)
            root(4, var, sq)
            root(5, var, sq)
            for n in range(8):
                act.wait_ge(mod_ready, n + 2)
                if n == 0:
                    act.wait_ge(ada_ready, 1)
                mark(A(rows[:, n // 2, (n % 2) * 512:(n % 2 + 1) * 512], psum[:, 5 + n % 2, :], ACT.Copy), rows_out)
            act.wait_ge(modc_out, 2)
            out_of_turn(2, lambda k: gm2[:, k:k + 1], lambda k: modc[:, k:k + 1])
            d = U_IN2
            pair_out(d + 2, 0, cols(qTs), SCALE)
            pair_out(d + 4, 2, cols(kTs))
            pair_out(d + 6, 0, lambda t: vsb[:, t, :])
            for b in range(3):
                act.wait_ge(units_used, d + 8 + 2 * b)
                for t in range(NT):
                    src, dst = psum[:, 2 * ((3 + b) % 2) + t, :], qkd[:, t, b * 512:(b + 1) * 512]
                    if b == 1:
                        step(A(dst[:, 0:256], src[:, 0:256], ACT.Copy, scale=SCALE))
                        mark(A(dst[:, 256:512], src[:, 256:512], ACT.Copy), proj_out)
                    else:
                        mark(A(dst, src, ACT.Copy, scale=SCALE if b == 0 else 1.0), proj_out)
            pair_out(d + 14, 0, lambda t: vd[:, t, 0:512])
            pair_out(d + 15, 2, lambda t: vd[:, t, 512:768], width=256)

            def gates_out(p):
                if p % 2 == 0:
                    act.wait_ge(gate_ready, p // 2 + 1)
                else:
                    act.wait_ge(units_used, U_GATES + p + 1)
                mark(A(gT[:, 2 * p:2 * p + 2, :].rearrange("p c s -> p (c s)"), psum[:, 6 + p % 2 if p < 4 else 1, :], ACT.Copy), gates_left)

            for c in range(6):
                act.wait_ge(qkT_ready, c + 1)
                mark(A(qkdT[:, 2 * c:2 * c + 2, :].rearrange("p c s -> p (c s)"), psum[:, 4 + c % 4, :], ACT.Copy), qkT_out)
            for h in range(HEADS + 2):
                if h < HEADS:
                    act.wait_ge(z_ready, h + 1)
                    b = h % 2
                    if h >= 2:
                        act.wait_ge(sbo_ready, h - 1)
                    step(A(sba[:, b, :], psum[:, b, 0:384], ACT.Abs))
                    step(A(sba[:, b, :], sba[:, b, :], ACT.Exp, scale=-1.0))
                    mark(A(sba[:, b, :], sba[:, b, :], ACT.Ln, bias=ones[:, 0:1]), e_ready)
                if h >= 1 and h <= HEADS:
                    g = h - 1
                    act.wait_ge(ex_ready, g + 1)
                    mark(A(sba[:, g % 2, :], sba[:, g % 2, :], ACT.Exp), at_ready)
                if h < HEADS and h % 2 == 1:
                    gates_out(h // 2)
                if h in (4, 6, 8):
                    c = h // 2 - 2
                    act.wait_ge(sbo_ready, 2 * c + 2)
                    mark(A(osbT[:, c, :], psum[:, 4 + c % 2, 0:256], ACT.Copy), sbo_out)
            act.wait_ge(sbo_ready, HEADS)
            mark(A(osbT[:, 3, :], psum[:, 5, 0:256], ACT.Copy), sbo_out)
            for n in range(8 + 2):
                if n < 8:
                    act.wait_ge(dmasked, n + 1)
                    w = DIL * P * (n % 2 + 1)
                    mark(A(S2[:, n % 2, 0:w], S2[:, n % 2, 0:w], ACT.Exp, bias=nmx1[:, n % 2:n % 2 + 1],
                           accum_out=sum1[:, n % 2:n % 2 + 1]), dprobs)
                    if n % 2 == 1:
                        gates_out(4 + n // 2)
                if 1 <= n <= 8:
                    g = n - 1
                    act.wait_ge(dpT_ready, g + 1)
                    if g >= 2:
                        act.wait_ge(do_ready, g - 1)
                    w = DIL * P * (g % 2 + 1)
                    src = psum[:, 4:6, :].rearrange("p b n -> p (b n)")[:, 0:w]
                    mark(A(PT2[:, g % 2, 0:w], src, ACT.Copy), dpT_out)
                if n >= 5 and n % 4 == 1:
                    c = (n - 5) // 4
                    act.wait_ge(do_ready, 4 * c + 4)
                    mark(A(odT[:, c, :], psum[:, 6 + c, 0:256], ACT.Copy), do_out)
            act.wait_ge(gates_left, 8)
            for c in range(KD):
                both = gT.rearrange("p (r c) s -> p r c s", r=2)[:, :, c, :]
                mark(A(both, both, ACT.Sigmoid), gate_on)
            def turned_tile(t):
                for b in range(4):
                    act.wait_ge(turned, 12 + 4 * t + b + 1)
                    src = psum[:, 4 + b, :].rearrange("p (c s) -> p c s", c=2)[:, :, t * P:(t + 1) * P]
                    mark(A(hT[:, 2 * b:2 * b + 2, t * P:(t + 1) * P], src, ACT.Copy), hT_act)

            def queries_out(b):
                pair_out(U_PQ + 2 * b + 2, 2 * (b % 2), cols(qpT, 4 * b))

            def scores_out(n, bank):
                act.wait_ge(sub_ready, n + 1)
                mark(A(sub[:, n * 512:(n + 1) * 512], psum[:, bank, :], ACT.Copy), sub_out)

            def stage(b, m):
                A(stg[:, b, :], sub[:, bass.ds(m * 256, 256)], ACT.Copy).then_inc(staged, 1)

            def gates(m):
                act.wait_ge(best_ready, m + 1)
                A(gexp[:, :], best[:, :], ACT.Exp, bias=gnb[:, :], accum_out=gsum[:, :]).then_inc(gexp_ready, 1)

            def gelus(b, m, quarters):
                for q in quarters:
                    act.wait_ge(u_used, m * TOPK + (4 * q + 4 + NU))
                    A(gel[:, b, 4 * q:4 * q + 4], dots[:, b, 4 * q:4 * q + 4], ACT.Gelu_apprx_tanh).then_inc(gelued, 1)

            def head(b, m, gate=True, more=True):
                gelus(b, m, (0, 1))
                if gate:
                    gates(m + 1)
                if more:
                    stage(1 - b, m + 3)
                gelus(b, m, (2, 3))

            root(6, var, sq)
            turned_tile(0)
            root(7, var, sq)
            act.wait_ge(first_ready, 1)
            for b in range(2):
                src = psum[:, b, :].rearrange("p (c s) -> p c s", c=2)[:, :, 0:P]
                mark(A(qpT[:, 2 * b:2 * b + 2, 0:P], src, ACT.Copy), proj_out)
            scores_out(0, 3)
            act.wait_ge(sub_out, 1)
            stage(0, 0)
            turned_tile(1)
            stage(1, 1)
            act.wait_ge(units_used, U_PQ + 2)
            for b in range(2):
                src = psum[:, b, :].rearrange("p (c s) -> p c s", c=2)[:, :, P:SEQ]
                mark(A(qpT[:, 2 * b:2 * b + 2, P:SEQ], src, ACT.Copy), proj_out)
            gates(0)
            queries_out(1)
            gelus(0, 0, (0,))
            gelus(0, 0, (1,))
            queries_out(2)
            gates(1)
            queries_out(3)
            for n in range(1, 8):
                scores_out(n, 4 + n % 4)
            act.wait_ge(sub_out, 8)
            stage(0, 2)
            stage(1, 3)
            gelus(0, 0, (2, 3))
            head(1, 1)
            with act.Fori(0, 5) as i:
                head(0, i * 2 + 2)
                head(1, i * 2 + 3)
            head(0, 12)
            head(1, 13, more=False)
            head(0, 14, more=False)
            root(8, var, sq)
            head(1, 15, gate=False, more=False)
            root(9, var, sq)

        @block.vector
        def _(dve):
            mark, step = stepper(dve, dve_step)
            TT, TS = nc.vector.tensor_tensor, nc.vector.tensor_scalar
            STT = nc.vector.scalar_tensor_tensor
            roots = [0]

            def root(v, s, y, t):
                roots[0] += 1
                dve.wait_ge(sqrt_ready, roots[0])
                step(nc.vector.reciprocal(y, s))
                step(TT(t, y, y, ALU.mult))
                step(TT(t, t, v, ALU.mult))
                step(TS(t, t, -0.5, 1.5, ALU.mult, ALU.add))
                step(TT(y, y, t, ALU.mult))

            def norm(tiles=(0, 1), junk_at=None):
                lo, hi = tiles[0], tiles[-1] + 1
                for t in tiles:
                    step(nc.vector.tensor_tensor_reduce(out=junk_at, in0=xres[:, t, :], in1=xres[:, t, :], scale=1.0,
                                                        scalar=0.0, op0=ALU.mult, op1=ALU.add, accum_out=ssq[:, t:t + 1]))
                step(TS(var, ssq, 1.0 / D, EPS, ALU.mult, ALU.add), var_ready)
                root(var, sq, rstd, nt1)

            def hT_out(n, scale, bias=None):
                for k in (2, 3, 6, 7):
                    dve.wait_ge(turned, 4 * n + k // 2 + 1)
                    src = psum[:, 4 + k // 2, (k % 2) * 256:(k % 2) * 256 + 256]
                    if bias is None:
                        ins = TS(hT[:, k, :], src, scale(k), None, ALU.mult)
                    else:
                        ins = TS(hT[:, k, :], src, scale(k), bias(k), ALU.mult, ALU.add)
                    mark(ins, hT_dve)

            dve.wait_ge(x_in, 16)
            norm(junk_at=take(1024, zo + 2048))
            for t in range(NT):
                mark(TS(xn1[:, t, :], xres[:, t, :], rstd[:, t:t + 1], None, ALU.mult), xn_ready)

            dve.wait_ge(vec_in, 16)
            lre, lim, ldt = (vec[:, v:v + 16] for v in (V_LRE, V_LIM, V_LDT))
            r_, th, cs, sn, cth, dt, t_, n_, p_, den, kr, ki, lbr, lbi = coef[0:14]
            hT_out(0, lambda k: vec[:, V_GMIX + k:V_GMIX + k + 1])
            MAGIC = 1.5 * 2.0 ** 23

            def exp_exact(dst, src):
                step(TS(n_, src, 1.4426950408889634, MAGIC, ALU.mult, ALU.add))
                step(TS(n_, n_, MAGIC, None, ALU.subtract))
                step(TS(n_, n_, -126.0, 127.0, ALU.max, ALU.min))
                step(STT(out=t_, in0=n_, scalar=-0.693359375, in1=src, op0=ALU.mult, op1=ALU.add))
                step(STT(out=t_, in0=n_, scalar=2.12194440e-4, in1=t_, op0=ALU.mult, op1=ALU.add))
                step(TS(p_, t_, 1.0 / 5040, None, ALU.mult))
                for c in (720.0, 120.0, 24.0, 6.0, 2.0, 1.0):
                    step(STT(out=p_, in0=p_, scalar=1.0 / c, in1=t_, op0=ALU.add, op1=ALU.mult))
                step(TS(t_.bitcast(I32), n_, 127.0, 2.0 ** 23, ALU.add, ALU.mult))
                step(STT(out=dst, in0=p_, scalar=1.0, in1=t_, op0=ALU.add, op1=ALU.mult))

            exp_exact(dt, ldt)
            step(TT(th, lim, dt, ALU.mult))
            step(TT(den, lre, dt, ALU.mult))
            exp_exact(r_, den)
            step(TS(n_, th, 0.15915494309189535, MAGIC, ALU.mult, ALU.add))
            step(TS(n_, n_, MAGIC, None, ALU.subtract))
            for c in (6.28125, 1.9350051879882812e-3, 3.0199159819567e-7):
                step(STT(out=th, in0=n_, scalar=-c, in1=th, op0=ALU.mult, op1=ALU.add))
            step(TS(th, th, 3.1415925, -3.1415925, ALU.min, ALU.max))
            step(STT(out=cth, in0=th, scalar=-1.0, in1=th, op0=ALU.mult, op1=ALU.max))
            step(TS(cth, cth, -1.0, 1.5707963267948966, ALU.mult, ALU.add), trig_in)
            dve.wait_ge(trig_out, 2)
            step(TT(lbr, r_, cs, ALU.mult))
            step(TS(lbr, lbr, -1.0, None, ALU.add))
            step(TT(lbi, r_, sn, ALU.mult))
            step(TT(den, lre, lre, ALU.mult))
            step(TT(t_, lim, lim, ALU.mult))
            step(TT(den, den, t_, ALU.add))
            step(nc.vector.reciprocal(den, den))
            step(TT(kr, lbr, lre, ALU.mult))
            step(TT(t_, lbi, lim, ALU.mult))
            step(TT(kr, kr, t_, ALU.add))
            step(TT(kr, kr, den, ALU.mult))
            step(TT(ki, lbi, lre, ALU.mult))
            step(TT(t_, lbr, lim, ALU.mult))
            step(TT(ki, ki, t_, ALU.subtract))
            step(TT(ki, ki, den, ALU.mult))
            dve.wait_ge(cc_in, 16)
            wide = [P, NST, 32]
            tc1 = T1.rearrange("p j r t -> p (j r t)")[:, 0:512].rearrange("p (j m) -> p j m", j=NST)
            krb, kib = kr.unsqueeze(2).to_broadcast(wide), ki.unsqueeze(2).to_broadcast(wide)
            step(TT(CP[:, :, 0, :], CT[:, :, 0, :], krb, ALU.mult))
            step(TT(tc1, CT[:, :, 1, :], kib, ALU.mult))
            step(TT(CP[:, :, 0, :], CP[:, :, 0, :], tc1, ALU.subtract))
            step(TT(CP[:, :, 1, :], CT[:, :, 0, :], kib, ALU.mult))
            step(TT(tc1, CT[:, :, 1, :], krb, ALU.mult))
            step(STT(out=CP[:, :, 1, :], in0=CP[:, :, 1, :], scalar=-1.0, in1=tc1, op0=ALU.mult, op1=ALU.subtract), cp_ready)
            pr, pi = coef[14], coef[15]
            step(nc.vector.memset(E[:, :, 0, 0:1], 1.0))
            step(nc.vector.memset(E[:, :, 1, 0:1], 0.0))
            step(nc.vector.tensor_copy(pr, cs))
            step(nc.vector.tensor_copy(pi, sn))
            n = 1
            while n < SEQ:
                new, old = E[:, :, :, n:2 * n], E[:, :, :, 0:n]
                shape = [P, NST, 2, n]
                tmp = etmp[:, 0:NST * 2 * n].rearrange("p (j r t) -> p j r t", j=NST, r=2)
                mark(TT(new, old, pr.unsqueeze(2).unsqueeze(3).to_broadcast(shape), ALU.mult))
                step(TT(tmp, old, pi.unsqueeze(2).unsqueeze(3).to_broadcast(shape), ALU.mult))
                mark(TT(new[:, :, 0, :], new[:, :, 0, :], tmp[:, :, 1, :], ALU.subtract))
                step(TT(new[:, :, 1, :], new[:, :, 1, :], tmp[:, :, 0, :], ALU.add))
                if 2 * n < SEQ:
                    step(TT(t_, pr, pr, ALU.mult))
                    step(TT(p_, pi, pi, ALU.mult))
                    step(STT(out=pi, in0=pi, scalar=2.0, in1=pr, op0=ALU.mult, op1=ALU.mult))
                    step(TT(pr, t_, p_, ALU.subtract))
                n *= 2

            def e_pair(q, ri):
                return E[:, 2 * q:2 * q + 2, ri, :].unsqueeze(2).to_broadcast([P, 2, 2, SEQ])

            for q in range(NST // 2):
                dve.wait_ge(bu_ready, q + 1)
                b = 4 + 2 * (q % 2)
                src = psum[:, b:b + 2, :].rearrange("p j (r t) -> p j r t", r=2)
                if q >= 2:
                    dve.wait_ge(turned_back, q - 1)
                mark(TT(T1s[q % 2], src, e_pair(q, 0), ALU.mult))
                mark(TT(T2s[0][q % 2], src, e_pair(q, 1), ALU.mult), bu_used)

            def states(q):
                dve.wait_ge(turned_back, q + 1)
                for j in (2 * q, 2 * q + 1):
                    for ri in range(2):
                        ins = nc.vector.tensor_tensor_scan(Z[:, j, ri, :], r_[:, j:j + 1].to_broadcast([P, SEQ]), Z[:, j, ri, :],
                                                           0.0, ALU.mult, ALU.add)
                        (step if j % 2 and ri else mark)(ins)
                if q >= 2:
                    dve.wait_ge(states_ready, q - 1)
                z = Z[:, 2 * q:2 * q + 2, :, :]
                mark(TT(T1s[q % 2], z, e_pair(q, 0), ALU.mult))
                mark(TT(T2s[1][q % 2], z, e_pair(q, 1), ALU.mult), forward)

            dve.wait_ge(turned_back, 8)

            def mask(h):
                b = h % 3
                dve.wait_ge(sc_ready, h + 1)
                if h >= 3:
                    dve.wait_ge(pT_ready, h - 2)
                step(TT(S1s[b], psum[:, h % 2, :].rearrange("p (t k) -> p t k", t=2), mask1, ALU.add))
                step(nc.vector.reduce_max(mx3[:, 2 * b:2 * b + 2], S1s[b], AX))
                step(TS(nmx3[:, 2 * b:2 * b + 2], mx3[:, 2 * b:2 * b + 2], -1.0, None, ALU.mult), masked)

            def normalise(h):
                b = h % 3
                dve.wait_ge(probs, 2 * h + 2)
                step(nc.vector.reciprocal(rs3[:, 2 * b:2 * b + 2], sum3[:, 2 * b:2 * b + 2]))
                mark(TS(S1s[b][:, 0, :], S1s[b][:, 0, :], rs3[:, 2 * b:2 * b + 1], None, ALU.mult))
                step(TS(S1s[b][:, 1, :], S1s[b][:, 1, :], rs3[:, 2 * b + 1:2 * b + 2], None, ALU.mult), probs_n)

            mask(0)
            mask(1)
            for h in range(HEADS):
                if h + 2 < HEADS:
                    mask(h + 2)
                normalise(h)
                states(h)
            dve.wait_ge(y_ready, 1)
            for c in range(4):
                mark(STT(out=T1v(c), in0=uT[:, c, :], scalar=vec[:, V_D + c:V_D + c + 1],
                         in1=psum[:, 6 + c // 2, (c % 2) * 256:(c % 2) * 256 + 256], op0=ALU.mult, op1=ALU.add), yd_ready)
            for c in range(4):
                dve.wait_ge(sig_ready, c + 1)
                mark(TT(mixT[:, c, :], gy[:, c, :], sg[:, c, :], ALU.mult), glu_ready)
            dve.wait_ge(csum_ready, 1)
            step(TS(cv, psum[:, 2, :], 1.0 / 512, EPS, ALU.mult, ALU.add), var_ready)
            root(cv, cq, cy, ct)
            for c in range(KD):
                g = vec[:, V_GSSM + c:V_GSSM + c + 1]
                mark(STT(out=mixT[:, c, :], in0=mixT[:, c, :], scalar=g, in1=cy[:, (c // 4) * 256:(c // 4) * 256 + 256],
                         op0=ALU.mult, op1=ALU.mult), mix_ready)
            for b in range(2):
                dve.wait_ge(units_used, U_OUT + 2 * b + 2)
                for t in range(NT):
                    step(TT(xres[:, t, b * 512:(b + 1) * 512], xres[:, t, b * 512:(b + 1) * 512], psum[:, 2 * b + t, :], ALU.add), xadd)

            norm(junk_at=take(1024, zo + 5120))
            for t in range(NT):
                mark(TS(xn2[:, t, :], xres[:, t, :], rstd[:, t:t + 1], None, ALU.mult), xn_ready)
            hT_out(1, lambda k: vec[:, V_GFFN + k:V_GFFN + k + 1])
            dve.wait_ge(siluc_ready, 1)
            dve.wait_ge(bada_in, 16)
            ada_order = sem("ada_order")

            def window(w, i=None, last=False):
                at = w if i is None else i * 2 + w
                dve.wait_ge(ada_in, 16 * (w + 1) if i is None else i * 32 + 16 * (w + 1))
                dst = ada_acc[:, bass.ds(at * 512, 512)] if i is not None else ada_acc[:, w * 512:(w + 1) * 512]
                for k in range(KD):
                    ins = STT(out=dst, in0=ada_slot[:, k, :], scalar=siluc[:, k:k + 1], in1=dst, op0=ALU.mult, op1=ALU.add)
                    if k < KD - 1:
                        ins.then_inc(ada_order, 1)
                        n = w * (KD - 1) + k + 1
                        dve.wait_ge(ada_order, n if i is None else i * (2 * (KD - 1)) + n)
                    else:
                        ins.then_inc(ada_ready if last else ada_used, 1)

            def act_out(par, f, i=None):
                dve.wait_ge(silu_ready, f + 1 if i is None else i * 2 + f + 1)
                if f >= 2:
                    done = U_FF + 5 + 3 * (f - 2)
                    dve.wait_ge(units_used, done if i is None else i * 6 + done)
                TT(actT[:, par, :, :].rearrange("p f s -> p (f s)"), silu[:, par, :], psum[:, 5 + 2 * par, :],
                   ALU.mult).then_inc(act_ready, 1)

            for f in range(3):
                act_out(f % 2, f)
                window(f)
            with dve.Fori(0, 4) as i:
                act_out(1, 3, i)
                window(3, i)
                act_out(0, 4, i)
                window(4, i)
            window(11, last=True)
            dve.wait_ge(units_used, U_FF + 3 * NFF)
            for t in range(NT):
                for b in range(2):
                    step(TT(xres[:, t, b * 512:(b + 1) * 512], xres[:, t, b * 512:(b + 1) * 512], psum[:, 2 * t + b, :], ALU.add), xadd)
            norm(junk_at=take(1024, zo + 5120))
            dve.wait_ge(gf_in, 16)
            for t in range(NT):
                step(STT(out=xres[:, t, :], in0=xres[:, t, :], scalar=rstd[:, t:t + 1], in1=gfin1, op0=ALU.mult, op1=ALU.mult))
            norm(junk_at=take(1024, zo + 5120))
            for t in range(NT):
                mark(TS(xn3[:, t, :], xres[:, t, :], rstd[:, t:t + 1], None, ALU.mult), xn_ready)
            dve.wait_ge(mod_ready, 1)
            step(nc.vector.tensor_copy(modc, psum[:, 4, 0:16]), modc_out)
            step(STT(out=gm2, in0=modc[:, 8:16], scalar=1.0, in1=vec[:, V_GMIX2:V_GMIX2 + 8], op0=ALU.add, op1=ALU.mult), modc_out)
            hT_out(2, lambda k: gm2[:, k:k + 1], lambda k: modc[:, k:k + 1])

            dve.wait_ge(proj_out, 8 + 12)
            for t in range(NT):
                qk = qkd[:, t, :].rearrange("p (h r d) -> p h r d", h=24, r=2)
                A3 = ropeA.rearrange("p (h r d) -> p h r d", h=24, r=2)
                B3 = ropeB.rearrange("p (h r d) -> p h r d", h=24, r=2)
                cb = cos[:, t, :].unsqueeze(1).to_broadcast([P, 24, 64])
                mark(TT(ropeA.rearrange("p (h d) -> p h d", h=24), qkd[:, t, :].rearrange("p (h d) -> p h d", h=24), cb, ALU.mult))
                for r in range(2):
                    sb_ = sin[:, t, 32 * r:32 * r + 32].unsqueeze(1).to_broadcast([P, 24, 32])
                    (mark if r == 0 else step)(TT(B3[:, :, r, :], qk[:, :, 1 - r, :], sb_, ALU.mult))
                step(TT(qkd[:, t, :], ropeA, ropeB, ALU.add), roped)

            for h in range(HEADS + 1):
                if h < HEADS:
                    b = h % 2
                    dve.wait_ge(e_ready, h + 1)
                    if h >= 2:
                        dve.wait_ge(cum_ready, h - 1)
                    step(STT(out=sbl[:, b, :], in0=psum[:, b, 0:384], scalar=0.0, in1=sba[:, b, :], op0=ALU.max, op1=ALU.add))
                    step(TT(sbl[:, b, :], sbl[:, b, :], negm, ALU.mult), l_ready)
                    dve.wait_ge(cum_ready, h + 1)
                    step(STT(out=sba[:, b, :], in0=psum[:, 2 + b, 0:384], scalar=0.0, in1=sbias, op0=ALU.min, op1=ALU.add), ex_ready)

            for n in range(8 + 1):
                if n < 8:
                    t, b = n % 2, n % 2
                    w = P * (t + 1)
                    dve.wait_ge(dsc_ready, n + 1)
                    if n >= 2:
                        dve.wait_ge(dpT_ready, n - 1)
                    src = psum[:, 2 * b:2 * b + 2, :].rearrange("p b n -> p (b n)")[:, 0:DIL * w]
                    step(TT(S2[:, b, 0:DIL * w], src, dmask[t].rearrange("p g k -> p (g k)"), ALU.add))
                    step(nc.vector.reduce_max(mx1[:, b:b + 1], S2[:, b, 0:DIL * w], AX))
                    step(TS(nmx1[:, b:b + 1], mx1[:, b:b + 1], -1.0, None, ALU.mult), dmasked)
                if n >= 1:
                    b = (n - 1) % 2
                    w = DIL * P * (b + 1)
                    dve.wait_ge(dprobs, n)
                    step(nc.vector.reciprocal(rs1[:, b:b + 1], sum1[:, b:b + 1]))
                    step(TS(S2[:, b, 0:w], S2[:, b, 0:w], rs1[:, b:b + 1], None, ALU.mult), dprobs_n)

            for c in range(KD):
                dve.wait_ge(br_ready, c + 1)
                dve.wait_ge(gate_on, c + 1)
                both = tmp2.rearrange("p (r s) -> p r s", r=2)
                gates = gT.rearrange("p (r c) s -> p r c s", r=2)[:, :, c, :]
                step(TT(both, psum[:, c % 4, :].rearrange("p (r s) -> p r s", r=2), gates, ALU.mult))
                step(TT(merT[:, c, :], both[:, 0, :], both[:, 1, :], ALU.add), mer_ready)
            dve.wait_ge(rows_out, 8)
            dve.wait_ge(rows_in, 32)
            step(STT(out=rows[:, 2, :], in0=rows[:, 2, :], scalar=1.0, in1=gffn2r, op0=ALU.add, op1=ALU.mult))
            step(nc.vector.memset(zeros, 0.0), zeros_ready)
            for t in range(NT):
                for b in range(2):
                    if (t, b) == (0, 1):
                        dve.wait_ge(out2_ready, 1)
                    else:
                        dve.wait_ge(units_used, U_OUT2 + (0 if t == 0 else 2 * b + 2))
                    cs_ = slice(b * 512, (b + 1) * 512)
                    step(TT(tmp2, psum[:, 2 * t + b, :], rows[:, 0, cs_], ALU.mult))
                    step(TT(xres[:, t, cs_], xres[:, t, cs_], tmp2, ALU.add), xadd)
                norm((t,), junk_at=norm_junk)
                step(STT(out=h2[:, t, :], in0=xres[:, t, :], scalar=rstd[:, t:t + 1], in1=rows[:, 2, :], op0=ALU.mult, op1=ALU.mult))
                step(TT(h2[:, t, :], h2[:, t, :], rows[:, 1, :], ALU.add), xn_ready)

            LOW = -3.4e38

            def route(b, m):
                def s(ins):
                    dve.drain()

                dve.wait_ge(staged, m + 1)
                nc.vector.memset(stat[:, 81:82], 0.0)
                dve.drain()
                for q in range(2):
                    row = stg[:, b, q * P:(q + 1) * P]
                    lo, hi = stop[:, b, q, 0:8], stop[:, b, q, 8:16]
                    s(nc.vector.max(lo, row))
                    s(nc.vector.max_index(itop[:, b, q, 0:8], lo, row))
                    s(nc.vector.match_replace(row, lo, row, LOW))
                    s(nc.vector.max(hi, row))
                    s(nc.vector.max_index(itop[:, b, q, 8:16], hi, row))
                c3 = cand.rearrange("p (i j) -> p i j", i=TOPK)
                sh = [P, TOPK, TOPK]
                s(TT(c3, stop[:, b, 0, :].unsqueeze(2).to_broadcast(sh), stop[:, b, 1, :].unsqueeze(1).to_broadcast(sh), ALU.add))
                s(nc.vector.max(best[:, 0:8], cand))
                s(nc.vector.max_index(pos[:, 0:8], best[:, 0:8], cand))
                s(nc.vector.match_replace(cand, best[:, 0:8], cand, LOW))
                s(nc.vector.max(best[:, 8:16], cand))
                s(TS(gnb, best[:, 0:1], -1.0, None, ALU.mult))
                nc.vector.max_index(pos[:, 8:16], best[:, 8:16], cand).then_inc(best_ready, 1)
                dve.wait_ge(best_ready, m + 1)
                s(nc.vector.tensor_copy(itopf, itop[:, b, :, :]))
                s(TS(ij[:, 0, :], pos, 4, None, ALU.logical_shift_right))
                s(TS(ij[:, 1, :], pos, 15, None, ALU.bitwise_and))
                s(nc.vector.tensor_copy(ijf, ij))
                sh4 = [P, 2, TOPK, TOPK]
                s(TT(oh, ijf.unsqueeze(3).to_broadcast(sh4), iota.unsqueeze(1).unsqueeze(1).to_broadcast(sh4), ALU.is_equal))
                s(TT(oh, oh, itopf.unsqueeze(2).to_broadcast(sh4), ALU.mult))
                s(nc.vector.tensor_reduce(e12, oh, AX, ALU.add))
                dve.wait_ge(gexp_ready, m + 1)
                s(nc.vector.reciprocal(grs, gsum))
                s(TS(gate[:, b, :], gexp, grs, None, ALU.mult))
                STT(out=expert[:, b, :], in0=e12[:, 0, :], scalar=128.0, in1=e12[:, 1, :], op0=ALU.mult,
                    op1=ALU.add).then_inc(routed, 1)
                dve.wait_ge(routed, m + 1)

            def dots_of(b, m, t, q):
                for k in range(4 * q, 4 * q + 4):
                    u = k % NU
                    dve.wait_ge(u_in[u], m * (TOPK // NU * 16) + 16 * (k // NU + 1))
                    nc.vector.tensor_tensor_reduce(out=U[u], in0=U[u], in1=h2[:, t, :], scale=1.0, scalar=0.0,
                                                   op0=ALU.mult, op1=ALU.add, accum_out=dots[:, b, k:k + 1]).then_inc(u_used, 1)

            def weigh(b, m, q):
                dve.wait_ge(gelued, m * 4 + q + 1)
                for k in range(4 * q, 4 * q + 4):
                    dve.wait_ge(v_used, m * TOPK + k + 1)
                    ins = TS(diag[:, k % ND, :], ident, gel[:, b, k:k + 1], gate[:, b, k:k + 1], ALU.mult, ALU.mult)
                ins.then_inc(diag_ready, 1)

            def head(b, m, t, more=True):
                dots_of(b, m, t, 0)
                dots_of(b, m, t, 1)
                weigh(b, m, 0)
                if more:
                    dve.wait_ge(idx_read, m + 1)
                    route(1 - b, m + 1)
                dots_of(b, m, t, 2)
                weigh(b, m, 1)
                dots_of(b, m, t, 3)
                weigh(b, m, 2)
                weigh(b, m, 3)

            for _ in range(NU):
                step(nc.vector.memset(junk, 0.0), u_used)
            for _ in range(ND):
                step(nc.vector.memset(junk, 0.0), v_used)
            step(nc.vector.memset(junk, 0.0), idx_read)
            step(nc.vector.memset(junk, 0.0), peer_go)

            def finish(t):
                dve.wait_ge(tile_done, t + 1)
                for c in range(2):
                    cs_ = slice(c * 512, (c + 1) * 512)
                    step(TT(fin[:, cs_], psum[:, 2 * t + c, :], rows[:, 3, cs_], ALU.mult))
                step(TT(xres[:, t, :], xres[:, t, :], fin, ALU.add))
                norm((t,), junk_at=fin)
                step(STT(out=xres[:, t, :], in0=xres[:, t, :], scalar=rstd[:, t:t + 1], in1=gfin2r, op0=ALU.mult, op1=ALU.mult), acc_out)

            route(0, 0)
            with dve.Fori(0, PEER_HEADS // 2) as i:
                head(0, i * 2, 0)
                head(1, i * 2 + 1, 0)
            with dve.Fori(0, PEER_HEADS // 2 - 1) as i:
                head(0, i * 2 + 8, 1)
                head(1, i * 2 + 9, 1)
            head(0, 14, 1)
            finish(0)
            head(1, 15, 1, more=False)
            finish(1)


def shape_constants(np):
    f = np.float32
    c = np.zeros((P, NCONST), f)
    i = np.arange(P)
    c[:, C_ID:C_ID + P] = np.eye(P)
    c[:, C_REV:C_REV + P] = np.eye(P)[::-1]
    c[:, C_TRI:C_TRI + P] = i[:, None] >= i[None, :]
    c[:, C_ONE:C_ONE + P] = 1.0
    q = np.arange(SEQ)
    seen = (q[None, :] // 64) <= (q[:, None] // 64)
    c[:, C_MASK1:C_MASK1 + 512] = np.where(seen, 0.0, NEG).reshape(NT, P, SEQ).transpose(1, 0, 2).reshape(P, 512)
    before = (i[:, None] < i[None, :])
    open_ = np.concatenate([before, np.ones((P, P), bool), before], axis=1)
    c[:, C_NEGM:C_NEGM + 384] = -open_.astype(f)
    c[:, C_BIAS:C_BIAS + 384] = np.where(open_, 0.0, NEG)
    back = q[:, None] - q[None, :]
    for t, at in ((0, C_DM0), (1, C_DM1)):
        w = P * (t + 1)
        for g, (win, r) in enumerate(((128, 1), (512, 4), (2048, 16))):
            ok = (back >= 0) & (back <= win) & (back % r == 0)
            c[:, at + g * w:at + (g + 1) * w] = np.where(ok, 0.0, NEG)[t * P:(t + 1) * P, :w]
    half = HD // 2
    inv = (f(10000.0) ** (-np.arange(half, dtype=f) / f(half))).astype(f)
    ang = q.astype(f)[:, None] * inv[None, :]
    cs, sn = np.cos(ang).astype(f), np.sin(ang).astype(f)
    c[:, C_COS:C_COS + 128] = np.concatenate([cs, cs], 1).reshape(NT, P, 64).transpose(1, 0, 2).reshape(P, 128)
    c[:, C_SIN:C_SIN + 128] = np.concatenate([-sn, sn], 1).reshape(NT, P, 64).transpose(1, 0, 2).reshape(P, 128)
    c[:, C_IOTA:C_IOTA + TOPK] = np.arange(TOPK)
    return c


def weight_stream(np, a):
    units = []

    def add(w):
        assert w.shape[0] == P and w[0].size == UNIT, w.shape
        units.append(w.reshape(P, UNIT))

    def chunked(w):
        return w.reshape(w.shape[0] // P, P, w.shape[1]).transpose(1, 0, 2)

    def columns(w, lo):
        w = chunked(w)
        for k in range(0, w.shape[1], 4):
            add(w[:, k:k + 4, lo:lo + 512])

    w_in = a["w_in"][0]
    for b in range(4):
        columns(w_in, b * 512)
    columns(a["ssm_w_glu"][0], 0)
    for b in range(2):
        columns(a["w_out"][0], b * 512)
    gate, up, down = (chunked(a[n][0]) for n in ("w_gate", "w_up", "w_down"))
    for f in range(NFF + 1):
        if f < NFF:
            add(gate[:, :, f * 256:(f + 1) * 256])
            add(up[:, :, f * 256:(f + 1) * 256])
        if f >= 1:
            add(down[:, 2 * (f - 1):2 * f, :])
    w_in2 = a["w_in_2"][0]
    for b in range(7):
        columns(w_in2, b * 512)
    add(chunked(w_in2)[:, :, 3584:3840])
    for b in range(4):
        columns(w_in2, 3840 + b * 512)
    for b in range(2):
        columns(a["w_sb_o_2"][0], b * 512)
    add(chunked(a["w_dil_o_2"][0]))
    for b in range(2):
        columns(a["w_out_2"][0], b * 512)
    for b in range(4):
        columns(a["w_pq_2"][0], b * 512)
    assert len(units) == UNITS
    return np.stack(units)


def kernel(**inputs):
    import numpy as np
    import concourse.bacc as bacc
    from concourse.bass_utils import run_bass_kernel_spmd

    a = {k: np.asarray(v) for k, v in inputs.items()}

    def cols(v):
        return v.reshape(-1, P).T

    def states(v):
        return v.reshape(NST, P).T

    vecs = np.concatenate([
        cols(a["norm_mix_g"]), cols(a["norm_ffn_g"]), cols(a["norm_ssm_out_g"]), cols(a["norm_att_out_g"]),
        cols(a["ssm_d"]), cols(a["ssm_b_glu"]), cols(a["g_mix_2"]), cols(a["c_2"]),
        states(a["ssm_lam_re"]), states(a["ssm_lam_im"]), states(np.repeat(a["ssm_log_dt"][0], STATE))], axis=1)
    ssm_b = np.zeros((P, 4, 2, P), np.float32)
    ssm_c = np.zeros((P, NST, 2, 32), np.float32)
    for g in range(GROUPS):
        j, half = g // 2, g % 2
        r = 32 * (j % 4) + GCH * half
        for ri, (b, c) in enumerate((("ssm_b_re", "ssm_c_re"), ("ssm_b_im", "ssm_c_im"))):
            ssm_b[r:r + GCH, j // 4, ri, STATE * half:STATE * (half + 1)] = a[b][0, g].T
            ssm_c[STATE * half:STATE * (half + 1), j, ri, GCH * half:GCH * (half + 1)] = a[c][0, g].T
    rel = a["attn_rel_bias"][0]
    rel_ext = np.concatenate([np.repeat(rel[:, :1], 127, axis=1), rel], axis=1)
    w_ada = a["w_ada_2"][0].reshape(KD, P, 12, 512).transpose(2, 1, 0, 3).reshape(12, P, KD * 512)
    arrays = {
        "x": a["x"][0], "consts": shape_constants(np), "vecs": vecs, "weights": weight_stream(np, a),
        "sub_keys": a["peer_keys_2"][0].reshape(16, P, P).transpose(2, 0, 1).reshape(P, UNIT),
        "ssm_b": ssm_b, "ssm_c": ssm_c, "rel_ext": rel_ext, "g_final1": a["norm_final_g"][None], "w_ada": w_ada,
        "b_ada": a["b_ada_2"], "g_ffn2": a["g_ffn_2"], "g_final2": a["g_final_2"][None],
        "peer_u": a["peer_u_2"][0], "peer_v": a["peer_v_2"][0],
    }
    arrays = {k: np.ascontiguousarray(v) for k, v in arrays.items()}
    nc = bacc.Bacc("TRN2", target_bir_lowering=False, num_devices=1)
    args = {k: nc.dram_tensor(f"in_{k}", v.shape, mybir.dt.from_np(v.dtype), kind="ExternalInput").ap()
            for k, v in arrays.items()}
    out = nc.dram_tensor("out_x", (SEQ, D), F32, kind="ExternalOutput").ap()
    build(nc, out=out, **args)
    r = run_bass_kernel_spmd(nc, [{f"in_{k}": v for k, v in arrays.items()}], core_ids=[0])
    return r.results[0]["out_x"].reshape(1, SEQ, D)
```

```python
from contextlib import ExitStack

import concourse.bass as bass
from concourse import mybir

F32 = mybir.dt.float32
U32 = mybir.dt.uint32
I32 = mybir.dt.int32
ALU = mybir.AluOpType
ACT = mybir.ActivationFunctionType
AX = mybir.AxisListType.X

P = 128
D = 1024
SEQ = 256
NT = SEQ // P
KD = D // P
DFF = 2816
NFF = DFF // 256
GROUPS, STATE, GCH = 32, 64, 16
NST = GROUPS * STATE // P
HD = 64
HEADS = 8
DIL = 3
DIL_HEADS = 4
PEER_HEADS = 8
TOPK = 16
EPS = 1e-6
NEG = -1e30
SCALE = HD ** -0.5
RING = 6
UNIT = 2048
NU, NV = 8, 8
LAG = 8
ND = 16

U_IN, U_GLU, U_OUT, U_FF = 0, 8, 9, 13
U_IN2 = U_FF + 3 * NFF
U_GATES, U_SBO, U_DILO, U_OUT2, U_PQ = U_IN2 + 15, U_IN2 + 23, U_IN2 + 25, U_IN2 + 26, U_IN2 + 30
UNITS = U_PQ + 8
assert U_PQ + 2 + RING >= UNITS

V_GMIX, V_GFFN, V_GSSM, V_GATT, V_D, V_BGLU, V_GMIX2, V_C, V_LRE, V_LIM, V_LDT = 0, 8, 16, 20, 24, 28, 32, 40, 48, 64, 80
NVEC = 96

C_ID, C_REV, C_TRI, C_ONE, C_MASK1, C_NEGM, C_BIAS, C_DM0, C_DM1, C_COS, C_SIN, C_IOTA = (
    0, 128, 256, 384, 512, 1024, 1408, 1792, 2176, 2944, 3072, 3200)
NCONST = 3216


def build(nc, x, consts, vecs, weights, sub_keys, ssm_b, ssm_c, rel_ext, g_final1, w_ada, b_ada, g_ffn2, g_final2,
          peer_u, peer_v, out, dbg=None):
    with ExitStack() as ctx:
        def sem(name):
            return ctx.enter_context(nc.semaphore(name))

        arena = ctx.enter_context(nc.sbuf_tensor("arena", [P, 53100], F32))
        psum = ctx.enter_context(nc.psum_tensor("psum", [P, 8, 512], F32))

        top = [0]

        def take(words, at=None):
            a = top[0] if at is None else at
            if at is None:
                top[0] += words
            assert a + words <= 53100, (a, words)
            return arena[:, a:a + words]

        cst = take(NCONST)
        vec = take(NVEC)
        xres = take(NT * D).rearrange("p (t d) -> p t d", t=NT)
        hT = take(KD * SEQ).rearrange("p (k s) -> p k s", k=KD)
        ring = take(RING * UNIT).rearrange("p (r w) -> p r w", r=RING)
        stat = take(256)
        ada_at = top[0]
        ada_slot = take(4096).rearrange("p (k n) -> p k n", k=KD)
        ada_acc = take(6144)
        ph = top[0]

        ident = cst[:, C_ID:C_ID + P]
        rev = cst[:, C_REV:C_REV + P]
        tri = cst[:, C_TRI:C_TRI + P]
        ones = cst[:, C_ONE:C_ONE + P]
        mask1 = cst[:, C_MASK1:C_MASK1 + 512].rearrange("p (t k) -> p t k", t=2)
        negm = cst[:, C_NEGM:C_NEGM + 384]
        sbias = cst[:, C_BIAS:C_BIAS + 384]
        dmask = [cst[:, C_DM0:C_DM0 + 384].rearrange("p (g k) -> p g k", g=DIL),
                 cst[:, C_DM1:C_DM1 + 768].rearrange("p (g k) -> p g k", g=DIL)]
        cos = cst[:, C_COS:C_COS + 128].rearrange("p (t d) -> p t d", t=NT)
        sin = cst[:, C_SIN:C_SIN + 128].rearrange("p (t d) -> p t d", t=NT)
        iota = cst[:, C_IOTA:C_IOTA + TOPK]

        o = ph
        Z = take(8192, o).rearrange("p (j r t) -> p j r t", j=NST, r=2); zo = o; o += 8192

        def pair_shape(place):
            return place.rearrange("p (j r t) -> p j r t", j=2, r=2)

        T1 = pair_shape(take(1024, o)); o += 1024
        T2 = pair_shape(take(1024, o)); o += 1024
        TB = hT.rearrange("p k s -> p (k s)")

        def T1v(c):
            return arena[:, zo + 8192 + 256 * c:zo + 8192 + 256 * (c + 1)]

        BZ = take(1024, o).rearrange("p (c r m) -> p c r m", c=4, r=2); o += 1024
        CT = take(1024, o).rearrange("p (j r m) -> p j r m", j=NST, r=2); o += 1024
        CP = take(1024, o).rearrange("p (j r m) -> p j r m", j=NST, r=2); o += 1024
        uT = take(1024, o).rearrange("p (c s) -> p c s", c=4); o += 1024
        qk_at = o
        qT = take(1024, o).rearrange("p (c s) -> p c s", c=4); o += 1024
        kT = take(1024, o).rearrange("p (c s) -> p c s", c=4); o += 1024
        vN = take(1024, o).rearrange("p (t c) -> p t c", t=NT); o += 1024
        hb_at = o
        HB = take(2048, o).rearrange("p (h m) -> p h m", h=HEADS); o += 2048
        S1 = take(1024, o); o += 1024
        S1s = [BZ.rearrange("p c r m -> p (c r m)")[:, 0:384], S1[:, 0:384], S1[:, 512:896]]
        PT1 = take(768, o).rearrange("p (b k) -> p b k", b=2); o += 768
        sm1 = take(256, o); o += 256
        T1s = [T1, pair_shape(take(1024, o))]; o += 1024
        T2s = [[T2, pair_shape(S1)], [T2, pair_shape(TB[:, 0:1024])]]
        E = take(8192, ada_at).rearrange("p (j r t) -> p j r t", j=NST, r=2)
        mixT = take(2048, ada_at + 8192).rearrange("p (k s) -> p k s", k=KD)
        xn1 = take(2048, zo).rearrange("p (t d) -> p t d", t=NT)
        etmp = take(4096, zo + 2048)
        gy = take(1024, zo).rearrange("p (c s) -> p c s", c=4)
        sg = take(1024, zo + 1024).rearrange("p (c s) -> p c s", c=4)
        sqr = take(2048, qk_at).rearrange("p (c s) -> p c s", c=KD)
        cv, cq, cy, ct = (take(512, hb_at + 512 * i) for i in range(4))
        fo = zo + 8192
        silu = take(1024, fo).rearrange("p (b n) -> p b n", b=2)
        actT = take(1024, fo + 1024).rearrange("p (b f s) -> p b f s", b=2, f=2)
        gfin1 = take(1024, fo + 2048)
        xn2 = take(2048, zo + 6144).rearrange("p (t d) -> p t d", t=NT)
        coef = [sm1[:, 16 * i:16 * i + 16] for i in range(16)]
        ssq, var, sq, rstd, nt1 = (stat[:, 2 * i:2 * i + 2] for i in range(5))
        siluc = stat[:, 16:24]
        modc = stat[:, 32:48]
        gm2 = stat[:, 48:56]
        mx3, nmx3, sum3, rs3 = (stat[:, 96 + 6 * i:102 + 6 * i] for i in range(4))
        mx1, nmx1 = stat[:, 64:68], stat[:, 68:72]
        sum1, rs1 = stat[:, 72:76], stat[:, 76:80]
        junk = stat[:, 80:81]

        o = ph
        qkd = take(3072, o).rearrange("p (t n) -> p t n", t=NT); o += 3072
        vd = take(1536, o).rearrange("p (t n) -> p t n", t=NT); o += 1536
        vsb = take(1024, o).rearrange("p (t n) -> p t n", t=NT); o += 1024
        qTs = take(1024, o).rearrange("p (c s) -> p c s", c=4); o += 1024
        kTs = take(1024, o).rearrange("p (c s) -> p c s", c=4); o += 1024
        gT = take(4096, o).rearrange("p (c s) -> p c s", c=16); o += 4096
        ropeA = take(1536, o); o += 1536
        ropeB = take(1536, o); o += 1536
        qkdT = take(3072, o).rearrange("p (c s) -> p c s", c=12); o += 3072
        xn3 = take(2048, o - 3072).rearrange("p (t d) -> p t d", t=NT)
        sba = take(768, o).rearrange("p (b n) -> p b n", b=2); o += 768
        sbl = take(768, o).rearrange("p (b n) -> p b n", b=2); o += 768
        S2 = take(1536, o).rearrange("p (b n) -> p b n", b=2); o += 1536
        PT2 = take(1536, o).rearrange("p (b n) -> p b n", b=2); o += 1536
        tmp2 = S2[:, 0, 0:512]
        rows = take(4096, ada_at).rearrange("p (v d) -> p v d", v=4)
        aa = ada_at + 4096
        osbT = take(1024, aa).rearrange("p (c s) -> p c s", c=4)
        odT = take(512, aa + 1024).rearrange("p (c s) -> p c s", c=2)
        merT = take(2048, aa + 1536).rearrange("p (c s) -> p c s", c=KD)
        gffn2r = take(1024, aa + 3584)
        gfin2r = take(1024, aa + 4608)

        o = ph
        h2 = take(2048, o).rearrange("p (t d) -> p t d", t=NT); o += 2048
        sub = take(16 * 256, o); o += 16 * 256
        qpT = take(4096, o).rearrange("p (c s) -> p c s", c=16); o += 4096
        U = [take(D, aa + D * b) for b in range(4)] + [take(D, o + D * b) for b in range(4)]; o += 4 * D
        V = [take(D, o + D * b) for b in range(6)] + [ring[:, (U_PQ + 2) % RING, D * b:D * (b + 1)] for b in range(2)]; o += 6 * D
        keys = cst[:, C_MASK1:C_MASK1 + UNIT].rearrange("p (c n) -> p c n", c=16)
        res_tmp, norm_junk = sub[:, 2048:2560], sub[:, 3072:4096]
        zeros = take(512, o); o += 512
        stg = take(512, o).rearrange("p (b n) -> p b n", b=2); o += 512
        stop = take(64, o).rearrange("p (b q k) -> p b q k", b=2, q=2); o += 64
        itop = take(64, o).bitcast(U32).rearrange("p (b q k) -> p b q k", b=2, q=2); o += 64
        itopf = take(32, o).rearrange("p (q k) -> p q k", q=2); o += 32
        cand = take(256, o); o += 256
        best = take(16, o); o += 16
        pos = take(16, o).bitcast(U32); o += 16
        ij = take(32, o).bitcast(U32).rearrange("p (q k) -> p q k", q=2); o += 32
        ijf = take(32, o).rearrange("p (q k) -> p q k", q=2); o += 32
        oh = take(512, o).rearrange("p (q k i) -> p q k i", q=2, k=TOPK); o += 512
        e12 = take(32, o).rearrange("p (q k) -> p q k", q=2); o += 32
        expert = take(32, o).bitcast(U32).rearrange("p (b k) -> p b k", b=2); o += 32
        gate = take(32, o).rearrange("p (b k) -> p b k", b=2); o += 32
        gexp = take(16, o); o += 16
        gnb, gsum, grs = take(1, o), take(1, o + 1), take(1, o + 2); o += 4
        dots = take(32, o).rearrange("p (b k) -> p b k", b=2); o += 32
        gel = take(32, o).rearrange("p (b k) -> p b k", b=2); o += 32
        diag = rows[:, 0:2, :].rearrange("p v d -> p (v d)").rearrange("p (b m) -> p b m", b=ND)
        fin = qpT[:, 0:4, :].rearrange("p c s -> p (c s)")

        x_in = [sem(f"x_in{t}") for t in range(NT)]
        c_in, vec_in, b_in, cc_in, h_in = (sem(n) for n in ("c_in", "vec_in", "b_in", "cc_in", "h_in"))
        gf_in, bada_in, ada_in, rows_in, out_done = (sem(n) for n in ("gf_in", "bada_in", "ada_in", "rows_in", "out_done"))
        unit_in = [sem(f"unit_in{s}") for s in range(RING)]
        units_used = sem("units_used")
        dve_step = sem("dve_step")
        act_step = sem("act_step")
        var_ready, sqrt_ready = sem("var_ready"), sem("sqrt_ready")
        xn_ready = sem("xn_ready")
        turned = sem("turned")
        hT_act, hT_dve = sem("hT_act"), sem("hT_dve")
        proj_out = sem("proj_out")
        trig_in, trig_out = sem("trig_in"), sem("trig_out")
        bu_ready, bu_used = sem("bu_ready"), sem("bu_used")
        cp_ready = sem("cp_ready")
        states_ready, y_ready = sem("states_ready"), sem("y_ready")
        turned_back, forward = sem("turned_back"), sem("forward")
        sc_ready, max_ready, probs, probs_n, pT_ready, pT_out, o_ready, o_out = (
            sem(n) for n in ("sc_ready", "max_ready", "probs", "probs_n", "pT_ready", "pT_out", "o_ready", "o_out"))
        out1_ready, down_ready, masks_in = sem("out1_ready"), sem("down_ready"), sem("masks_in")
        yd_ready, gy_ready, sig_ready, glu_ready, sqr_ready, csum_ready, mix_ready = (
            sem(n) for n in ("yd_ready", "gy_ready", "sig_ready", "glu_ready", "sqr_ready", "csum_ready", "mix_ready"))
        xadd = sem("xadd")
        silu_ready, act_ready = sem("silu_ready"), sem("act_ready")
        ada_used, siluc_ready, acc_zero = (sem(n) for n in ("ada_used", "siluc_ready", "acc_zero"))
        mod_ready, modc_out, rows_out = sem("mod_ready"), sem("modc_out"), sem("rows_out")
        z_ready, e_ready, l_ready, ex_ready, cum_ready, at_ready = (
            sem(n) for n in ("z_ready", "e_ready", "l_ready", "ex_ready", "cum_ready", "at_ready"))
        sbo_ready, sbo_out = sem("sbo_ready"), sem("sbo_out")
        roped, qkT_ready, qkT_out = sem("roped"), sem("qkT_ready"), sem("qkT_out")
        dsc_ready, dmasked, dprobs, dprobs_n, dpT_ready, dpT_out, do_ready, do_out = (
            sem(n) for n in ("dsc_ready", "dmasked", "dprobs", "dprobs_n", "dpT_ready", "dpT_out", "do_ready", "do_out"))
        gate_ready, gates_left, gate_on = (sem(n) for n in ("gate_ready", "gates_left", "gate_on"))
        br_ready, mer_ready = sem("br_ready"), sem("mer_ready")
        sub_ready, sub_out, keys_in = sem("sub_ready"), sem("sub_out"), sem("keys_in")
        out2_ready, first_ready = sem("out2_ready"), sem("first_ready")
        staged, routing, best_ready, gexp_ready, routed = (
            sem(n) for n in ("staged", "routing", "best_ready", "gexp_ready", "routed"))
        u_in = [sem(f"u_in{b}") for b in range(NU)]
        v_in = [sem(f"v_in{b}") for b in range(NV)]
        u_used = sem("u_used")
        v_used = sem("v_used")
        gelued, diag_ready, tile_done, acc_out = (
            sem(n) for n in ("gelued", "diag_ready", "tile_done", "acc_out"))
        zeros_ready = sem("zeros_ready")
        idx_read = sem("idx_read")
        peer_go = sem("peer_go")

        block = ctx.enter_context(nc.Block())

        def stepper(eng, own):
            counts = {}

            def mark(ins, s=own):
                ins.then_inc(s, 1)
                counts[s.name] = counts.get(s.name, 0) + 1
                return counts[s.name]

            def step(ins, s=own):
                eng.wait_ge(s, mark(ins, s))

            return mark, step

        @block.sync
        def _(sp):
            for t in range(NT):
                sp.dma_start(xres[:, t, :], x[t * P:(t + 1) * P, :]).then_inc(x_in[t], 16)
            sp.dma_start(vec, vecs).then_inc(vec_in, 16)
            sp.dma_start(cst[:, 0:C_MASK1], consts[:, 0:C_MASK1]).then_inc(c_in, 16)
            for s in range(RING):
                sp.dma_start(ring[:, s, :], weights[s]).then_inc(unit_in[s], 16)
                if s == 1:
                    sp.dma_start(cst[:, C_MASK1:], consts[:, C_MASK1:]).then_inc(masks_in, 16)
            rounds = (UNITS - RING) // RING
            with sp.Fori(0, rounds) as i:
                for s in range(RING):
                    sp.wait_ge(units_used, i * RING + s + 1)
                    sp.dma_start(ring[:, s, :], weights[bass.ds((i + 1) * RING + s, 1)].rearrange("a p w -> (a p) w")
                                 ).then_inc(unit_in[s], 16)
            for n in range(RING * (rounds + 1), UNITS):
                sp.wait_ge(units_used, n - RING + 1)
                sp.dma_start(ring[:, n % RING, :], weights[n]).then_inc(unit_in[n % RING], 16)
            for t in range(NT):
                sp.wait_ge(acc_out, t + 1)
                sp.dma_start(out[t * P:(t + 1) * P, :], xres[:, t, :]).then_inc(out_done, 16)
            sp.wait_ge(out_done, 16 * NT)
            if dbg is not None:
                sp.dma_start(dbg, arena[:, :]).then_inc(out_done, 16)
                sp.wait_ge(out_done, 16 * (NT + 1))

        @block.gpsimd
        def _(pool):
            pool.dma_start(BZ, ssm_b).then_inc(b_in, 16)
            pool.dma_start(CT, ssm_c).then_inc(cc_in, 16)
            for h in range(HEADS):
                src = bass.AP(rel_ext.tensor, h * 384, [[1, P], [1, 256]])
                pool.dma_start(HB[:, h, :], src).then_inc(h_in, 16)
            for q in range(NST // 2):
                pool.wait_ge(bu_used, q + 1)
                z, t1, t2 = Z[:, 2 * q:2 * q + 2, :, :], T1s[q % 2], T2s[0][q % 2]
                nc.gpsimd.tensor_tensor(z[:, :, 0, :], t1[:, :, 0, :], t2[:, :, 1, :], ALU.add)
                nc.gpsimd.tensor_tensor(z[:, :, 1, :], t1[:, :, 1, :], t2[:, :, 0, :], ALU.subtract).then_inc(turned_back, 1)
            for q in range(NST // 2):
                pool.wait_ge(forward, q + 1)
                z, t1, t2 = Z[:, 2 * q:2 * q + 2, :, :], T1s[q % 2], T2s[1][q % 2]
                nc.gpsimd.tensor_tensor(z[:, :, 0, :], t1[:, :, 0, :], t2[:, :, 1, :], ALU.subtract)
                nc.gpsimd.tensor_tensor(z[:, :, 1, :], t1[:, :, 1, :], t2[:, :, 0, :], ALU.add).then_inc(states_ready, 1)
            pool.dma_start(ada_slot, w_ada[0].rearrange("p (k n) -> p k n", k=KD)).then_inc(ada_in, 16)
            pool.wait_ge(xadd, 4)
            nc.gpsimd.memset(ada_acc, 0.0).then_inc(acc_zero, 1)
            pool.wait_ge(acc_zero, 1)
            pool.dma_start(ada_acc[0:1, :], b_ada).then_inc(bada_in, 16)
            pool.dma_start(gfin1, g_final1.partition_broadcast(P)).then_inc(gf_in, 16)
            with pool.Fori(0, 11) as i:
                pool.wait_ge(ada_used, i + 1)
                pool.nop()
                pool.dma_start(ada_slot, w_ada[bass.ds(i + 1, 1)].rearrange("a p (k n) -> (a p) k n", k=KD)
                               ).then_inc(ada_in, 16)
            pool.wait_ge(mod_ready, 9)
            pool.wait_ge(rows_out, 8)
            pool.dma_start(gffn2r, g_ffn2.partition_broadcast(P)).then_inc(rows_in, 16)
            pool.dma_start(gfin2r, g_final2.partition_broadcast(P)).then_inc(rows_in, 16)
            pool.wait_ge(dmasked, 8)
            pool.dma_start(cst[:, C_MASK1:C_MASK1 + UNIT], sub_keys).then_inc(keys_in, 16)
            pool.wait_ge(peer_go, 1)

            def gather(table, buf, used, ahead, arrived, b, k, n, read=None):
                turn = pool.to_reg(n + ahead)
                pool.wait_ge(peer_go, 1)
                pool.wait_ge(used, turn)
                pool.indirect_dma_start(buf, None, table, bass.IndirectOffsetOnAxis(ap=expert[:, b, k:k + 1], axis=0),
                                        engine_sem=read).then_inc(arrived, 16)

            def row_u(b, k, n):
                gather(peer_u, U[k % NU], u_used, 1, u_in[k % NU], b, k, n)

            def row_v(b, k, n):
                if k == 6:
                    pool.wait_ge(units_used, U_PQ + 4)
                gather(peer_v, V[k % NV], v_used, ND - NV + 1, v_in[k % NV], b, k, n, idx_read if k == TOPK - 1 else None)

            def head(b, m, last=False):
                for k in range(TOPK):
                    row_v(b, k, m * TOPK + k)
                    if k < TOPK - LAG:
                        row_u(b, k + LAG, m * TOPK + (k + LAG))
                    elif not last:
                        if k == TOPK - LAG:
                            following = pool.to_reg(m + 2)
                            pool.wait_ge(peer_go, 1)
                            pool.wait_ge(routed, following)
                        row_u(1 - b, k + LAG - TOPK, m * TOPK + (k + LAG))

            pool.wait_ge(units_used, U_OUT2 + 4)
            pool.wait_ge(routed, 1)
            for k in range(LAG):
                row_u(0, k, k)
            with pool.Fori(0, NT * PEER_HEADS // 2 - 1) as i:
                head(0, i * 2)
                head(1, i * 2 + 1)
            head(0, 14)
            head(1, 15, last=True)

        @block.tensor
        def _(pe):
            mm = nc.tensor.matmul

            def unit(n, i=None, per=1):
                value = 16 * (n // RING + 1)
                pe.wait_ge(unit_in[n % RING], value if i is None else i * (16 * per) + value)
                return ring[:, n % RING, :]

            def turn(src, want, tiles=range(NT)):
                for t in tiles:
                    pe.wait_ge(xn_ready, want + t + 1)
                    for k in range(KD):
                        ins = nc.tensor.transpose(
                            psum[:, 4 + k // 2, (k % 2) * 256 + t * P:(k % 2) * 256 + (t + 1) * P],
                            src[:, t, k * P:(k + 1) * P], ident)
                        if k % 2 == 1 and t == tiles[-1]:
                            ins.then_inc(turned, 1)

            def have_hT(n):
                pe.wait_ge(hT_act, 4 * n)
                pe.wait_ge(hT_dve, 4 * n)

            def block_T(banks, lo, hi, src, lo_t=0, hi_t=SEQ):
                for c in range(4):
                    for k in range(KD):
                        w = (lo if k < 4 else hi).rearrange("p (k n) -> p k n", k=4)
                        ins = mm(psum[:, banks + c // 2, (c % 2) * 256 + lo_t:(c % 2) * 256 + hi_t],
                                 w[:, k % 4, c * P:(c + 1) * P], src[:, k, lo_t:hi_t], start=k == 0, stop=k == KD - 1)
                return ins

            def block_N(banks, lo, hi, src, tiles=range(NT)):
                for t in tiles:
                    for k in range(KD):
                        w = (lo if k < 4 else hi).rearrange("p (k n) -> p k n", k=4)
                        ins = mm(psum[:, banks + t, :], src[:, k, t * P:(t + 1) * P], w[:, k % 4, :],
                                 start=k == 0, stop=k == KD - 1)
                return ins

            pe.wait_ge(c_in, 16)
            turn(xn1, 0)
            have_hT(1)
            pe.wait_ge(b_in, 16)

            def bu(q):
                if q < 2:
                    pe.wait_ge(hT_act, 4); pe.wait_ge(hT_dve, 4)
                else:
                    pe.wait_ge(bu_used, q - 1)
                for j in (2 * q, 2 * q + 1):
                    r = 32 * (j % 4)
                    for ri in range(2):
                        ins = mm(psum[:, 4 + j % 4, ri * 256:ri * 256 + 256], BZ[r:r + 32, j // 4, ri, :],
                                 uT[r:r + 32, j // 4, :], start=True, stop=True)
                ins.then_inc(bu_ready, 1)

            for b in range(4):
                lo, hi = unit(U_IN + 2 * b), unit(U_IN + 2 * b + 1)
                if b >= 2:
                    pe.wait_ge(proj_out, 2 * (b - 1))
                if b == 3:
                    block_N(2, lo, hi, hT, tiles=(0,))
                    bu(2)
                    bu(3)
                    block_N(2, lo, hi, hT, tiles=(1,)).then_inc(units_used, 2)
                else:
                    block_T(2 * (b % 2), lo, hi, hT).then_inc(units_used, 2)
                if b == 0:
                    pe.wait_ge(proj_out, 2)
                    bu(0)
                    bu(1)
            for q in range(4, NST // 2):
                bu(q)

            pe.wait_ge(proj_out, 8)
            pe.wait_ge(h_in, 16 * HEADS)
            pe.wait_ge(masks_in, 16)
            pe.wait_ge(cp_ready, 1)

            def scores(h):
                r, c = 64 * (h % 2), h // 2
                if h >= 2:
                    pe.wait_ge(probs, 2 * (h - 1))
                bank = psum[:, h % 2, :]
                mm(bank[:, 0:P], qT[r:r + 64, c, 0:P], kT[r:r + 64, c, 0:P], start=True, stop=False)
                mm(bank[:, 0:P], rev, HB[:, h, P:2 * P], start=False, stop=False)
                mm(bank[:, 0:P], ident, mask1[:, 0, 0:P], start=False, stop=True)
                mm(bank[:, P:3 * P], qT[r:r + 64, c, P:SEQ], kT[r:r + 64, c, :], start=True, stop=False)
                mm(bank[:, P:3 * P], rev, HB[:, h, :], start=False, stop=False)
                mm(bank[:, 2 * P:3 * P], ident, mask1[:, 1, P:SEQ], start=False, stop=True).then_inc(sc_ready, 1)

            def turn_probs(h):
                pe.wait_ge(probs_n, h + 1)
                if h >= 2:
                    pe.wait_ge(pT_out, h - 1)
                for n in range(3):
                    ins = nc.tensor.transpose(psum[:, 2 + h % 2, n * P:(n + 1) * P], S1s[h % 3][:, n * P:(n + 1) * P], ident)
                ins.then_inc(pT_ready, 1)

            def values(h):
                pe.wait_ge(pT_out, h + 1)
                if h % 2 == 0 and h >= 4:
                    pe.wait_ge(o_out, h // 2 - 1)
                dst = psum[64 * (h % 2):64 * (h % 2) + 64, 4 + (h // 2) % 2, :]
                mm(dst[:, 0:256], vN[:, 0, h * HD:(h + 1) * HD], PT1[:, h % 2, 0:256], start=True, stop=False)
                mm(dst[:, P:256], vN[:, 1, h * HD:(h + 1) * HD], PT1[:, h % 2, 256:384],
                   start=False, stop=True).then_inc(o_ready, 1)

            def read_states(q):
                pe.wait_ge(states_ready, q + 1)
                for j in (2 * q, 2 * q + 1):
                    c, r = j // 4, 32 * (j % 4)
                    dst = psum[r:r + 32, 6 + c // 2, (c % 2) * 256:(c % 2) * 256 + 256]
                    for ri in range(2):
                        ins = mm(dst, CP[:, j, ri, :], Z[:, j, ri, :], start=ri == 0, stop=ri == 1)
                return ins

            for h in range(3):
                scores(h)
            pe.wait_ge(bu_used, 8)
            for h in range(HEADS):
                turn_probs(h)
                if h + 3 < HEADS:
                    scores(h + 3)
                if h >= 2:
                    read_states(h - 2)
                values(h)
            read_states(6)

            def channel_sums(br, n):
                pe.wait_ge(sqr_ready, n)
                for k in range(4):
                    ins = mm(psum[:, 4 + n - 1, 0:256], ones, sqr[:, 4 * br + k, :], start=k == 0, stop=k == 3)
                ins.then_inc(csum_ready, 1)

            channel_sums(1, 1)
            read_states(7).then_inc(y_ready, 1)

            glu = unit(U_GLU).rearrange("p (k n) -> p k n", k=4)
            pe.wait_ge(gy_ready, 4)
            for c in range(4):
                for k in range(4):
                    ins = mm(psum[:, 6 + c // 2, (c % 2) * 256:(c % 2) * 256 + 256], glu[:, k, c * P:(c + 1) * P],
                             gy[:, k, :], start=k == 0, stop=k == 3)
            ins.then_inc(units_used, 1)

            def out_half(t, b, half):
                w = unit(U_OUT + 2 * b + half).rearrange("p (k n) -> p k n", k=4)
                for k in range(4):
                    ins = mm(psum[:, 2 * t + b, :], mixT[:, 4 * half + k, t * P:(t + 1) * P], w[:, k, :],
                             start=half == 1 and k == 0, stop=half == 0 and k == 3, skip_group_check=True)
                return ins

            pe.wait_ge(mix_ready, 4)
            out_half(0, 0, 1)
            out_half(1, 0, 1)
            channel_sums(0, 2)
            out_half(0, 1, 1)
            out_half(1, 1, 1)
            pe.wait_ge(mix_ready, 8)
            out_half(0, 0, 0)
            out_half(0, 1, 0).then_inc(out1_ready, 1)
            out_half(1, 0, 0)
            out_half(1, 1, 0).then_inc(units_used, 4)

            turn(xn2, 2)
            have_hT(2)

            def gate_up(par, n, f, i=None):
                g, u = unit(n, i), unit(n + 1, i)
                if f >= 2:
                    pe.wait_ge(act_ready, f - 1 if i is None else i * 2 + (f - 1))
                for which, w in enumerate((g, u)):
                    w = w.rearrange("p (k n) -> p k n", k=KD)
                    for s in range(2):
                        for k in range(KD):
                            ins = mm(psum[:, 4 + 2 * par + which, s * 256:s * 256 + 256], w[:, k, s * P:(s + 1) * P],
                                     hT[:, k, :], start=k == 0, stop=k == KD - 1)
                ins.then_inc(units_used, 2)

            def down(par, n, f, i=None):
                w = unit(n, i).rearrange("p (s n) -> p s n", s=2)
                pe.wait_ge(act_ready, f + 1 if i is None else i * 2 + (f + 1))
                first, last = (f == 0), (i is None and f == NFF - 1)
                for t, s in ((0, 0), (0, 1), (1, 0), (1, 1)):
                    if last and (t, s) == (1, 0):
                        ins.then_inc(down_ready, 1)
                    for b in range(2):
                        ins = mm(psum[:, 2 * t + b, :], actT[:, par, s, t * P:(t + 1) * P], w[:, s, b * 512:(b + 1) * 512],
                                 start=first and s == 0, stop=last and s == 1, skip_group_check=True)
                ins.then_inc(units_used, 1)

            gate_up(0, U_FF, 0)
            gate_up(1, U_FF + 2, 1)
            down(0, U_FF + 4, 0)
            gate_up(0, U_FF + 5, 2)
            down(1, U_FF + 7, 1)
            with pe.Fori(0, 4) as i:
                gate_up(1, U_FF + 8, 3, i)
                down(0, U_FF + 10, 2, i)
                gate_up(0, U_FF + 11, 4, i)
                down(1, U_FF + 13, 3, i)
            down(0, U_FF + 32, 10)

            pe.wait_ge(ada_used, 12)
            for n in range(16):
                ins = mm(psum[:, 4, n:n + 1], ada_acc[:, n * P:(n + 1) * P], ones[:, 0:1], start=True, stop=True)
            ins.then_inc(mod_ready, 1)
            for n in range(8):
                bank = 5 + n % 2
                if n >= 2:
                    pe.wait_ge(rows_out, n - 1)
                mm(psum[:, bank, :], ones, ada_acc[:, 2048 + n * 512:2048 + (n + 1) * 512],
                   start=True, stop=True).then_inc(mod_ready, 1)

            pe.wait_ge(modc_out, 1)
            pe.wait_ge(rows_out, 8)
            turn(xn3, 4)
            have_hT(3)
            n = U_IN2
            for b in range(8):
                if b >= 2:
                    pe.wait_ge(proj_out, 8 + 2 * (b - 1))
                if b == 7:
                    w = unit(n).rearrange("p (k n) -> p k n", k=KD)
                    for t in range(NT):
                        for k in range(KD):
                            ins = mm(psum[:, 2 * (b % 2) + t, 0:256], hT[:, k, t * P:(t + 1) * P], w[:, k, :],
                                     start=k == 0, stop=k == KD - 1)
                    ins.then_inc(units_used, 1)
                    n += 1
                    continue
                lo, hi = unit(n), unit(n + 1)
                (block_T if b < 2 else block_N)(2 * (b % 2), lo, hi, hT).then_inc(units_used, 2)
                n += 2

            for c in range(12):
                if c == 0:
                    pe.wait_ge(roped, 2)
                if c >= 8 and c % 2 == 0:
                    pe.wait_ge(qkT_out, c // 2 - 3)
                for t in range(NT):
                    ins = nc.tensor.transpose(
                        psum[:, 4 + (c // 2) % 4, (c % 2) * 256 + t * P:(c % 2) * 256 + (t + 1) * P],
                        qkd[:, t, c * P:(c + 1) * P], ident)
                if c % 2 == 1:
                    ins.then_inc(qkT_ready, 1)

            def gate_chunk(m):
                b, c, bank = m // 4, m % 4, 6 + (m // 2) % 2 if m < 8 else 1
                lo, hi = unit(U_GATES + 2 * b), unit(U_GATES + 2 * b + 1)
                if m == 0:
                    pe.wait_ge(qkT_out, 6)
                elif m == 8:
                    pe.wait_ge(l_ready, HEADS)
                elif m >= 4 and m % 2 == 0:
                    pe.wait_ge(gates_left, m // 2 - (1 if m < 8 else 0))
                for k in range(KD):
                    w = (lo if k < 4 else hi).rearrange("p (k n) -> p k n", k=4)
                    ins = mm(psum[:, bank, (m % 2) * 256:(m % 2) * 256 + 256], w[:, k % 4, c * P:(c + 1) * P],
                             hT[:, k, :], start=k == 0, stop=k == KD - 1)
                if c == 1:
                    ins.then_inc(gate_ready, 1)
                if c == 3:
                    ins.then_inc(units_used, 2)

            pe.wait_ge(proj_out, 8 + 16)

            def logits(h, bank, stop):
                r, c = 64 * (h % 2), h // 2
                mm(psum[:, bank, 0:256], kTs[r:r + 64, c, 0:P], qTs[r:r + 64, c, :], start=True, stop=stop)
                if not stop:
                    mm(psum[:, bank, 0:256], tri, sbl[:, h % 2, 0:256], start=False, stop=False)
                    mm(psum[:, bank, P:256], ones, sbl[:, h % 2, 256:384], start=False, stop=True)
                ins = mm(psum[:, bank, 256:384], kTs[r:r + 64, c, P:256], qTs[r:r + 64, c, P:256], start=True, stop=stop)
                if not stop:
                    ins = mm(psum[:, bank, 256:384], tri, sbl[:, h % 2, 256:384], start=False, stop=True)
                return ins

            def dunit(n):
                return n % NT, n // NT

            def dscores(n):
                t, i = dunit(n)
                if n == 0:
                    pe.wait_ge(l_ready, HEADS - 1)
                if n == 1:
                    pe.wait_ge(ex_ready, HEADS)
                if n >= 2:
                    pe.wait_ge(dmasked, n - 1)
                keys = P * (t + 1)
                for g in range(DIL):
                    hd = g * DIL_HEADS + i
                    r, c = 64 * (hd % 2), hd // 2
                    bank, off = 2 * (n % 2) + (g * keys) // 512, (g * keys) % 512
                    ins = mm(psum[:, bank, off:off + keys], qkdT[r:r + 64, c, t * P:(t + 1) * P],
                             qkdT[r:r + 64, 6 + c, 0:keys], start=True, stop=True)
                ins.then_inc(dsc_ready, 1)

            for h in range(HEADS + 2):
                if h < HEADS:
                    if h >= 2:
                        pe.wait_ge(l_ready, h - 1)
                    logits(h, h % 2, True).then_inc(z_ready, 1)
                    gate_chunk(h)
                if 1 <= h <= HEADS:
                    g = h - 1
                    pe.wait_ge(l_ready, g + 1)
                    if g >= 2:
                        pe.wait_ge(ex_ready, g - 1)
                    logits(g, 2 + g % 2, False).then_inc(cum_ready, 1)
                if h == HEADS:
                    dscores(0)
                    gate_chunk(8)
                if h >= 2:
                    g = h - 2
                    pe.wait_ge(at_ready, g + 1)
                    if g == 0:
                        pe.wait_ge(qkT_out, 6)
                    if g % 2 == 0 and g >= 4:
                        pe.wait_ge(sbo_out, g // 2 - 1)
                    dst = psum[64 * (g % 2):64 * (g % 2) + 64, 4 + (g // 2) % 2, :]
                    mm(dst[:, 0:256], vsb[:, 0, g * HD:(g + 1) * HD], sba[:, g % 2, 0:256], start=True, stop=False)
                    mm(dst[:, P:256], vsb[:, 1, g * HD:(g + 1) * HD], sba[:, g % 2, 256:384],
                       start=False, stop=True).then_inc(sbo_ready, 1)

            def dturn(n):
                t, i = dunit(n)
                pe.wait_ge(dprobs_n, n + 1)
                if n == 0:
                    pe.wait_ge(sbo_out, 4)
                if n >= 1:
                    pe.wait_ge(dpT_out, n)
                for m in range(DIL * (t + 1)):
                    ins = nc.tensor.transpose(psum[:, 4 + m // 4, (m % 4) * P:(m % 4 + 1) * P],
                                              S2[:, n % 2, m * P:(m + 1) * P], ident)
                ins.then_inc(dpT_ready, 1)

            def dvalues(n):
                t, i = dunit(n)
                pe.wait_ge(dpT_out, n + 1)
                if n == 0:
                    pe.wait_ge(gates_left, 4)
                dst = psum[64 * (i % 2):64 * (i % 2) + 64, 6 + (i // 2) % 2, t * P:(t + 1) * P]
                for m in range(DIL * (t + 1)):
                    g, st = m // (t + 1), m % (t + 1)
                    hd = g * DIL_HEADS + i
                    ins = mm(dst, vd[:, st, hd * HD:(hd + 1) * HD], PT2[:, n % 2, m * P:(m + 1) * P],
                             start=m == 0, stop=m == DIL * (t + 1) - 1)
                ins.then_inc(do_ready, 1)

            for n in range(8 + 2):
                if 1 <= n < 8:
                    dscores(n)
                    gate_chunk(8 + n)
                if 1 <= n <= 8:
                    dturn(n - 1)
                if n >= 2:
                    dvalues(n - 2)

            pe.wait_ge(do_out, 2)
            wsb = [unit(U_SBO), unit(U_SBO + 1)]
            wdl = unit(U_DILO).rearrange("p (k n) -> p k n", k=2)
            for c in range(KD):
                if c >= 4:
                    pe.wait_ge(mer_ready, c - 3)
                ws = wsb[c // 4].rearrange("p (k n) -> p k n", k=4)
                for k in range(4):
                    ins = mm(psum[:, c % 4, 0:256], ws[:, k, (c % 4) * P:(c % 4 + 1) * P], osbT[:, k, :], start=k == 0, stop=k == 3)
                if c == 4 or c == KD - 1:
                    ins.then_inc(units_used, 1)
                for k in range(2):
                    ins = mm(psum[:, c % 4, 256:512], wdl[:, k, c * P:(c + 1) * P], odT[:, k, :], start=k == 0, stop=k == 1)
                ins.then_inc(br_ready, 1)

            pe.wait_ge(mer_ready, KD)

            def out2(t, b):
                return block_N(t + b, unit(U_OUT2 + 2 * b), unit(U_OUT2 + 2 * b + 1), merT, tiles=(t,))

            out2(0, 0).then_inc(units_used, 1)
            out2(0, 1).then_inc(out2_ready, 1)
            out2(1, 0).then_inc(units_used, 2)

            def open_sum(t):
                pe.wait_ge(zeros_ready, 1)
                for c in range(2):
                    mm(psum[:, 4 + 2 * t + c, :], ident, zeros, start=True, stop=False, skip_group_check=True)

            def close_sum(t):
                for c in range(2):
                    ins = mm(psum[:, 4 + 2 * t + c, :], ident, zeros, start=False, stop=True, skip_group_check=True)
                ins.then_inc(tile_done, 1)

            def products(b, m, slots=range(TOPK), i=None, last=False):
                for k in slots:
                    v, uses, quarters = k % NV, m * (TOPK // NV) + k // NV + 1, m * 4 + k // 4 + 1
                    pe.wait_ge(v_in[v], 16 * uses if i is None else i * (2 * TOPK // NV * 16) + 16 * uses)
                    if k % 4 == 0:
                        pe.wait_ge(diag_ready, quarters if i is None else i * 8 + quarters)
                    end = last and k == TOPK - 1
                    for c in range(2):
                        ins = mm(psum[:, 4 + 2 * (m // PEER_HEADS) + c, :], diag[:, k % ND, :], V[v][:, c * 512:(c + 1) * 512],
                                 start=False, stop=end, skip_group_check=True)
                    ins.then_inc(tile_done if end else v_used, 1)

            def sub_scores(n, bank):
                t, g = n // 4, n % 4
                for c in range(4):
                    ins = mm(psum[:, bank, c * P:(c + 1) * P], qpT[:, 4 * g + c, t * P:(t + 1) * P],
                             keys[:, 4 * g + c, :], start=True, stop=True)
                ins.then_inc(sub_ready, 1)

            lo, hi = unit(U_PQ), unit(U_PQ + 1)
            turn(h2, 6, tiles=(0,))
            pe.wait_ge(hT_act, 12 + 4)
            block_T(0, lo, hi, hT, 0, P).then_inc(first_ready, 1)
            pe.wait_ge(keys_in, 16)
            pe.wait_ge(proj_out, 24 + 2)
            sub_scores(0, 4)
            out2(1, 1).then_inc(units_used, 2)
            lo1, hi1 = unit(U_PQ + 2), unit(U_PQ + 3)
            for c in range(4):
                for k in range(KD):
                    w = (lo1 if k < 4 else hi1).rearrange("p (k n) -> p k n", k=4)
                    ins = mm(psum[:, 5, c * P:(c + 1) * P], w[:, k % 4, c * P:(c + 1) * P], hT[:, k, 0:P],
                             start=k == 0, stop=k == KD - 1)
            ins.then_inc(first_ready, 1)
            pe.wait_ge(proj_out, 24 + 3)
            sub_scores(1, 6)
            pe.wait_ge(sub_out, 2)
            turn(h2, 6, tiles=(1,))
            pe.wait_ge(hT_act, 12 + 8)
            block_T(0, lo, hi, hT, P, SEQ).then_inc(units_used, 2)
            block_T(2, lo1, hi1, hT, P, SEQ).then_inc(units_used, 2)

            def queries(b):
                lo, hi = unit(U_PQ + 2 * b), unit(U_PQ + 2 * b + 1)
                block_T(2 * (b % 2), lo, hi, hT).then_inc(units_used, 2)

            open_sum(0)
            products(0, 0, range(0, 4))
            pe.wait_ge(proj_out, 24 + 5)
            queries(2)
            products(0, 0, range(4, TOPK))
            pe.wait_ge(proj_out, 24 + 7)
            queries(3)

            products(1, 1, range(0, NV))
            pe.wait_ge(proj_out, 24 + 11)
            for n in range(2, 8):
                if n >= 6:
                    pe.wait_ge(sub_out, n - 3)
                sub_scores(n, n % 4)

            products(1, 1, range(NV, TOPK))
            with pe.Fori(0, PEER_HEADS // 2 - 1) as i:
                products(0, 2, i=i)
                products(1, 3, i=i)
            close_sum(0)
            open_sum(1)
            with pe.Fori(0, PEER_HEADS // 2 - 1) as i:
                products(0, 8, i=i)
                products(1, 9, i=i)
            products(0, 14)
            products(1, 15, last=True)

        @block.scalar
        def _(act):
            mark, step = stepper(act, act_step)
            A = nc.scalar.activation

            def root(n, src, dst):
                act.wait_ge(var_ready, n)
                mark(A(dst, src, ACT.Sqrt), sqrt_ready)

            def out_of_turn(n, scale, bias):
                for k in (0, 1, 4, 5):
                    act.wait_ge(turned, 4 * n + k // 2 + 1)
                    mark(A(hT[:, k, :], psum[:, 4 + k // 2, (k % 2) * 256:(k % 2) * 256 + 256], ACT.Identity, scale=scale(k), bias=bias(k)), hT_act)

            root(1, var, sq)
            act.wait_ge(vec_in, 16)
            out_of_turn(0, lambda k: vec[:, V_GMIX + k:V_GMIX + k + 1], lambda k: 0.0)
            act.wait_ge(trig_in, 1)
            mark(A(coef[3], coef[1], ACT.Sin), trig_out)
            mark(A(coef[2], coef[4], ACT.Sin), trig_out)

            def pair_out(done, banks, dst, scale=1.0, func=ACT.Copy, width=512):
                act.wait_ge(units_used, done)
                for t in range(2):
                    mark(A(dst(t), psum[:, banks + t, 0:width], func, scale=scale), proj_out)

            def cols(dst, at=0):
                return lambda t: dst[:, at + 2 * t:at + 2 * t + 2, :].rearrange("p c s -> p (c s)")

            pair_out(U_IN + 2, 0, cols(uT))
            pair_out(U_IN + 4, 2, cols(qT), SCALE)
            pair_out(U_IN + 6, 0, cols(kT))
            pair_out(U_IN + 8, 2, lambda t: vN[:, t, :])
            def exponentials(h):
                act.wait_ge(max_ready, h + 1)
                for t in range(NT):
                    n = 2 * (h % 3) + t
                    keys = slice(t * P, (2 * t + 1) * P)
                    mark(A(S1s[h % 3][:, keys], psum[:, h % 2, keys], ACT.Exp, bias=nmx3[:, n:n + 1],
                           accum_out=sum3[:, n:n + 1]), probs)

            exponentials(0)
            exponentials(1)
            for h in range(HEADS):
                if h + 2 < HEADS:
                    exponentials(h + 2)
                act.wait_ge(pT_ready, h + 1)
                if h >= 2:
                    act.wait_ge(o_ready, h - 1)
                mark(A(PT1[:, h % 2, :], psum[:, 2 + h % 2, 0:384], ACT.Copy), pT_out)
                if h >= 3 and h % 2 == 1:
                    c = (h - 3) // 2
                    act.wait_ge(o_ready, 2 * c + 2)
                    mark(A(mixT[:, 4 + c, :], psum[:, 4 + c % 2, 0:256], ACT.Copy), o_out)
            act.wait_ge(o_ready, HEADS)
            mark(A(mixT[:, 7, :], psum[:, 5, 0:256], ACT.Copy), o_out)
            act.wait_ge(o_out, 4)
            mark(A(sqr[:, 4:8, :], mixT[:, 4:8, :], ACT.Square), sqr_ready)
            root(2, cv[:, 0:256], cq[:, 0:256])
            for c in range(4):
                act.wait_ge(yd_ready, c + 1)
                mark(A(gy[:, c, :], T1v(c), ACT.Gelu_apprx_tanh), gy_ready)
            act.wait_ge(units_used, U_GLU + 1)
            for c in range(4):
                mark(A(sg[:, c, :], psum[:, 6 + c // 2, (c % 2) * 256:(c % 2) * 256 + 256], ACT.Sigmoid,
                       bias=vec[:, V_BGLU + c:V_BGLU + c + 1]), sig_ready)
            act.wait_ge(glu_ready, 4)
            mark(A(sqr[:, 0:4, :], mixT[:, 0:4, :], ACT.Square), sqr_ready)
            root(3, cv[:, 256:512], cq[:, 256:512])
            root(4, var, sq)
            root(5, var, sq)
            out_of_turn(1, lambda k: vec[:, V_GFFN + k:V_GFFN + k + 1], lambda k: 0.0)
            mark(A(siluc, vec[:, V_C:V_C + 8], ACT.Silu), siluc_ready)

            def gate_out(par, done, f, i=None):
                act.wait_ge(units_used, done if i is None else i * 6 + done)
                if f >= 2:
                    act.wait_ge(act_ready, f - 1 if i is None else i * 2 + (f - 1))
                A(silu[:, par, :], psum[:, 4 + 2 * par, :], ACT.Silu).then_inc(silu_ready, 1)

            gate_out(0, U_FF + 2, 0)
            gate_out(1, U_FF + 4, 1)
            gate_out(0, U_FF + 7, 2)
            with act.Fori(0, 4) as i:
                gate_out(1, U_FF + 10, 3, i)
                gate_out(0, U_FF + 13, 4, i)
            root(6, var, sq)
            root(7, var, sq)
            for n in range(8):
                act.wait_ge(mod_ready, n + 2)
                if n == 0:
                    act.wait_ge(ada_used, 12)
                mark(A(rows[:, n // 2, (n % 2) * 512:(n % 2 + 1) * 512], psum[:, 5 + n % 2, :], ACT.Copy), rows_out)
            act.wait_ge(modc_out, 2)
            out_of_turn(2, lambda k: gm2[:, k:k + 1], lambda k: modc[:, k:k + 1])
            d = U_IN2
            pair_out(d + 2, 0, cols(qTs), SCALE)
            pair_out(d + 4, 2, cols(kTs))
            pair_out(d + 6, 0, lambda t: vsb[:, t, :])
            for b in range(3):
                act.wait_ge(units_used, d + 8 + 2 * b)
                for t in range(NT):
                    src, dst = psum[:, 2 * ((3 + b) % 2) + t, :], qkd[:, t, b * 512:(b + 1) * 512]
                    if b == 1:
                        step(A(dst[:, 0:256], src[:, 0:256], ACT.Copy, scale=SCALE))
                        mark(A(dst[:, 256:512], src[:, 256:512], ACT.Copy), proj_out)
                    else:
                        mark(A(dst, src, ACT.Copy, scale=SCALE if b == 0 else 1.0), proj_out)
            pair_out(d + 14, 0, lambda t: vd[:, t, 0:512])
            pair_out(d + 15, 2, lambda t: vd[:, t, 512:768], width=256)

            def gates_out(p):
                if p % 2 == 0:
                    act.wait_ge(gate_ready, p // 2 + 1)
                else:
                    act.wait_ge(units_used, U_GATES + p + 1)
                mark(A(gT[:, 2 * p:2 * p + 2, :].rearrange("p c s -> p (c s)"), psum[:, 6 + p % 2 if p < 4 else 1, :], ACT.Copy), gates_left)

            for c in range(6):
                act.wait_ge(qkT_ready, c + 1)
                mark(A(qkdT[:, 2 * c:2 * c + 2, :].rearrange("p c s -> p (c s)"), psum[:, 4 + c % 4, :], ACT.Copy), qkT_out)
            for h in range(HEADS + 2):
                if h < HEADS:
                    act.wait_ge(z_ready, h + 1)
                    b = h % 2
                    if h >= 2:
                        act.wait_ge(sbo_ready, h - 1)
                    step(A(sba[:, b, :], psum[:, b, 0:384], ACT.Abs))
                    step(A(sba[:, b, :], sba[:, b, :], ACT.Exp, scale=-1.0))
                    mark(A(sba[:, b, :], sba[:, b, :], ACT.Ln, bias=ones[:, 0:1]), e_ready)
                if h >= 1 and h <= HEADS:
                    g = h - 1
                    act.wait_ge(ex_ready, g + 1)
                    mark(A(sba[:, g % 2, :], sba[:, g % 2, :], ACT.Exp), at_ready)
                if h < HEADS and h % 2 == 1:
                    gates_out(h // 2)
                if h in (4, 6, 8):
                    c = h // 2 - 2
                    act.wait_ge(sbo_ready, 2 * c + 2)
                    mark(A(osbT[:, c, :], psum[:, 4 + c % 2, 0:256], ACT.Copy), sbo_out)
            act.wait_ge(sbo_ready, HEADS)
            mark(A(osbT[:, 3, :], psum[:, 5, 0:256], ACT.Copy), sbo_out)
            for n in range(8 + 2):
                if n < 8:
                    act.wait_ge(dmasked, n + 1)
                    w = DIL * P * (n % 2 + 1)
                    mark(A(S2[:, n % 2, 0:w], S2[:, n % 2, 0:w], ACT.Exp, bias=nmx1[:, n % 2:n % 2 + 1],
                           accum_out=sum1[:, n % 2:n % 2 + 1]), dprobs)
                    if n % 2 == 1:
                        gates_out(4 + n // 2)
                if 1 <= n <= 8:
                    g = n - 1
                    act.wait_ge(dpT_ready, g + 1)
                    if g >= 2:
                        act.wait_ge(do_ready, g - 1)
                    w = DIL * P * (g % 2 + 1)
                    src = psum[:, 4:6, :].rearrange("p b n -> p (b n)")[:, 0:w]
                    mark(A(PT2[:, g % 2, 0:w], src, ACT.Copy), dpT_out)
                if n >= 5 and n % 4 == 1:
                    c = (n - 5) // 4
                    act.wait_ge(do_ready, 4 * c + 4)
                    mark(A(odT[:, c, :], psum[:, 6 + c, 0:256], ACT.Copy), do_out)
            act.wait_ge(gates_left, 8)
            for c in range(KD):
                both = gT.rearrange("p (r c) s -> p r c s", r=2)[:, :, c, :]
                mark(A(both, both, ACT.Sigmoid), gate_on)
            def turned_tile(t):
                for b in range(4):
                    act.wait_ge(turned, 12 + 4 * t + b + 1)
                    src = psum[:, 4 + b, :].rearrange("p (c s) -> p c s", c=2)[:, :, t * P:(t + 1) * P]
                    mark(A(hT[:, 2 * b:2 * b + 2, t * P:(t + 1) * P], src, ACT.Copy), hT_act)

            def queries_out(b):
                pair_out(U_PQ + 2 * b + 2, 2 * (b % 2), cols(qpT, 4 * b))

            def scores_out(n, bank):
                act.wait_ge(sub_ready, n + 1)
                mark(A(sub[:, n * 512:(n + 1) * 512], psum[:, bank, :], ACT.Copy), sub_out)

            def stage(b, m):
                A(stg[:, b, :], sub[:, bass.ds(m * 256, 256)], ACT.Copy).then_inc(staged, 1)

            def gates(m):
                act.wait_ge(best_ready, m + 1)
                A(gexp[:, :], best[:, :], ACT.Exp, bias=gnb[:, :], accum_out=gsum[:, :]).then_inc(gexp_ready, 1)

            def gelus(b, m, quarters):
                for q in quarters:
                    act.wait_ge(u_used, m * TOPK + (4 * q + 4 + NU))
                    A(gel[:, b, 4 * q:4 * q + 4], dots[:, b, 4 * q:4 * q + 4], ACT.Gelu_apprx_tanh).then_inc(gelued, 1)

            def head(b, m, gate=True, more=True):
                gelus(b, m, (0, 1))
                if gate:
                    gates(m + 1)
                if more:
                    stage(1 - b, m + 3)
                gelus(b, m, (2, 3))

            root(8, var, sq)
            turned_tile(0)
            act.wait_ge(first_ready, 1)
            for b in range(2):
                src = psum[:, b, :].rearrange("p (c s) -> p c s", c=2)[:, :, 0:P]
                mark(A(qpT[:, 2 * b:2 * b + 2, 0:P], src, ACT.Copy), proj_out)
            scores_out(0, 4)
            act.wait_ge(sub_out, 1)
            stage(0, 0)
            stage(1, 1)
            gates(0)
            act.wait_ge(first_ready, 2)
            mark(A(qpT[:, 4:8, 0:P], psum[:, 5, :].rearrange("p (c s) -> p c s", c=4), ACT.Copy), proj_out)
            scores_out(1, 6)
            act.wait_ge(sub_out, 2)
            stage(0, 2)
            root(9, var, sq)
            turned_tile(1)

            def second_queries_out(b):
                act.wait_ge(units_used, U_PQ + 2 * b + 2)
                for n in range(2):
                    src = psum[:, 2 * b + n, :].rearrange("p (c s) -> p c s", c=2)[:, :, P:SEQ]
                    mark(A(qpT[:, 4 * b + 2 * n:4 * b + 2 * n + 2, P:SEQ], src, ACT.Copy), proj_out)

            second_queries_out(0)
            gelus(0, 0, (0, 1))
            second_queries_out(1)
            gates(1)
            stage(1, 3)
            gelus(0, 0, (2, 3))
            queries_out(2)
            gelus(1, 1, (0, 1))
            gates(2)
            queries_out(3)
            gelus(1, 1, (2, 3))
            for n in range(2, 8):
                scores_out(n, n % 4)
            act.wait_ge(sub_out, 8)
            stage(0, 4)
            with act.Fori(0, 5) as i:
                head(0, i * 2 + 2)
                head(1, i * 2 + 3)
            head(0, 12)
            head(1, 13, more=False)
            head(0, 14, more=False)
            root(10, var, sq)
            head(1, 15, gate=False, more=False)
            root(11, var, sq)

        @block.vector
        def _(dve):
            mark, step = stepper(dve, dve_step)
            TT, TS = nc.vector.tensor_tensor, nc.vector.tensor_scalar
            STT = nc.vector.scalar_tensor_tensor
            roots = [0]

            def root(v, s, y, t):
                roots[0] += 1
                dve.wait_ge(sqrt_ready, roots[0])
                step(nc.vector.reciprocal(y, s))
                step(TT(t, y, y, ALU.mult))
                step(TT(t, t, v, ALU.mult))
                step(TS(t, t, -0.5, 1.5, ALU.mult, ALU.add))
                step(TT(y, y, t, ALU.mult))

            def squares(t, junk_at):
                step(nc.vector.tensor_tensor_reduce(out=junk_at, in0=xres[:, t, :], in1=xres[:, t, :], scale=1.0,
                                                    scalar=0.0, op0=ALU.mult, op1=ALU.add, accum_out=ssq[:, t:t + 1]))

            def norm(tiles=(), junk_at=None):
                for t in tiles:
                    squares(t, junk_at)
                step(TS(var, ssq, 1.0 / D, EPS, ALU.mult, ALU.add), var_ready)
                root(var, sq, rstd, nt1)

            def hT_out(n, scale, bias=None):
                for k in (2, 3, 6, 7):
                    dve.wait_ge(turned, 4 * n + k // 2 + 1)
                    src = psum[:, 4 + k // 2, (k % 2) * 256:(k % 2) * 256 + 256]
                    if bias is None:
                        ins = TS(hT[:, k, :], src, scale(k), None, ALU.mult)
                    else:
                        ins = TS(hT[:, k, :], src, scale(k), bias(k), ALU.mult, ALU.add)
                    mark(ins, hT_dve)

            for t in range(NT):
                dve.wait_ge(x_in[t], 16)
                squares(t, take(1024, zo + 2048))
            norm()
            for t in range(NT):
                mark(TS(xn1[:, t, :], xres[:, t, :], rstd[:, t:t + 1], None, ALU.mult), xn_ready)

            dve.wait_ge(vec_in, 16)
            lre, lim, ldt = (vec[:, v:v + 16] for v in (V_LRE, V_LIM, V_LDT))
            r_, th, cs, sn, cth, dt, t_, n_, p_, den, kr, ki, lbr, lbi = coef[0:14]
            hT_out(0, lambda k: vec[:, V_GMIX + k:V_GMIX + k + 1])
            MAGIC = 1.5 * 2.0 ** 23

            def exp_exact(dst, src):
                step(TS(n_, src, 1.4426950408889634, MAGIC, ALU.mult, ALU.add))
                step(TS(n_, n_, MAGIC, None, ALU.subtract))
                step(TS(n_, n_, -126.0, 127.0, ALU.max, ALU.min))
                step(STT(out=t_, in0=n_, scalar=-0.693359375, in1=src, op0=ALU.mult, op1=ALU.add))
                step(STT(out=t_, in0=n_, scalar=2.12194440e-4, in1=t_, op0=ALU.mult, op1=ALU.add))
                step(TS(p_, t_, 1.0 / 5040, None, ALU.mult))
                for c in (720.0, 120.0, 24.0, 6.0, 2.0, 1.0):
                    step(STT(out=p_, in0=p_, scalar=1.0 / c, in1=t_, op0=ALU.add, op1=ALU.mult))
                step(TS(t_.bitcast(I32), n_, 127.0, 2.0 ** 23, ALU.add, ALU.mult))
                step(STT(out=dst, in0=p_, scalar=1.0, in1=t_, op0=ALU.add, op1=ALU.mult))

            exp_exact(dt, ldt)
            step(TT(th, lim, dt, ALU.mult))
            step(TT(den, lre, dt, ALU.mult))
            exp_exact(r_, den)
            step(TS(n_, th, 0.15915494309189535, MAGIC, ALU.mult, ALU.add))
            step(TS(n_, n_, MAGIC, None, ALU.subtract))
            for c in (6.28125, 1.9350051879882812e-3, 3.0199159819567e-7):
                step(STT(out=th, in0=n_, scalar=-c, in1=th, op0=ALU.mult, op1=ALU.add))
            step(TS(th, th, 3.1415925, -3.1415925, ALU.min, ALU.max))
            step(STT(out=cth, in0=th, scalar=-1.0, in1=th, op0=ALU.mult, op1=ALU.max))
            step(TS(cth, cth, -1.0, 1.5707963267948966, ALU.mult, ALU.add), trig_in)
            dve.wait_ge(trig_out, 2)
            step(TT(lbr, r_, cs, ALU.mult))
            step(TS(lbr, lbr, -1.0, None, ALU.add))
            step(TT(lbi, r_, sn, ALU.mult))
            step(TT(den, lre, lre, ALU.mult))
            step(TT(t_, lim, lim, ALU.mult))
            step(TT(den, den, t_, ALU.add))
            step(nc.vector.reciprocal(den, den))
            step(TT(kr, lbr, lre, ALU.mult))
            step(TT(t_, lbi, lim, ALU.mult))
            step(TT(kr, kr, t_, ALU.add))
            step(TT(kr, kr, den, ALU.mult))
            step(TT(ki, lbi, lre, ALU.mult))
            step(TT(t_, lbr, lim, ALU.mult))
            step(TT(ki, ki, t_, ALU.subtract))
            step(TT(ki, ki, den, ALU.mult))
            dve.wait_ge(cc_in, 16)
            wide = [P, NST, 32]
            tc1 = T1.rearrange("p j r t -> p (j r t)")[:, 0:512].rearrange("p (j m) -> p j m", j=NST)
            krb, kib = kr.unsqueeze(2).to_broadcast(wide), ki.unsqueeze(2).to_broadcast(wide)
            step(TT(CP[:, :, 0, :], CT[:, :, 0, :], krb, ALU.mult))
            step(TT(tc1, CT[:, :, 1, :], kib, ALU.mult))
            step(TT(CP[:, :, 0, :], CP[:, :, 0, :], tc1, ALU.subtract))
            step(TT(CP[:, :, 1, :], CT[:, :, 0, :], kib, ALU.mult))
            step(TT(tc1, CT[:, :, 1, :], krb, ALU.mult))
            step(STT(out=CP[:, :, 1, :], in0=CP[:, :, 1, :], scalar=-1.0, in1=tc1, op0=ALU.mult, op1=ALU.subtract), cp_ready)
            pr, pi = coef[14], coef[15]
            step(nc.vector.memset(E[:, :, 0, 0:1], 1.0))
            step(nc.vector.memset(E[:, :, 1, 0:1], 0.0))
            step(nc.vector.tensor_copy(pr, cs))
            step(nc.vector.tensor_copy(pi, sn))
            n = 1
            while n < SEQ:
                new, old = E[:, :, :, n:2 * n], E[:, :, :, 0:n]
                shape = [P, NST, 2, n]
                tmp = etmp[:, 0:NST * 2 * n].rearrange("p (j r t) -> p j r t", j=NST, r=2)
                mark(TT(new, old, pr.unsqueeze(2).unsqueeze(3).to_broadcast(shape), ALU.mult))
                step(TT(tmp, old, pi.unsqueeze(2).unsqueeze(3).to_broadcast(shape), ALU.mult))
                mark(TT(new[:, :, 0, :], new[:, :, 0, :], tmp[:, :, 1, :], ALU.subtract))
                step(TT(new[:, :, 1, :], new[:, :, 1, :], tmp[:, :, 0, :], ALU.add))
                if 2 * n < SEQ:
                    step(TT(t_, pr, pr, ALU.mult))
                    step(TT(p_, pi, pi, ALU.mult))
                    step(STT(out=pi, in0=pi, scalar=2.0, in1=pr, op0=ALU.mult, op1=ALU.mult))
                    step(TT(pr, t_, p_, ALU.subtract))
                n *= 2

            def e_pair(q, ri):
                return E[:, 2 * q:2 * q + 2, ri, :].unsqueeze(2).to_broadcast([P, 2, 2, SEQ])

            for q in range(NST // 2):
                dve.wait_ge(bu_ready, q + 1)
                b = 4 + 2 * (q % 2)
                src = psum[:, b:b + 2, :].rearrange("p j (r t) -> p j r t", r=2)
                if q >= 2:
                    dve.wait_ge(turned_back, q - 1)
                mark(TT(T1s[q % 2], src, e_pair(q, 0), ALU.mult))
                mark(TT(T2s[0][q % 2], src, e_pair(q, 1), ALU.mult), bu_used)

            def states(q):
                dve.wait_ge(turned_back, q + 1)
                for j in (2 * q, 2 * q + 1):
                    for ri in range(2):
                        ins = nc.vector.tensor_tensor_scan(Z[:, j, ri, :], r_[:, j:j + 1].to_broadcast([P, SEQ]), Z[:, j, ri, :],
                                                           0.0, ALU.mult, ALU.add)
                        (step if j % 2 and ri else mark)(ins)
                if q >= 2:
                    dve.wait_ge(states_ready, q - 1)
                z = Z[:, 2 * q:2 * q + 2, :, :]
                mark(TT(T1s[q % 2], z, e_pair(q, 0), ALU.mult))
                mark(TT(T2s[1][q % 2], z, e_pair(q, 1), ALU.mult), forward)


            def maximum(h):
                b = h % 3
                dve.wait_ge(sc_ready, h + 1)
                if h == 1:
                    dve.wait_ge(turned_back, 8)
                for t in range(NT):
                    (mark if t == 0 else step)(nc.vector.reduce_max(mx3[:, 2 * b + t:2 * b + t + 1], psum[:, h % 2, t * P:(2 * t + 1) * P], AX))
                step(TS(nmx3[:, 2 * b:2 * b + 2], mx3[:, 2 * b:2 * b + 2], -1.0, None, ALU.mult), max_ready)

            def normalise(h):
                b = h % 3
                dve.wait_ge(probs, 2 * h + 2)
                step(nc.vector.reciprocal(rs3[:, 2 * b:2 * b + 2], sum3[:, 2 * b:2 * b + 2]))
                mark(TS(S1s[b][:, 0:P], S1s[b][:, 0:P], rs3[:, 2 * b:2 * b + 1], None, ALU.mult))
                step(TS(S1s[b][:, P:3 * P], S1s[b][:, P:3 * P], rs3[:, 2 * b + 1:2 * b + 2], None, ALU.mult), probs_n)

            maximum(0)
            maximum(1)
            for h in range(HEADS):
                if h + 2 < HEADS:
                    maximum(h + 2)
                normalise(h)
                states(h)

            def branch_norm(br, n):
                half = slice(256 * (n - 1), 256 * n)
                root(cv[:, half], cq[:, half], cy[:, half], ct[:, half])
                for c in range(4 * br, 4 * br + 4):
                    g = vec[:, V_GSSM + c:V_GSSM + c + 1]
                    mark(STT(out=mixT[:, c, :], in0=mixT[:, c, :], scalar=g, in1=cy[:, half], op0=ALU.mult, op1=ALU.mult), mix_ready)

            def branch_var(n):
                dve.wait_ge(csum_ready, n)
                step(TS(cv[:, 256 * (n - 1):256 * n], psum[:, 3 + n, 0:256], 1.0 / 512, EPS, ALU.mult, ALU.add), var_ready)

            branch_var(1)
            dve.wait_ge(y_ready, 1)
            for c in range(4):
                mark(STT(out=T1v(c), in0=uT[:, c, :], scalar=vec[:, V_D + c:V_D + c + 1],
                         in1=psum[:, 6 + c // 2, (c % 2) * 256:(c % 2) * 256 + 256], op0=ALU.mult, op1=ALU.add), yd_ready)
            branch_norm(1, 1)
            for c in range(4):
                dve.wait_ge(sig_ready, c + 1)
                mark(TT(mixT[:, c, :], gy[:, c, :], sg[:, c, :], ALU.mult), glu_ready)
            branch_var(2)
            branch_norm(0, 2)
            for t in range(NT):
                dve.wait_ge(*((out1_ready, 1) if t == 0 else (units_used, U_OUT + 4)))
                for b in range(2):
                    step(TT(xres[:, t, b * 512:(b + 1) * 512], xres[:, t, b * 512:(b + 1) * 512], psum[:, 2 * t + b, :], ALU.add), xadd)
                norm((t,), junk_at=take(1024, zo + 5120))
                mark(TS(xn2[:, t, :], xres[:, t, :], rstd[:, t:t + 1], None, ALU.mult), xn_ready)

            hT_out(1, lambda k: vec[:, V_GFFN + k:V_GFFN + k + 1])
            dve.wait_ge(siluc_ready, 1)
            dve.wait_ge(bada_in, 16)
            ada_order = sem("ada_order")

            def window(w, i=None):
                at = w if i is None else i * 2 + w
                dve.wait_ge(ada_in, 16 * (w + 1) if i is None else i * 32 + 16 * (w + 1))
                dst = ada_acc[:, bass.ds(at * 512, 512)] if i is not None else ada_acc[:, w * 512:(w + 1) * 512]
                for k in range(KD):
                    ins = STT(out=dst, in0=ada_slot[:, k, :], scalar=siluc[:, k:k + 1], in1=dst, op0=ALU.mult, op1=ALU.add)
                    if k < KD - 1:
                        ins.then_inc(ada_order, 1)
                        n = w * (KD - 1) + k + 1
                        dve.wait_ge(ada_order, n if i is None else i * (2 * (KD - 1)) + n)
                    else:
                        ins.then_inc(ada_used, 1)

            def act_out(par, f, i=None):
                dve.wait_ge(silu_ready, f + 1 if i is None else i * 2 + f + 1)
                if f >= 2:
                    done = U_FF + 5 + 3 * (f - 2)
                    dve.wait_ge(units_used, done if i is None else i * 6 + done)
                TT(actT[:, par, :, :].rearrange("p f s -> p (f s)"), silu[:, par, :], psum[:, 5 + 2 * par, :],
                   ALU.mult).then_inc(act_ready, 1)

            for f in range(3):
                window(f)
                act_out(f % 2, f)
            window(3)
            with dve.Fori(0, 4) as i:
                act_out(1, 3, i)
                window(4, i)
                act_out(0, 4, i)
                window(5, i)
            for t in range(NT):
                dve.wait_ge(*((down_ready, 1) if t == 0 else (units_used, U_FF + 3 * NFF)))
                for b in range(2):
                    step(TT(xres[:, t, b * 512:(b + 1) * 512], xres[:, t, b * 512:(b + 1) * 512], psum[:, 2 * t + b, :], ALU.add), xadd)
                squares(t, take(1024, zo + 5120))
            norm()
            dve.wait_ge(gf_in, 16)
            for t in range(NT):
                step(STT(out=xres[:, t, :], in0=xres[:, t, :], scalar=rstd[:, t:t + 1], in1=gfin1, op0=ALU.mult, op1=ALU.mult))
            norm((0, 1), junk_at=take(1024, zo + 5120))
            for t in range(NT):
                mark(TS(xn3[:, t, :], xres[:, t, :], rstd[:, t:t + 1], None, ALU.mult), xn_ready)
            dve.wait_ge(mod_ready, 1)
            step(nc.vector.tensor_copy(modc, psum[:, 4, 0:16]), modc_out)
            step(STT(out=gm2, in0=modc[:, 8:16], scalar=1.0, in1=vec[:, V_GMIX2:V_GMIX2 + 8], op0=ALU.add, op1=ALU.mult), modc_out)
            hT_out(2, lambda k: gm2[:, k:k + 1], lambda k: modc[:, k:k + 1])

            dve.wait_ge(proj_out, 8 + 12)
            for t in range(NT):
                qk = qkd[:, t, :].rearrange("p (h r d) -> p h r d", h=24, r=2)
                B3 = ropeB.rearrange("p (h r d) -> p h r d", h=24, r=2)
                cb = cos[:, t, :].unsqueeze(1).to_broadcast([P, 24, 64])
                mark(TT(ropeA.rearrange("p (h d) -> p h d", h=24), qkd[:, t, :].rearrange("p (h d) -> p h d", h=24), cb, ALU.mult))
                for r in range(2):
                    sb_ = sin[:, t, 32 * r:32 * r + 32].unsqueeze(1).to_broadcast([P, 24, 32])
                    (mark if r == 0 else step)(TT(B3[:, :, r, :], qk[:, :, 1 - r, :], sb_, ALU.mult))
                step(TT(qkd[:, t, :], ropeA, ropeB, ALU.add), roped)

            for h in range(HEADS + 1):
                if h < HEADS:
                    b = h % 2
                    dve.wait_ge(e_ready, h + 1)
                    if h >= 2:
                        dve.wait_ge(cum_ready, h - 1)
                    step(STT(out=sbl[:, b, :], in0=psum[:, b, 0:384], scalar=0.0, in1=sba[:, b, :], op0=ALU.max, op1=ALU.add))
                    step(TT(sbl[:, b, :], sbl[:, b, :], negm, ALU.mult), l_ready)
                    dve.wait_ge(cum_ready, h + 1)
                    step(STT(out=sba[:, b, :], in0=psum[:, 2 + b, 0:384], scalar=0.0, in1=sbias, op0=ALU.min, op1=ALU.add), ex_ready)

            for n in range(8 + 1):
                if n < 8:
                    t, b = n % 2, n % 2
                    w = P * (t + 1)
                    dve.wait_ge(dsc_ready, n + 1)
                    if n >= 2:
                        dve.wait_ge(dpT_ready, n - 1)
                    src = psum[:, 2 * b:2 * b + 2, :].rearrange("p b n -> p (b n)")[:, 0:DIL * w]
                    step(TT(S2[:, b, 0:DIL * w], src, dmask[t].rearrange("p g k -> p (g k)"), ALU.add))
                    step(nc.vector.reduce_max(mx1[:, b:b + 1], S2[:, b, 0:DIL * w], AX))
                    step(TS(nmx1[:, b:b + 1], mx1[:, b:b + 1], -1.0, None, ALU.mult), dmasked)
                if n >= 1:
                    b = (n - 1) % 2
                    w = DIL * P * (b + 1)
                    dve.wait_ge(dprobs, n)
                    step(nc.vector.reciprocal(rs1[:, b:b + 1], sum1[:, b:b + 1]))
                    step(TS(S2[:, b, 0:w], S2[:, b, 0:w], rs1[:, b:b + 1], None, ALU.mult), dprobs_n)

            for c in range(KD):
                dve.wait_ge(br_ready, c + 1)
                dve.wait_ge(gate_on, c + 1)
                both = tmp2.rearrange("p (r s) -> p r s", r=2)
                gates = gT.rearrange("p (r c) s -> p r c s", r=2)[:, :, c, :]
                step(TT(both, psum[:, c % 4, :].rearrange("p (r s) -> p r s", r=2), gates, ALU.mult))
                step(TT(merT[:, c, :], both[:, 0, :], both[:, 1, :], ALU.add), mer_ready)
            dve.wait_ge(rows_out, 8)
            dve.wait_ge(rows_in, 32)
            step(STT(out=rows[:, 2, :], in0=rows[:, 2, :], scalar=1.0, in1=gffn2r, op0=ALU.add, op1=ALU.mult))
            step(nc.vector.memset(zeros, 0.0), zeros_ready)

            def residual(t, b):
                if (t, b) == (0, 1):
                    dve.wait_ge(out2_ready, 1)
                else:
                    dve.wait_ge(units_used, U_OUT2 + (0 if t == 0 else 2 * b + 2))
                cs_ = slice(b * 512, (b + 1) * 512)
                step(TT(res_tmp, psum[:, 2 * t + b, :], rows[:, 0, cs_], ALU.mult))
                step(TT(xres[:, t, cs_], xres[:, t, cs_], res_tmp, ALU.add), xadd)

            def peer_input(t):
                norm((t,), junk_at=norm_junk)
                step(STT(out=h2[:, t, :], in0=xres[:, t, :], scalar=rstd[:, t:t + 1], in1=rows[:, 2, :], op0=ALU.mult, op1=ALU.mult))
                step(TT(h2[:, t, :], h2[:, t, :], rows[:, 1, :], ALU.add), xn_ready)

            residual(0, 0)
            residual(0, 1)
            peer_input(0)
            residual(1, 0)

            LOW = -3.4e38

            def route(b, m):
                drain = dve.drain
                dve.wait_ge(staged, m + 1)
                nc.vector.memset(junk, 0.0)
                drain()
                rows_ = [stg[:, b, q * P:(q + 1) * P] for q in range(2)]
                lo, hi = ([stop[:, b, q, 8 * i:8 * i + 8] for q in range(2)] for i in range(2))
                for q in range(2):
                    nc.vector.max(lo[q], rows_[q])
                drain()
                for q in range(2):
                    nc.vector.max_index(itop[:, b, q, 0:8], lo[q], rows_[q])
                drain()
                for q in range(2):
                    nc.vector.match_replace(rows_[q], lo[q], rows_[q], LOW)
                drain()
                for q in range(2):
                    nc.vector.max(hi[q], rows_[q])
                drain()
                for q in range(2):
                    nc.vector.max_index(itop[:, b, q, 8:16], hi[q], rows_[q])
                c3 = cand.rearrange("p (i j) -> p i j", i=TOPK)
                sh = [P, TOPK, TOPK]
                TT(c3, stop[:, b, 0, :].unsqueeze(2).to_broadcast(sh), stop[:, b, 1, :].unsqueeze(1).to_broadcast(sh), ALU.add)
                drain()
                nc.vector.max(best[:, 0:8], cand)
                drain()
                nc.vector.max_index(pos[:, 0:8], best[:, 0:8], cand)
                drain()
                nc.vector.match_replace(cand, best[:, 0:8], cand, LOW)
                drain()
                nc.vector.max(best[:, 8:16], cand)
                TS(gnb, best[:, 0:1], -1.0, None, ALU.mult)
                drain()
                nc.vector.max_index(pos[:, 8:16], best[:, 8:16], cand).then_inc(best_ready, 1)
                dve.wait_ge(best_ready, m + 1)
                nc.vector.tensor_copy(itopf, itop[:, b, :, :])
                TS(ij[:, 0, :], pos, 4, None, ALU.logical_shift_right)
                TS(ij[:, 1, :], pos, 15, None, ALU.bitwise_and)
                drain()
                nc.vector.tensor_copy(ijf, ij)
                drain()
                sh4 = [P, 2, TOPK, TOPK]
                TT(oh, ijf.unsqueeze(3).to_broadcast(sh4), iota.unsqueeze(1).unsqueeze(1).to_broadcast(sh4), ALU.is_equal)
                drain()
                TT(oh, oh, itopf.unsqueeze(2).to_broadcast(sh4), ALU.mult)
                drain()
                nc.vector.tensor_reduce(e12, oh, AX, ALU.add)
                dve.wait_ge(gexp_ready, m + 1)
                nc.vector.reciprocal(grs, gsum)
                drain()
                TS(gate[:, b, :], gexp, grs, None, ALU.mult)
                STT(out=expert[:, b, :], in0=e12[:, 0, :], scalar=128.0, in1=e12[:, 1, :], op0=ALU.mult,
                    op1=ALU.add).then_inc(routed, 1)
                dve.wait_ge(routed, m + 1)

            def dots_of(b, m, t, q):
                for k in range(4 * q, 4 * q + 4):
                    u = k % NU
                    dve.wait_ge(u_in[u], m * (TOPK // NU * 16) + 16 * (k // NU + 1))
                    nc.vector.tensor_tensor_reduce(out=U[u], in0=U[u], in1=h2[:, t, :], scale=1.0, scalar=0.0,
                                                   op0=ALU.mult, op1=ALU.add, accum_out=dots[:, b, k:k + 1]).then_inc(u_used, 1)

            def weigh(b, m, q):
                dve.wait_ge(gelued, m * 4 + q + 1)
                for k in range(4 * q, 4 * q + 4):
                    dve.wait_ge(v_used, m * TOPK + k + 1)
                    ins = TS(diag[:, k % ND, :], ident, gel[:, b, k:k + 1], gate[:, b, k:k + 1], ALU.mult, ALU.mult)
                ins.then_inc(diag_ready, 1)

            def head(b, m, t, more=True):
                dots_of(b, m, t, 0)
                dots_of(b, m, t, 1)
                weigh(b, m, 0)
                if more:
                    dve.wait_ge(idx_read, m + 1)
                    route(1 - b, m + 1)
                dots_of(b, m, t, 2)
                weigh(b, m, 1)
                dots_of(b, m, t, 3)
                weigh(b, m, 2)
                weigh(b, m, 3)

            for _ in range(NU):
                step(nc.vector.memset(junk, 0.0), u_used)
            for _ in range(ND):
                step(nc.vector.memset(junk, 0.0), v_used)
            step(nc.vector.memset(junk, 0.0), idx_read)
            step(nc.vector.memset(junk, 0.0), peer_go)

            def finish(t):
                dve.wait_ge(tile_done, t + 1)
                for c in range(2):
                    cs_ = slice(c * 512, (c + 1) * 512)
                    step(TT(fin[:, cs_], psum[:, 4 + 2 * t + c, :], rows[:, 3, cs_], ALU.mult))
                step(TT(xres[:, t, :], xres[:, t, :], fin, ALU.add))
                norm((t,), junk_at=fin)
                step(STT(out=xres[:, t, :], in0=xres[:, t, :], scalar=rstd[:, t:t + 1], in1=gfin2r, op0=ALU.mult, op1=ALU.mult), acc_out)

            route(0, 0)
            residual(1, 1)
            peer_input(1)
            with dve.Fori(0, PEER_HEADS // 2) as i:
                head(0, i * 2, 0)
                head(1, i * 2 + 1, 0)
            with dve.Fori(0, PEER_HEADS // 2 - 1) as i:
                head(0, i * 2 + 8, 1)
                head(1, i * 2 + 9, 1)
            head(0, 14, 1)
            finish(0)
            head(1, 15, 1, more=False)
            finish(1)


def shape_constants(np):
    f = np.float32
    c = np.zeros((P, NCONST), f)
    i = np.arange(P)
    c[:, C_ID:C_ID + P] = np.eye(P)
    c[:, C_REV:C_REV + P] = np.eye(P)[::-1]
    c[:, C_TRI:C_TRI + P] = i[:, None] >= i[None, :]
    c[:, C_ONE:C_ONE + P] = 1.0
    q = np.arange(SEQ)
    seen = (q[None, :] // 64) <= (q[:, None] // 64)
    c[:, C_MASK1:C_MASK1 + 512] = np.where(seen, 0.0, NEG).reshape(NT, P, SEQ).transpose(1, 0, 2).reshape(P, 512)
    before = (i[:, None] < i[None, :])
    open_ = np.concatenate([before, np.ones((P, P), bool), before], axis=1)
    c[:, C_NEGM:C_NEGM + 384] = -open_.astype(f)
    c[:, C_BIAS:C_BIAS + 384] = np.where(open_, 0.0, NEG)
    back = q[:, None] - q[None, :]
    for t, at in ((0, C_DM0), (1, C_DM1)):
        w = P * (t + 1)
        for g, (win, r) in enumerate(((128, 1), (512, 4), (2048, 16))):
            ok = (back >= 0) & (back <= win) & (back % r == 0)
            c[:, at + g * w:at + (g + 1) * w] = np.where(ok, 0.0, NEG)[t * P:(t + 1) * P, :w]
    half = HD // 2
    inv = (f(10000.0) ** (-np.arange(half, dtype=f) / f(half))).astype(f)
    ang = q.astype(f)[:, None] * inv[None, :]
    cs, sn = np.cos(ang).astype(f), np.sin(ang).astype(f)
    c[:, C_COS:C_COS + 128] = np.concatenate([cs, cs], 1).reshape(NT, P, 64).transpose(1, 0, 2).reshape(P, 128)
    c[:, C_SIN:C_SIN + 128] = np.concatenate([-sn, sn], 1).reshape(NT, P, 64).transpose(1, 0, 2).reshape(P, 128)
    c[:, C_IOTA:C_IOTA + TOPK] = np.arange(TOPK)
    return c


def weight_stream(np, a):
    units = []

    def add(w):
        assert w.shape[0] == P and w[0].size == UNIT, w.shape
        units.append(w.reshape(P, UNIT))

    def chunked(w):
        return w.reshape(w.shape[0] // P, P, w.shape[1]).transpose(1, 0, 2)

    def columns(w, lo):
        w = chunked(w)
        for k in range(0, w.shape[1], 4):
            add(w[:, k:k + 4, lo:lo + 512])

    w_in = a["w_in"][0]
    for b in range(4):
        columns(w_in, b * 512)
    columns(a["ssm_w_glu"][0], 0)
    for b in range(2):
        columns(a["w_out"][0], b * 512)
    gate, up, down = (chunked(a[n][0]) for n in ("w_gate", "w_up", "w_down"))
    for f in range(NFF + 1):
        if f < NFF:
            add(gate[:, :, f * 256:(f + 1) * 256])
            add(up[:, :, f * 256:(f + 1) * 256])
        if f >= 1:
            add(down[:, 2 * (f - 1):2 * f, :])
    w_in2 = a["w_in_2"][0]
    for b in range(7):
        columns(w_in2, b * 512)
    add(chunked(w_in2)[:, :, 3584:3840])
    for b in range(4):
        columns(w_in2, 3840 + b * 512)
    for b in range(2):
        columns(a["w_sb_o_2"][0], b * 512)
    add(chunked(a["w_dil_o_2"][0]))
    for b in range(2):
        columns(a["w_out_2"][0], b * 512)
    for b in range(4):
        columns(a["w_pq_2"][0], b * 512)
    assert len(units) == UNITS
    return np.stack(units)


def kernel(**inputs):
    import numpy as np
    import concourse.bacc as bacc
    from concourse.bass_utils import run_bass_kernel_spmd

    a = {k: np.asarray(v) for k, v in inputs.items()}

    def cols(v):
        return v.reshape(-1, P).T

    def states(v):
        return v.reshape(NST, P).T

    vecs = np.concatenate([
        cols(a["norm_mix_g"]), cols(a["norm_ffn_g"]), cols(a["norm_ssm_out_g"]), cols(a["norm_att_out_g"]),
        cols(a["ssm_d"]), cols(a["ssm_b_glu"]), cols(a["g_mix_2"]), cols(a["c_2"]),
        states(a["ssm_lam_re"]), states(a["ssm_lam_im"]), states(np.repeat(a["ssm_log_dt"][0], STATE))], axis=1)
    ssm_b = np.zeros((P, 4, 2, P), np.float32)
    ssm_c = np.zeros((P, NST, 2, 32), np.float32)
    for g in range(GROUPS):
        j, half = g // 2, g % 2
        r = 32 * (j % 4) + GCH * half
        for ri, (b, c) in enumerate((("ssm_b_re", "ssm_c_re"), ("ssm_b_im", "ssm_c_im"))):
            ssm_b[r:r + GCH, j // 4, ri, STATE * half:STATE * (half + 1)] = a[b][0, g].T
            ssm_c[STATE * half:STATE * (half + 1), j, ri, GCH * half:GCH * (half + 1)] = a[c][0, g].T
    rel = a["attn_rel_bias"][0]
    rel_ext = np.concatenate([np.repeat(rel[:, :1], 127, axis=1), rel], axis=1)
    w_ada = a["w_ada_2"][0].reshape(KD, P, 12, 512).transpose(2, 1, 0, 3).reshape(12, P, KD * 512)
    arrays = {
        "x": a["x"][0], "consts": shape_constants(np), "vecs": vecs, "weights": weight_stream(np, a),
        "sub_keys": a["peer_keys_2"][0].reshape(16, P, P).transpose(2, 0, 1).reshape(P, UNIT),
        "ssm_b": ssm_b, "ssm_c": ssm_c, "rel_ext": rel_ext, "g_final1": a["norm_final_g"][None], "w_ada": w_ada,
        "b_ada": a["b_ada_2"], "g_ffn2": a["g_ffn_2"], "g_final2": a["g_final_2"][None],
        "peer_u": a["peer_u_2"][0], "peer_v": a["peer_v_2"][0],
    }
    arrays = {k: np.ascontiguousarray(v) for k, v in arrays.items()}
    nc = bacc.Bacc("TRN2", target_bir_lowering=False, num_devices=1)
    args = {k: nc.dram_tensor(f"in_{k}", v.shape, mybir.dt.from_np(v.dtype), kind="ExternalInput").ap()
            for k, v in arrays.items()}
    out = nc.dram_tensor("out_x", (SEQ, D), F32, kind="ExternalOutput").ap()
    build(nc, out=out, **args)
    r = run_bass_kernel_spmd(nc, [{f"in_{k}": v for k, v in arrays.items()}], core_ids=[0])
    return r.results[0]["out_x"].reshape(1, SEQ, D)
```
